# Optimizing a Trainium2 kernel written in Bass

```python
import jax, jax.numpy as jnp
from jax import lax
import numpy as np

D_MODEL = 1024
BATCH = 1
SEQ = 2048
DEPTH = 1

M_HEADS = 4
M_DH = D_MODEL // 8
M_W = M_HEADS * M_DH
M_CHUNK = 64
CONV_K = 4
F_HEADS = 8
F_DH = D_MODEL // 16
F_W = F_HEADS * F_DH
Q_BLOCK = 128
D_MIX = M_W + F_W
EPS = 1e-6

SPLITS = (M_W, M_W, M_W, M_W, M_W, M_HEADS, M_HEADS,
          F_W, F_W, F_W, F_W, F_HEADS)
SPLIT_IDX = [int(s) for s in np.cumsum(SPLITS)[:-1]]
D_IN = int(sum(SPLITS))

kernel_name = "hymba_mlstm_fox_adaln_layer"

def rms_norm(x, g):
    xf = x.astype(jnp.float32)
    y = xf * lax.rsqrt(jnp.mean(xf * xf, axis=-1, keepdims=True) + EPS)
    return (y * g.astype(jnp.float32)).astype(x.dtype)

def head_layer_norm(x, g):
    xf = x.astype(jnp.float32)
    mu = jnp.mean(xf, axis=-1, keepdims=True)
    var = jnp.mean((xf - mu) ** 2, axis=-1, keepdims=True)
    y = (xf - mu) * lax.rsqrt(var + EPS)
    y = y.reshape(x.shape[:-2] + (x.shape[-2] * x.shape[-1],))
    return (y * g.astype(jnp.float32)).astype(x.dtype)

def causal_depthwise_conv(x, w, b):
    rhs = w.reshape(CONV_K, 1, x.shape[-1])
    y = lax.conv_general_dilated(x, rhs.astype(x.dtype), window_strides=(1,),
                                 padding=[(CONV_K - 1, 0)],
                                 dimension_numbers=('NWC', 'WIO', 'NWC'),
                                 feature_group_count=x.shape[-1])
    return y + b

def mlstm_chunkwise(q, k, v, ig, lf):
    B, H, S, d = q.shape
    L = M_CHUNK
    NC = S // L

    def to_chunks(a):
        return jnp.moveaxis(a.reshape(a.shape[:2] + (NC, L) + a.shape[3:]), 2, 0)

    qc, kc, vc = to_chunks(q), to_chunks(k), to_chunks(v)
    ic = to_chunks(ig)
    bc = jnp.cumsum(to_chunks(lf), axis=-1)
    causal = jnp.tril(jnp.ones((L, L), dtype=bool))

    def step(carry, inp):
        C, n, m = carry
        qj, kj, vj, ij, bj = inp
        D = bj[..., :, None] - bj[..., None, :] + ij[..., None, :]
        D = jnp.where(causal, D, -jnp.inf)
        inter = bj + m[..., None]
        m_t = jnp.maximum(inter, jnp.max(D, axis=-1))
        w_inter = jnp.exp(inter - m_t)
        s = jnp.einsum('bhtd,bhsd->bhts', qj, kj) * jnp.exp(D - m_t[..., None])
        num = (w_inter[..., None] * jnp.einsum('bhtd,bhde->bhte', qj, C)
               + jnp.einsum('bhts,bhse->bhte', s, vj))
        den = w_inter * jnp.einsum('bhtd,bhd->bht', qj, n) + jnp.sum(s, axis=-1)
        h = num / jnp.maximum(jnp.abs(den), jnp.exp(-m_t))[..., None]
        bL = bj[..., -1]
        a = bL[..., None] - bj + ij
        m_new = jnp.maximum(bL + m, jnp.max(a, axis=-1))
        decay = jnp.exp(bL + m - m_new)
        ws = jnp.exp(a - m_new[..., None])
        C_new = decay[..., None, None] * C + jnp.einsum('bhs,bhsd,bhse->bhde', ws, kj, vj)
        n_new = decay[..., None] * n + jnp.einsum('bhs,bhsd->bhd', ws, kj)
        return (C_new, n_new, m_new), h

    init = (jnp.zeros((B, H, d, d), jnp.float32), jnp.zeros((B, H, d), jnp.float32),
            jnp.zeros((B, H), jnp.float32))
    _, hs = lax.scan(step, init, (qc, kc, vc, ic, bc))
    return hs.transpose(1, 0, 3, 2, 4).reshape(B, S, H, d)

def forgetting_attention(q, k, v, logf):
    B, H, S, d = q.shape
    NB = S // Q_BLOCK
    F = jnp.cumsum(logf, axis=-1)
    qb = q.reshape(B, H, NB, Q_BLOCK, d).transpose(2, 0, 1, 3, 4)
    Fb = F.reshape(B, H, NB, Q_BLOCK).transpose(2, 0, 1, 3)
    kpos = jnp.arange(S)
    scale = 1.0 / np.sqrt(d)

    def block(args):
        qi, Fi, i = args
        qpos = i * Q_BLOCK + jnp.arange(Q_BLOCK)
        logits = (jnp.einsum('bhqd,bhkd->bhqk', qi, k).astype(jnp.float32) * scale
                  + Fi[..., :, None] - F[..., None, :])
        logits = jnp.where(kpos[None, :] <= qpos[:, None], logits, -jnp.inf)
        p = jax.nn.softmax(logits, axis=-1)
        return jnp.einsum('bhqk,bhkd->bhqd', p.astype(v.dtype), v)

    out = lax.map(block, (qb, Fb, jnp.arange(NB)))
    return out.transpose(1, 0, 3, 2, 4).reshape(B, S, H, d)

def setup_inputs(seed: int = 0) -> dict:
    key = jax.random.key(seed)
    ks = jax.random.split(key, 16)
    f32 = jnp.float32
    x = jax.random.normal(ks[0], (BATCH, SEQ, D_MODEL), f32)
    c = jax.random.normal(ks[1], (BATCH, D_MODEL), f32)
    norm_g = 1.0 + 0.02 * jax.random.normal(ks[2], (DEPTH, D_MODEL), f32)
    w_ada = 0.5 * D_MODEL ** -0.5 * jax.random.normal(ks[3], (DEPTH, D_MODEL, 3 * D_MODEL), f32)
    b_ada = 0.02 * jax.random.normal(ks[4], (DEPTH, 3 * D_MODEL), f32)
    w_in = D_MODEL ** -0.5 * jax.random.normal(ks[5], (DEPTH, D_MODEL, D_IN), f32)
    conv_w = CONV_K ** -0.5 * jax.random.normal(ks[6], (DEPTH, CONV_K, 2 * M_W), f32)
    conv_b = 0.01 * jax.random.normal(ks[7], (DEPTH, 2 * M_W), f32)
    b_igate = 0.1 * jax.random.normal(ks[8], (DEPTH, M_HEADS), f32)
    b_fgate_m = (jnp.linspace(3.0, 6.0, M_HEADS, dtype=f32)[None, :]
                 + 0.1 * jax.random.normal(ks[9], (DEPTH, M_HEADS), f32))
    mlstm_norm_g = 1.0 + 0.02 * jax.random.normal(ks[10], (DEPTH, M_W), f32)
    b_fgate_f = (jnp.linspace(1.0, 5.0, F_HEADS, dtype=f32)[None, :]
                 + 0.1 * jax.random.normal(ks[11], (DEPTH, F_HEADS), f32))
    fox_qnorm_g = 1.0 + 0.02 * jax.random.normal(ks[12], (DEPTH, F_DH), f32)
    fox_knorm_g = 1.0 + 0.02 * jax.random.normal(ks[13], (DEPTH, F_DH), f32)
    w_out = D_MIX ** -0.5 * jax.random.normal(ks[14], (DEPTH, D_MIX, D_MODEL), f32)
    return {"x": x, "c": c, "norm_g": norm_g, "w_ada": w_ada, "b_ada": b_ada,
            "w_in": w_in, "conv_w": conv_w, "conv_b": conv_b, "b_igate": b_igate,
            "b_fgate_m": b_fgate_m, "mlstm_norm_g": mlstm_norm_g, "b_fgate_f": b_fgate_f,
            "fox_qnorm_g": fox_qnorm_g, "fox_knorm_g": fox_knorm_g, "w_out": w_out}

def reference(x, c, norm_g, w_ada, b_ada, w_in, conv_w, conv_b, b_igate, b_fgate_m,
              mlstm_norm_g, b_fgate_f, fox_qnorm_g, fox_knorm_g, w_out):
    B, S, _ = x.shape
    f32 = jnp.float32
    for l in range(DEPTH):
        mod = c @ w_ada[l] + b_ada[l]
        shift, scale, gate = jnp.split(mod, 3, axis=-1)
        h = rms_norm(x, norm_g[l]) * (1.0 + scale[:, None, :]) + shift[:, None, :]

        u = h @ w_in[l]
        (m_q, m_k, m_v, m_o, m_z, m_i, m_f,
         f_q, f_k, f_v, f_z, f_f) = jnp.split(u, SPLIT_IDX, axis=-1)

        qk = jax.nn.silu(causal_depthwise_conv(jnp.concatenate([m_q, m_k], axis=-1),
                                               conv_w[l], conv_b[l]))
        mq, mk = jnp.split(qk, 2, axis=-1)
        to_bhsd = lambda a, H, d: a.reshape(B, S, H, d).transpose(0, 2, 1, 3).astype(f32)
        mq = to_bhsd(mq, M_HEADS, M_DH)
        mk = to_bhsd(mk, M_HEADS, M_DH) * (1.0 / np.sqrt(M_DH))
        mv = to_bhsd(m_v, M_HEADS, M_DH)
        ig = (m_i.astype(f32) + b_igate[l].astype(f32)).transpose(0, 2, 1)
        lf = jax.nn.log_sigmoid(m_f.astype(f32) + b_fgate_m[l].astype(f32)).transpose(0, 2, 1)
        h_m = mlstm_chunkwise(mq, mk, mv, ig, lf)
        h_m = jax.nn.sigmoid(m_o.astype(f32)).reshape(B, S, M_HEADS, M_DH) * h_m
        y_m = head_layer_norm(h_m, mlstm_norm_g[l]).astype(x.dtype) * jax.nn.silu(m_z)

        fq = rms_norm(f_q.reshape(B, S, F_HEADS, F_DH), fox_qnorm_g[l]).transpose(0, 2, 1, 3)
        fk = rms_norm(f_k.reshape(B, S, F_HEADS, F_DH), fox_knorm_g[l]).transpose(0, 2, 1, 3)
        fv = f_v.reshape(B, S, F_HEADS, F_DH).transpose(0, 2, 1, 3)
        logf = jax.nn.log_sigmoid(f_f.astype(f32) + b_fgate_f[l].astype(f32)).transpose(0, 2, 1)
        h_f = forgetting_attention(fq, fk, fv, logf)
        y_f = h_f.reshape(B, S, F_W).astype(x.dtype) * jax.nn.silu(f_z)

        y = jnp.concatenate([y_m, y_f], axis=-1) @ w_out[l]
        x = x + gate[:, None, :] * y
    return x


_drawn_inputs = setup_inputs


def setup_inputs(seed=0):
    import zlib

    import numpy as np

    out = dict(_drawn_inputs(seed))
    spreads = {}
    factors = {'norm_g': 6.396,
     'b_ada': 2.937,
     'conv_b': 64.0,
     'b_igate': 64.0,
     'mlstm_norm_g': 29.023,
     'fox_qnorm_g': 8.0,
     'fox_knorm_g': 8.0}
    for name, (base, spread) in spreads.items():
        noise = np.random.default_rng([zlib.crc32(name.encode()), seed]).standard_normal(out[name].shape)
        drawn = base * np.exp(spread * noise) if base else spread * noise
        out[name] = __import__('jax').numpy.asarray(drawn.astype(out[name].dtype))
    for name, factor in factors.items():
        out[name] = (out[name] * factor).astype(out[name].dtype)
    return out
```

```python
from contextlib import ExitStack

import concourse.bass as bass
from concourse import mybir

F32 = mybir.dt.float32
F32R = mybir.dt.float32r
ALU = mybir.AluOpType
ACT = mybir.ActivationFunctionType
AX_X = mybir.AxisListType.X

P = 128
D_MODEL = 1024
SEQ = 2048
EPS = 1e-6
KT = D_MODEL // P
TT = SEQ // P
NB = 512
TB = SEQ // NB

M_HEADS, M_DH = 4, 128
F_HEADS, F_DH = 8, 64
M_W, F_W = M_HEADS * M_DH, F_HEADS * F_DH
CONV_K = 4

M_GATES = 5 * M_W
F_Q = M_GATES + 2 * M_HEADS
F_GATES = F_Q + 4 * F_W
D_IN = F_GATES + F_HEADS
M_TILES = 5 * M_W // P
F_TILES = 4 * F_W // P
U_TILES = M_TILES + F_TILES
HEADS_IN_TILE = P // F_DH
PARAM_ROWS = (CONV_K + 1) * 2 * M_HEADS + 2 + M_HEADS
CHUNK = 128
CHUNKS = SEQ // CHUNK
A_FV, A_MV, A_MO, A_MQ, A_MK, A_MZ, A_FZ = (i * M_HEADS for i in range(7))
COL_G, COL_WS, COL_EM, GATE_COLS = 0, 32, 64, 64 + M_HEADS
NORM_GAIN = (CONV_K + 1) * 2 * M_HEADS + 2
EXP_MAX = 88.0
MASKED = -1e30
X_GROUPS = TT * P // NB
X_FOLD = [g if g < X_GROUPS else X_GROUPS + 2 * (g - X_GROUPS) for g in range(2 * X_GROUPS)]
X_Y = [X_GROUPS + 2 * (J + 1) for J in range(X_GROUPS)]
X_READS = 3 * X_GROUPS
ROW_I, ROW_F, ROW_FF = 0, 32, 64


def modulate_and_project(nc, a, scratch, keep):
    with ExitStack() as ctx:
        def sb(name, shape, dt=F32):
            return ctx.enter_context(nc.sbuf_tensor("a_" + name, shape, dt))

        def sem(name):
            return ctx.enter_context(nc.semaphore("a_" + name))

        UN = 4
        WP = 256
        AR = 4
        PIECES = 3 * D_MODEL // WP
        COL_PIECES = 2 * D_MODEL // WP
        assert PIECES % AR == 0 and COL_PIECES % AR == 0

        H_SLOTS = 2
        params, qk_gain = keep["params"], keep["qk_gain"]
        h_hi = sb("h_hi", [P, KT, SEQ], F32R)
        h_lo = sb("h_lo", [P, KT, SEQ], F32R)

        with ExitStack() as early:
            def esb(name, shape, dt=F32):
                return early.enter_context(nc.sbuf_tensor("a0_" + name, shape, dt))

            x_ring = esb("x_ring", [P, UN, D_MODEL])
            w_ring = esb("w_ring", [P, AR, KT, WP])
            h_part = esb("h_part", [P, 2, KT, P])
            vec_rows = esb("vec_rows", [4 * KT, P])
            vec_cols = esb("vec_cols", [P, 4 * KT])
            c_wide = esb("c_wide", [P, KT, P])
            ident = esb("ident", [P, P])
            mod_a = esb("mod_a", [P, KT])
            mod_b = esb("mod_b", [P, KT])
            scale1 = esb("scale1", [P, KT])
            b_gate = esb("b_gate", [P, D_MODEL])
            sumsq = esb("sumsq", [P, TT])
            meansq = esb("meansq", [P, TT])
            inv_ms = esb("inv_ms", [P, TT])
            rstd = esb("rstd", [P, TT])
            junk = esb("junk", [P, D_MODEL])
            ps_t = early.enter_context(nc.psum_tensor("a0_ps_t", [P, 2, KT, P], F32))
            ps_v = early.enter_context(nc.psum_tensor("a0_ps_v", [P, NB], F32))
            ps_m = early.enter_context(nc.psum_tensor("a0_ps_m", [P, NB], F32))
            ps_g = early.enter_context(nc.psum_tensor("a0_ps_g", [P, NB], F32))

            vec_landed = sem("vec_landed")
            bgate_landed = sem("bgate_landed")
            x_landed = [sem(f"x_landed{u}") for u in range(UN)]
            w_landed = [sem(f"w_landed{u}") for u in range(AR)]
            w_used = sem("w_used")
            zeroed = sem("zeroed")
            ident_ready = sem("ident_ready")
            vec_transposed = sem("vec_transposed")
            vec_ready = sem("vec_ready")
            cwide_ready = sem("cwide_ready")
            scale1_done = sem("scale1_done")
            mod_ready = sem("mod_ready")
            gate_psum = sem("gate_psum")
            gate_taken = sem("gate_taken")
            gate_stored = sem("gate_stored")
            sumsq_ready = sem("sumsq_ready")
            meansq_ready = sem("meansq_ready")
            inv_ready = sem("inv_ready")
            rstd_ready = sem("rstd_ready")
            x_scaled = sem("x_scaled")
            xt_psum = sem("xt_psum")
            xt_taken = sem("xt_taken")
            hi_ready = sem("hi_ready")
            split_done = sem("split_done")

            block = early.enter_context(nc.Block())

            @block.sync
            def _(sp):
                sp.dma_start(vec_rows[0:KT, :], a["c"].rearrange("b (k p) -> (b k) p", p=P)).then_inc(vec_landed, 16)
                sp.dma_start(vec_rows[KT:2 * KT, :],
                             a["norm_g"].rearrange("b (k p) -> (b k) p", p=P)).then_inc(vec_landed, 16)
                sp.dma_start(vec_rows[2 * KT:4 * KT, :],
                             a["b_ada"].rearrange("b (k p) -> (b k) p", p=P)[0:2 * KT, :]).then_inc(vec_landed, 16)
                with sp.Fori(0, TT // UN) as n:
                    for u in range(UN):
                        sp.wait_ge(xt_psum, n * UN + u + 1)
                        sp.dma_start(x_ring[:, u, :],
                                     a["x"][0, bass.ds((n * UN + u) * P, P), :]).then_inc(x_landed[u], 16)
                sp.dma_start(b_gate[:, :],
                             a["b_ada"][0:1, 2 * D_MODEL:3 * D_MODEL].broadcast_to([P, D_MODEL])).then_inc(bgate_landed, 16)
                sp.wait_ge(gate_taken, PIECES - COL_PIECES)
                sp.dma_start(scratch["gate"], b_gate[:, :]).then_inc(gate_stored, 16)
                sp.wait_ge(gate_stored, 16)

            @block.gpsimd
            def _(pool):
                w_view = a["w_ada"][0].rearrange("(k p) n -> p k n", p=P)
                pool.memset(ident[:, :], 0.0).then_inc(zeroed, 1)
                pool.wait_ge(zeroed, 1)
                pool.affine_select(out=ident[:, :], in_=ident[:, :], compare_op=ALU.not_equal, fill=1.0, base=0,
                                   pattern=[[-1, P]], channel_multiplier=1).then_inc(ident_ready, 1)
                with pool.Fori(0, PIECES // AR) as n:
                    for u in range(AR):
                        pool.wait_ge(w_used, n * AR + u + 1)
                        pool.dma_start(w_ring[:, u], w_view[:, :, bass.ds((n * AR + u) * WP, WP)]).then_inc(w_landed[u], 16)

            @block.scalar
            def _(act):
                act.preload_act_table(ACT.Sqrt)
                act.sem_inc(xt_taken, H_SLOTS)

                def rms(n, u, t):
                    act.wait_ge(x_landed[u], (n + 1) * 16)
                    act.activation(junk[:, :], x_ring[:, u, :], ACT.Square,
                                   accum_out=sumsq[:, bass.ds(t, 1)]).then_inc(sumsq_ready, 1)
                    act.wait_ge(inv_ready, t + 1)
                    act.activation(rstd[:, bass.ds(t, 1)], inv_ms[:, bass.ds(t, 1)], ACT.Sqrt).then_inc(rstd_ready, 1)

                def modulated(u, t):
                    act.wait_ge(xt_psum, t + 1 + UN)
                    act.wait_ge(split_done, t + 1)
                    for k in range(KT):
                        ins = act.activation(h_part[:, u % 2, k, :], ps_t[:, u % 2, k, :], ACT.Identity,
                                             bias=mod_b[:, k:k + 1], scale=mod_a[:, k:k + 1])
                    ins.then_inc(xt_taken, 1)

                rms(0, 0, 0)
                act.wait_ge(mod_ready, 2)
                with act.Fori(0, TT // UN - 1) as n:
                    for u in range(UN):
                        rms(n + (u + 1) // UN, (u + 1) % UN, n * UN + u + 1)
                        modulated(u, n * UN + u)
                for u in range(UN):
                    if u + 1 < UN:
                        rms(TT // UN - 1, u + 1, TT - UN + u + 1)
                    modulated(u, TT - UN + u)

            @block.vector
            def _(dve):
                dve.sem_inc(split_done, H_SLOTS)
                dve.wait_ge(vec_transposed, 1)
                dve.tensor_copy(vec_cols[:, :], ps_v[:, 0:4 * KT]).then_inc(vec_ready, 1)
                dve.wait_ge(vec_ready, 1)
                dve.tensor_copy(c_wide[:, :, :],
                                vec_cols[:, 0:KT].unsqueeze(2).broadcast_to([P, KT, P])).then_inc(cwide_ready, 1)

                def normalised(u, t):
                    dve.wait_ge(sumsq_ready, t + 1)
                    dve.tensor_scalar(meansq[:, bass.ds(t, 1)], sumsq[:, bass.ds(t, 1)], 1.0 / D_MODEL, EPS,
                                      ALU.mult, ALU.add).then_inc(meansq_ready, 1)
                    dve.wait_ge(meansq_ready, t + 1)
                    dve.reciprocal(inv_ms[:, bass.ds(t, 1)], meansq[:, bass.ds(t, 1)]).then_inc(inv_ready, 1)
                    dve.wait_ge(rstd_ready, t + 1)
                    dve.tensor_scalar(x_ring[:, u, :], x_ring[:, u, :], rstd[:, bass.ds(t, 1)], None,
                                      ALU.mult).then_inc(x_scaled, 1)

                def split(u, t):
                    dve.wait_ge(xt_taken, t + 1 + H_SLOTS)
                    dve.tensor_copy(h_hi[:, :, bass.ds(t * P, P)], h_part[:, u % 2]).then_inc(hi_ready, 1)
                    dve.wait_ge(hi_ready, t + 1)
                    dve.tensor_sub(h_lo[:, :, bass.ds(t * P, P)], h_part[:, u % 2],
                                   h_hi[:, :, bass.ds(t * P, P)].bitcast(F32)).then_inc(split_done, 1)

                normalised(0, 0)
                dve.wait_ge(w_used, AR + COL_PIECES)
                dve.tensor_scalar(scale1[:, :], ps_m[:, KT:2 * KT], 1.0, None, ALU.add).then_inc(scale1_done, 1)
                dve.wait_ge(scale1_done, 1)
                dve.tensor_add(scale1[:, :], scale1[:, :], vec_cols[:, 3 * KT:4 * KT]).then_inc(scale1_done, 1)
                dve.wait_ge(scale1_done, 2)
                dve.tensor_mul(mod_a[:, :], scale1[:, :], vec_cols[:, KT:2 * KT]).then_inc(mod_ready, 1)
                dve.tensor_add(mod_b[:, :], ps_m[:, 0:KT], vec_cols[:, 2 * KT:3 * KT]).then_inc(mod_ready, 1)
                with dve.Fori(0, TT // UN - 1) as n:
                    for u in range(UN):
                        normalised((u + 1) % UN, n * UN + u + 1)
                        split(u, n * UN + u)
                for u in range(UN):
                    if u + 1 < UN:
                        normalised(u + 1, TT - UN + u + 1)
                    split(u, TT - UN + u)
                dve.wait_ge(bgate_landed, 16)
                for q in range(PIECES - COL_PIECES):
                    dve.wait_ge(gate_psum, q + 1)
                    part = b_gate[:, q * WP:(q + 1) * WP]
                    dve.tensor_add(part, ps_g[:, 0:WP], part).then_inc(gate_taken, 1)

            @block.tensor
            def _(pe):
                pe.sem_inc(xt_psum, UN)
                pe.sem_inc(w_used, AR)
                pe.wait_ge(vec_landed, 48)
                pe.wait_ge(ident_ready, 1)
                pe.transpose(ps_v[:, 0:4 * KT], vec_rows[:, :], ident[0:4 * KT, 0:4 * KT]).then_inc(vec_transposed, 1)
                pe.wait_ge(vec_ready, 1)
                for q in range(COL_PIECES):
                    pe.wait_ge(w_landed[q % AR], (q // AR + 1) * 16)
                    for j in range(WP // P):
                        col = q * (WP // P) + j
                        for k in range(KT):
                            ins = pe.matmul(ps_m[:, col:col + 1], w_ring[:, q % AR, k, j * P:(j + 1) * P],
                                            vec_cols[:, k:k + 1], start=(k == 0), stop=(k == KT - 1))
                    ins.then_inc(w_used, 1)
                with pe.Fori(0, TT // UN) as n:
                    for u in range(UN):
                        t = n * UN + u
                        pe.wait_ge(x_scaled, t + 1)
                        pe.wait_ge(xt_taken, t + 1)
                        for k in range(KT):
                            ins = pe.transpose(ps_t[:, u % 2, k, :], x_ring[:, u, k * P:(k + 1) * P], ident[:, :])
                        ins.then_inc(xt_psum, 1)
                pe.wait_ge(cwide_ready, 1)
                for q in range(COL_PIECES, PIECES):
                    pe.wait_ge(w_landed[q % AR], (q // AR + 1) * 16)
                    if q > COL_PIECES:
                        pe.wait_ge(gate_taken, q - COL_PIECES)
                    for k in range(KT):
                        ins = pe.matmul(ps_g[:, 0:WP], c_wide[:, k, :], w_ring[:, q % AR, k, :],
                                        start=(k == 0), stop=(k == KT - 1))
                    ins.then_inc(gate_psum, 1)

        with ExitStack() as late:
            def lsb(name, shape, dt=F32):
                return late.enter_context(nc.sbuf_tensor("a1_" + name, shape, dt))

            w_land = lsb("w_land", [P, 2, KT, P])
            w_hi = lsb("w_hi", [P, 2, KT, P], F32R)
            w_lo = lsb("w_lo", [P, 2, KT, P], F32R)
            wg_land = lsb("wg_land", [P, KT, 2 * M_HEADS + F_HEADS])
            wg_hi = lsb("wg_hi", [P, KT, P], F32R)
            wg_lo = lsb("wg_lo", [P, KT, P], F32R)
            u_copy = lsb("u_copy", [P, 2, SEQ])
            work = lsb("work", [P, SEQ])
            stage = lsb("stage", [P, 2, SEQ])
            head_mean = lsb("head_mean", [P, HEADS_IN_TILE])
            inv_rms = lsb("inv_rms", [P, TT * HEADS_IN_TILE])
            ident = lsb("ident", [P, P])
            par_rows = lsb("par_rows", [PARAM_ROWS, P])
            ps_u = late.enter_context(nc.psum_tensor("a1_ps_u", [P, 2, TB, NB], F32))

            w_landed = [sem(f"wi_landed{u}") for u in range(2)]
            wg_landed = sem("wg_landed")
            param_landed = sem("param_landed")
            const_zeroed = sem("const_zeroed")
            const_ready = sem("const_ready")
            hi_ready = sem("w_hi_ready")
            w_split = sem("w_split")
            wg_split = sem("wg_split")
            u_psum = sem("u_psum")
            half_free = sem("half_free")
            param_psum = sem("param_psum")
            gain_ready = sem("gain_ready")
            u_copied = sem("u_copied")
            squared = sem("squared")
            means_psum = sem("means_psum")
            spread = sem("spread")
            post_psum = sem("post_psum")
            mean_ready = sem("mean_ready")
            inverse_ready = sem("inverse_ready")
            root_ready = sem("root_ready")
            stage_hi = sem("stage_hi")
            sigmoid_ready = sem("sigmoid_ready")
            conv_started = sem("conv_started")
            tap_done = sem("tap_done")
            finished = sem("finished")
            stored = sem("stored")
            rows_stored = sem("rows_stored")

            w_view = a["w_in"][0].rearrange("(k p) n -> p k n", p=P)
            G = M_HEADS
            LOADS = ((0, 3 * G, F_Q), (3 * G, 2 * G, 2 * M_W), (5 * G, 2 * G, 0), (7 * G, G, 4 * M_W),
                     (8 * G, G, F_Q + 3 * F_W))
            NORM, TURN, CONV, SILU = 0, 2 * G, 5 * G, 7 * G
            END = 9 * G
            assert END == U_TILES and G % 2 == 0
            block = late.enter_context(nc.Block())

            @block.sync
            def _(sp):
                sp.dma_start(wg_land[:, :, 0:2 * M_HEADS], w_view[:, :, M_GATES:F_Q]).then_inc(wg_landed, 16)
                sp.dma_start(wg_land[:, :, 2 * M_HEADS:], w_view[:, :, F_GATES:D_IN]).then_inc(wg_landed, 16)
                for first, count, column in LOADS:
                    with sp.Fori(0, count // 2) as n:
                        for par in range(2):
                            sp.wait_ge(w_split, n * 2 + par + first + 1)
                            sp.dma_start(w_land[:, par],
                                         w_view[:, :, bass.ds((n * 2 + par) * P + column, P)]).then_inc(w_landed[par], 16)

            @block.gpsimd
            def _(pool):
                pool.memset(ident[:, :], 0.0).then_inc(const_zeroed, 1)
                pool.memset(head_mean[:, :], 0.0).then_inc(const_zeroed, 1)
                pool.wait_ge(const_zeroed, 2)
                pool.affine_select(out=ident[:, :], in_=ident[:, :], compare_op=ALU.not_equal, fill=1.0, base=0,
                                   pattern=[[-1, P]], channel_multiplier=1).then_inc(const_ready, 1)
                for h in range(HEADS_IN_TILE):
                    part = slice(h * F_DH, (h + 1) * F_DH)
                    pool.wait_ge(const_ready, h + 1)
                    pool.memset(head_mean[part, h:h + 1], 1.0 / F_DH).then_inc(const_ready, 1)
                pool.dma_start(par_rows[0:32, :], a["conv_w"][0].rearrange("k (j p) -> (k j) p", p=P)).then_inc(param_landed, 16)
                pool.dma_start(par_rows[32:40, :], a["conv_b"].rearrange("b (j p) -> (b j) p", p=P)).then_inc(param_landed, 16)
                for h in range(HEADS_IN_TILE):
                    part = slice(h * F_DH, (h + 1) * F_DH)
                    pool.dma_start(par_rows[40:41, part], a["fox_qnorm_g"][:, :]).then_inc(param_landed, 16)
                    pool.dma_start(par_rows[41:42, part], a["fox_knorm_g"][:, :]).then_inc(param_landed, 16)
                pool.dma_start(par_rows[42:46, :],
                               a["mlstm_norm_g"].rearrange("b (j p) -> (b j) p", p=P)).then_inc(param_landed, 16)
                pool.wait_ge(finished, 1 + 2)
                pool.dma_start(scratch["gate_rows"], stage[0:ROW_FF + F_HEADS, 0, :]).then_inc(rows_stored, 16)

                def store(out, j, sb_view):
                    pool.wait_ge(finished, j + 4)
                    pool.dma_start(out, sb_view).then_inc(stored, 16)

                with pool.Fori(0, (TURN - NORM)) as n:
                    store(scratch["qkT"][:, bass.ds(n * P, P), :].rearrange("s p c -> p s c"), n + NORM, stage[:, :, :])
                with pool.Fori(0, END - TURN) as n:
                    store(scratch["arrays"][bass.ds(n * P, P), :], n + TURN, stage[:, 0, :])
                pool.wait_ge(stored, END * 16)
                pool.wait_ge(rows_stored, 16)

            @block.vector
            def _(dve):
                dve.sem_inc(w_split, 2)
                dve.sem_inc(finished, 2)

                def split_w(par, n, j):
                    dve.wait_ge(w_landed[par], (n + 1) * 16)
                    dve.tensor_copy(w_hi[:, par], w_land[:, par]).then_inc(hi_ready, 1)
                    dve.wait_ge(hi_ready, j + 1)
                    dve.tensor_sub(w_lo[:, par], w_land[:, par], w_hi[:, par].bitcast(F32)).then_inc(w_split, 1)

                dve.memset(wg_hi[:, :, :].bitcast(F32), 0.0).then_inc(wg_split, 1)
                dve.memset(wg_lo[:, :, :].bitcast(F32), 0.0).then_inc(wg_split, 1)
                dve.wait_ge(wg_landed, 32)
                dve.wait_ge(wg_split, 2)
                for n, (row, first, count) in enumerate(((ROW_I, 0, M_HEADS), (ROW_F, M_HEADS, M_HEADS),
                                                         (ROW_FF, 2 * M_HEADS, F_HEADS))):
                    part = wg_land[:, :, first:first + count]
                    hi = wg_hi[:, :, row:row + count]
                    dve.tensor_copy(hi, part).then_inc(wg_split, 1)
                    dve.wait_ge(wg_split, 3 + 2 * n)
                    dve.tensor_sub(wg_lo[:, :, row:row + count], part, hi.bitcast(F32)).then_inc(wg_split, 1)
                split_w(0, 0, 0)
                split_w(1, 0, 1)
                dve.wait_ge(param_psum, 1)
                dve.tensor_copy(params[:, :], ps_u[:, 0, 0, 0:PARAM_ROWS]).then_inc(half_free, 1)
                dve.wait_ge(u_psum, 1)
                dve.tensor_copy(stage[0:ROW_FF + F_HEADS, 0, :],
                                ps_u[0:ROW_FF + F_HEADS, 1].rearrange("p b n -> p (b n)")).then_inc(half_free, 1)
                dve.wait_ge(half_free, 2)
                dve.sem_inc(finished, 1)
                dve.wait_ge(rows_stored, 16)

                def begin(par, n, j, split=True):
                    dve.wait_ge(u_psum, j + 2)
                    if split:
                        split_w(par, n + 1, j + 2)

                def flat(par):
                    return ps_u[:, par].rearrange("p b n -> p (b n)")

                dve.wait_ge(gain_ready, 1)
                with dve.Fori(0, (TURN - NORM) // 2) as n:
                    for par in range(2):
                        j = n * 2 + par
                        begin(par, n, j)
                        dve.wait_ge(means_psum, j + 1)
                        dve.tensor_scalar(inv_rms[:, :], ps_u[:, par, 0, 0:TT * HEADS_IN_TILE], EPS, None,
                                          ALU.add).then_inc(mean_ready, 1)
                        dve.wait_ge(mean_ready, j + 1)
                        dve.reciprocal(inv_rms[:, :], inv_rms[:, :]).then_inc(inverse_ready, 1)
                        dve.wait_ge(root_ready, j + 1)
                        dve.tensor_copy(work[:, :].rearrange("p (t d) -> p t d", d=F_DH),
                                        inv_rms[:, :].unsqueeze(2).broadcast_to([P, TT * HEADS_IN_TILE, F_DH])
                                        ).then_inc(spread, 1)
                        dve.wait_ge(post_psum, j + 1)
                        dve.scalar_tensor_tensor(out=u_copy[:, par, :], in0=u_copy[:, par, :],
                                                 scalar=qk_gain[:, bass.ds(j, 1)], in1=flat(par),
                                                 op0=ALU.mult, op1=ALU.mult).then_inc(half_free, 1)
                        dve.wait_ge(half_free, j + 3)
                        dve.wait_ge(stored, j * 16)
                        dve.tensor_copy(stage[:, 0, :].bitcast(F32R), u_copy[:, par, :]).then_inc(stage_hi, 1)
                        dve.wait_ge(stage_hi, j + 1)
                        dve.tensor_sub(stage[:, 1, :].bitcast(F32R), u_copy[:, par, :],
                                       stage[:, 0, :]).then_inc(finished, 1)
                with dve.Fori(0, (CONV - TURN) // 2) as n:
                    for par in range(2):
                        j = n * 2 + par + TURN
                        begin(par, n + TURN // 2, j)
                        dve.wait_ge(post_psum, j + 1)
                        dve.wait_ge(stored, j * 16)
                        dve.tensor_copy(stage[:, 0, :], flat(par)).then_inc(finished, 1)
                        dve.wait_ge(finished, j + 4)
                        dve.sem_inc(half_free, 1)
                for kind, factor in ((0, 1.0), (1, float(M_DH) ** -0.5)):
                    with dve.Fori(0, G // 2) as n:
                        for par in range(2):
                            i = n * 2 + par + kind * G
                            j = i + CONV
                            begin(par, n + (CONV + kind * G) // 2, j)
                            dve.wait_ge(conv_started, i + 1)
                            for s in range(1, CONV_K):
                                dve.scalar_tensor_tensor(
                                    out=work[:, s:], in0=u_copy[:, par, 0:SEQ - s],
                                    scalar=params[:, bass.ds(i + (CONV_K - 1 - s) * 2 * G, 1)],
                                    in1=work[:, s:], op0=ALU.mult, op1=ALU.add).then_inc(tap_done, 1)
                                dve.wait_ge(tap_done, i * (CONV_K - 1) + s)
                                if s == 1:
                                    dve.sem_inc(half_free, 1)
                            dve.wait_ge(sigmoid_ready, i + 1)
                            dve.wait_ge(stored, j * 16)
                            dve.scalar_tensor_tensor(out=stage[:, 0, :], in0=work[:, :], scalar=factor,
                                                     in1=stage[:, 1, :], op0=ALU.mult, op1=ALU.mult).then_inc(finished, 1)

                def silu(par, n, j, split):
                    begin(par, n, j, split)
                    dve.wait_ge(sigmoid_ready, j - CONV + 1)
                    dve.wait_ge(stored, j * 16)
                    dve.tensor_mul(stage[:, 0, :], flat(par), work[:, :]).then_inc(finished, 1)
                    dve.wait_ge(finished, j + 4)
                    dve.sem_inc(half_free, 1)

                with dve.Fori(0, (END - SILU) // 2 - 1) as n:
                    for par in range(2):
                        silu(par, n + SILU // 2, n * 2 + par + SILU, True)
                for par in range(2):
                    silu(par, 0, END - 2 + par, False)

            @block.tensor
            def _(pe):
                def project(par, j, hi, lo, post=()):
                    for k in range(KT):
                        for b in range(TB):
                            cols = slice(b * NB, (b + 1) * NB)
                            pe.matmul(ps_u[:, par, b, :], hi[:, k, :], h_hi[:, k, cols], start=(k == 0), stop=False)
                            pe.matmul(ps_u[:, par, b, :], hi[:, k, :], h_lo[:, k, cols], start=False, stop=False)
                        for b in range(TB):
                            cols = slice(b * NB, (b + 1) * NB)
                            ins = pe.matmul(ps_u[:, par, b, :], lo[:, k, :], h_hi[:, k, cols],
                                            start=False, stop=(k == KT - 1))
                        for at, step in post:
                            if k == at:
                                step(1 - par, j - 1)
                    ins.then_inc(u_psum, 1)

                def tile(par, j, post=()):
                    pe.wait_ge(w_split, j + 3)
                    pe.wait_ge(half_free, j + 1)
                    project(par, j, w_hi[:, par], w_lo[:, par], post)

                def head_means(par, j):
                    pe.wait_ge(squared, j + 1)
                    for t in range(TT):
                        ins = pe.matmul(ps_u[:, par, 0, t * HEADS_IN_TILE:(t + 1) * HEADS_IN_TILE],
                                        work[:, t * P:(t + 1) * P], head_mean[:, :], start=True, stop=True)
                    ins.then_inc(means_psum, 1)

                def turn(par, source):
                    view = ps_u[:, par].rearrange("p b (t n) -> p (b t) n", n=P)
                    for t in range(TT):
                        ins = pe.transpose(view[:, t, :], source[:, t * P:(t + 1) * P], ident[:, :])
                    ins.then_inc(post_psum, 1)

                def turned_norms(par, j):
                    pe.wait_ge(spread, j + 1)
                    turn(par, work)

                def turned(par, j):
                    pe.wait_ge(u_copied, j + 1)
                    turn(par, u_copy[:, par])

                pe.wait_ge(const_ready, 3)
                pe.wait_ge(param_landed, 7 * 16)
                pe.transpose(ps_u[:, 0, 0, 0:PARAM_ROWS], par_rows[:, :],
                             ident[0:PARAM_ROWS, 0:PARAM_ROWS]).then_inc(param_psum, 1)
                pe.wait_ge(wg_split, 8)
                project(1, 0, wg_hi[:, :, :], wg_lo[:, :, :])
                tile(0, 0)
                with pe.Fori(0, (TURN - NORM) // 2) as n:
                    tile(1, n * 2 + 1, ((2, head_means), (5, turned_norms)))
                    tile(0, n * 2 + 2, ((2, head_means), (5, turned_norms)))
                with pe.Fori(0, (CONV - TURN) // 2) as n:
                    tile(1, n * 2 + 1 + TURN, ((2, turned),))
                    tile(0, n * 2 + 2 + TURN, ((2, turned),))
                with pe.Fori(0, (END - CONV) // 2 - 1) as n:
                    tile(1, n * 2 + 1 + CONV)
                    tile(0, n * 2 + 2 + CONV)
                tile(1, END - 1)

            @block.scalar
            def _(act):
                def copy(par, j, func=ACT.Copy):
                    act.wait_ge(u_psum, j + 2)
                    act.wait_ge(finished, j + 2)
                    return act.activation(u_copy[:, par, :], flat(par), func)

                def flat(par):
                    return ps_u[:, par].rearrange("p b n -> p (b n)")

                act.preload_act_table(ACT.Sqrt)
                act.wait_ge(half_free, 1)
                act.activation(qk_gain[:, 0:G], params[:, 40:41].broadcast_to([P, G]), ACT.Copy,
                               scale=float(F_DH) ** -0.5)
                act.activation(qk_gain[:, G:2 * G], params[:, 41:42].broadcast_to([P, G]), ACT.Copy).then_inc(gain_ready, 1)
                with act.Fori(0, (TURN - NORM) // 2) as n:
                    for par in range(2):
                        j = n * 2 + par
                        copy(par, j).then_inc(u_copied, 1)
                        act.wait_ge(finished, j + 3)
                        act.activation(work[:, :], flat(par), ACT.Square).then_inc(squared, 1)
                        act.wait_ge(inverse_ready, j + 1)
                        act.activation(inv_rms[:, :], inv_rms[:, :], ACT.Sqrt).then_inc(root_ready, 1)
                with act.Fori(0, G) as n:
                    for par in range(2):
                        copy(par, n * 2 + par + TURN).then_inc(u_copied, 1)
                act.preload_act_table(ACT.Sigmoid)
                with act.Fori(0, G // 2) as n:
                    for par in range(2):
                        copy(par, n * 2 + par + TURN + 2 * G, ACT.Sigmoid).then_inc(u_copied, 1)
                with act.Fori(0, G) as n:
                    for par in range(2):
                        i = n * 2 + par
                        copy(par, i + CONV)
                        act.wait_ge(finished, i + CONV + 3)
                        act.activation(work[:, :], flat(par), ACT.Identity,
                                       bias=params[:, bass.ds(i + CONV_K * 2 * G, 1)],
                                       scale=params[:, bass.ds(i + (CONV_K - 1) * 2 * G, 1)]).then_inc(conv_started, 1)
                        act.wait_ge(tap_done, (i + 1) * (CONV_K - 1))
                        act.activation(stage[:, 1, :], work[:, :], ACT.Sigmoid).then_inc(sigmoid_ready, 1)
                with act.Fori(0, (END - SILU) // 2) as n:
                    for par in range(2):
                        j = n * 2 + par + SILU
                        act.wait_ge(u_psum, j + 2)
                        act.wait_ge(finished, j + 3)
                        act.activation(work[:, :], flat(par), ACT.Sigmoid).then_inc(sigmoid_ready, 1)




def gate_rows(nc, a, scratch, keep):
    with ExitStack() as ctx:
        def sb(name, shape, dt=F32):
            return ctx.enter_context(nc.sbuf_tensor("g_" + name, shape, dt))

        def sem(name):
            return ctx.enter_context(nc.semaphore("g_" + name))

        R = ROW_FF + F_HEADS
        I, F, FF = slice(ROW_I, ROW_I + M_HEADS), slice(ROW_F, ROW_F + M_HEADS), slice(ROW_FF, ROW_FF + F_HEADS)
        LOGS = slice(0, R)
        pre = sb("pre", [R, SEQ])
        bias = sb("bias", [R, 1])
        log_f = sb("log_f", [R, SEQ])
        keep_on = sb("keep_on", [R, SEQ])
        neg_sum = sb("neg_sum", [R, SEQ])
        chunk_sum = sb("chunk_sum", [R, SEQ])
        b_row = sb("b_row", [M_HEADS, SEQ])
        carried = sb("carried", [M_HEADS, SEQ])
        g_max = sb("g_max", [M_HEADS, SEQ])
        m_prev = sb("m_prev", [M_HEADS, CHUNKS])
        last_b = sb("last_b", [M_HEADS, CHUNKS])
        weight_in = sb("weight_in", [M_HEADS, SEQ])
        decay = sb("decay", [M_HEADS, CHUNKS])
        columns = sb("columns", [GATE_COLS, SEQ])
        ident = sb("ident", [P, P])
        ps = ctx.enter_context(nc.psum_tensor("g_ps", [P, CHUNKS, P], F32))

        landed = sem("landed")
        zeroed = sem("zeroed")
        ident_ready = sem("ident_ready")
        reset_ready = sem("reset_ready")
        step = {name: sem(name) for name in (
            "bias_zero", "biased", "magnitude", "exp_neg", "log1p", "log_ready", "neg_sum_ready", "chunk_ready",
            "b_ready", "g_ready", "last_ready", "carried_ready", "g_max_ready", "m_prev_ready", "differences",
            "exponentials", "turned", "stored")}

        def chunked(row):
            return row.rearrange("h (c t) -> h c t", t=CHUNK)

        block = ctx.enter_context(nc.Block())

        @block.sync
        def _(sp):
            sp.dma_start(pre[:, :], scratch["gate_rows"]).then_inc(landed, 16)
            sp.wait_ge(step["bias_zero"], 1)
            for rows, name in ((I, "b_igate"), (F, "b_fgate_m"), (FF, "b_fgate_f")):
                sp.dma_start(bias[rows, :], a[name].rearrange("b h -> h b")).then_inc(landed, 16)
            sp.wait_ge(step["neg_sum_ready"], 1)
            sp.dma_start(scratch["f_negF"], neg_sum[FF, :]).then_inc(step["stored"], 16)
            sp.wait_ge(step["g_max_ready"], 1)
            sp.dma_start(scratch["m_G"], g_max[:, :]).then_inc(step["stored"], 16)
            sp.wait_ge(step["exponentials"], 4)
            sp.dma_start(scratch["m_in"], weight_in[:, :]).then_inc(step["stored"], 16)
            sp.dma_start(scratch["m_decay"], decay[:, :]).then_inc(step["stored"], 16)
            sp.wait_ge(step["stored"], 4 * 16)

        @block.gpsimd
        def _(pool):
            pool.memset(ident[:, :], 0.0).then_inc(zeroed, 1)
            pool.wait_ge(zeroed, 1)
            pool.affine_select(out=ident[:, :], in_=ident[:, :], compare_op=ALU.not_equal, fill=1.0, base=0,
                               pattern=[[-1, P]], channel_multiplier=1).then_inc(ident_ready, 1)
            pool.memset(columns[:, :], 0.0).then_inc(zeroed, 1)
            pool.memset(carried[:, :], 0.0).then_inc(zeroed, 1)
            pool.memset(keep_on[:, :], 1.0).then_inc(zeroed, 1)
            pool.wait_ge(zeroed, 4)
            pool.memset(chunked(keep_on[F, :])[:, :, 0:1], 0.0).then_inc(reset_ready, 1)

        @block.scalar
        def _(act):
            act.preload_act_table_set("natural_log_exp_and_others")
            act.wait_ge(step["biased"], 1)
            act.activation(log_f[LOGS, :], pre[LOGS, :], ACT.Abs).then_inc(step["magnitude"], 1)
            act.wait_ge(step["magnitude"], 1)
            act.activation(log_f[LOGS, :], log_f[LOGS, :], ACT.Exp, scale=-1.0).then_inc(step["exp_neg"], 1)
            act.wait_ge(step["exp_neg"], 1)
            act.activation(log_f[LOGS, :], log_f[LOGS, :], ACT.Ln, bias=1.0).then_inc(step["log1p"], 1)
            act.wait_ge(step["differences"], 4)
            act.activation(weight_in[:, :], weight_in[:, :], ACT.Exp).then_inc(step["exponentials"], 1)
            act.activation(columns[COL_WS:COL_WS + M_HEADS, :], columns[COL_WS:COL_WS + M_HEADS, :],
                           ACT.Exp).then_inc(step["exponentials"], 1)
            act.activation(columns[COL_EM:COL_EM + M_HEADS, :], columns[COL_EM:COL_EM + M_HEADS, :],
                           ACT.Exp).then_inc(step["exponentials"], 1)
            act.activation(decay[:, :], decay[:, :], ACT.Exp).then_inc(step["exponentials"], 1)

        @block.vector
        def _(dve):
            def done(name, count=1):
                dve.wait_ge(step[name], count)

            dve.memset(bias[:, :], 0.0).then_inc(step["bias_zero"], 1)
            dve.wait_ge(landed, 64)
            dve.tensor_scalar(pre[:, :], pre[:, :], bias[:, 0:1], None, ALU.add).then_inc(step["biased"], 1)
            dve.wait_ge(step["log1p"], 1)
            dve.scalar_tensor_tensor(out=log_f[LOGS, :], in0=pre[LOGS, :], scalar=0.0, in1=log_f[LOGS, :],
                                     op0=ALU.min, op1=ALU.subtract).then_inc(step["log_ready"], 1)
            done("log_ready")
            dve.wait_ge(reset_ready, 1)
            dve.tensor_tensor_scan(out=neg_sum[FF, :], data0=keep_on[FF, :], data1=log_f[FF, :], initial=0.0,
                                   op0=ALU.mult, op1=ALU.subtract).then_inc(step["neg_sum_ready"], 1)
            dve.tensor_tensor_scan(out=chunk_sum[F, :], data0=keep_on[F, :], data1=log_f[F, :], initial=0.0,
                                   op0=ALU.mult, op1=ALU.add).then_inc(step["chunk_ready"], 1)
            done("chunk_ready")
            dve.tensor_copy(b_row[:, :], chunk_sum[F, :]).then_inc(step["b_ready"], 1)
            done("b_ready")
            g_row = columns[COL_G:COL_G + M_HEADS, :]
            dve.tensor_sub(g_row, pre[I, :], b_row[:, :]).then_inc(step["g_ready"], 1)
            dve.tensor_copy(chunked(carried[:, :])[:, 1:, 0], chunked(b_row[:, :])[:, :-1, CHUNK - 1]
                            ).then_inc(step["carried_ready"], 1)
            done("g_ready")
            done("carried_ready")
            dve.tensor_tensor_scan(out=g_max[:, :], data0=carried[:, :], data1=g_row, initial=0.0,
                                   op0=ALU.add, op1=ALU.max).then_inc(step["g_max_ready"], 1)
            dve.memset(m_prev[:, 0:1], 0.0)
            done("g_max_ready")
            last_G = chunked(g_max[:, :])[:, :, CHUNK - 1]
            dve.tensor_add(m_prev[:, 1:], chunked(carried[:, :])[:, 1:, 0], last_G[:, :-1]).then_inc(step["m_prev_ready"], 1)
            dve.tensor_sub(chunked(columns[COL_WS:COL_WS + M_HEADS, :]), chunked(g_row),
                           last_G.unsqueeze(2).broadcast_to([M_HEADS, CHUNKS, CHUNK])).then_inc(step["differences"], 1)
            em_row = columns[COL_EM:COL_EM + M_HEADS, :]
            dve.tensor_add(em_row, b_row[:, :], g_max[:, :]).then_inc(step["last_ready"], 1)
            done("last_ready")
            dve.tensor_scalar(em_row, em_row, -1.0, EXP_MAX, ALU.mult, ALU.min).then_inc(step["differences"], 1)
            done("m_prev_ready")
            dve.tensor_sub(chunked(weight_in[:, :]), m_prev[:, :].unsqueeze(2).broadcast_to([M_HEADS, CHUNKS, CHUNK]),
                           chunked(g_max[:, :])).then_inc(step["differences"], 1)
            dve.tensor_sub(decay[:, :], m_prev[:, :], last_G).then_inc(step["differences"], 1)
            dve.wait_ge(step["turned"], 1)
            dve.tensor_copy(keep["gate_cols"][:, :, :], ps[:, :, 0:GATE_COLS])

        @block.tensor
        def _(pe):
            pe.wait_ge(ident_ready, 1)
            pe.wait_ge(step["exponentials"], 4)
            for c in range(CHUNKS):
                ins = pe.transpose(ps[:, c, 0:GATE_COLS], columns[:, c * CHUNK:(c + 1) * CHUNK],
                                   ident[0:GATE_COLS, 0:GATE_COLS])
            ins.then_inc(step["turned"], 1)


def forgetting_heads(nc, a, scratch):
    with ExitStack() as ctx:
        def sb(name, shape, dt=F32):
            return ctx.enter_context(nc.sbuf_tensor("f_" + name, shape, dt))

        def psum(name, shape):
            return ctx.enter_context(nc.psum_tensor("f_" + name, shape, F32))

        def sem(name):
            return ctx.enter_context(nc.semaphore("f_" + name))

        QT = NB // P
        GROUPS = TT // QT
        HP = HEADS_IN_TILE
        PAIRS = F_HEADS // HP
        q_pack = sb("q_pack", [P, HP, SEQ], F32R)
        k_hi2 = sb("k_hi2", [P, HP, SEQ], F32R)
        k_lo2 = sb("k_lo2", [P, HP, SEQ], F32R)
        neg_f = sb("neg_f", [P, HP, SEQ])
        v_tok = sb("v_tok", [P, TT, HP, F_DH])
        gate_z = sb("gate_z", [P, SEQ])
        probs = sb("probs", [P, 2, QT, SEQ])
        probs_t = sb("probs_t", [P, 2, 2, NB])
        out_t = sb("out_t", [P, NB])
        out_tok = sb("out_tok", [P, TT, HP, F_DH])
        y_out = sb("y_out", [P, 2, NB])
        part_max = sb("part_max", [P, 2, QT, GROUPS])
        neg_max = sb("neg_max", [P, 2, QT])
        row_sum = sb("row_sum", [P, 4, QT])
        inv_sum = sb("inv_sum", [P, 4, QT])
        ident = sb("ident", [P, P])
        mask = sb("mask", [P, P])
        ident_r = sb("ident_r", [P, P], F32R)
        mask_r = sb("mask_r", [P, P], F32R)
        fold = sb("fold", [P, F_DH])
        ps_s = psum("ps_s", [P, 2, NB])
        ps_t = psum("ps_t", [P, 2, 2, NB])
        ps_o = psum("ps_o", [P, NB])
        ps_x = psum("ps_x", [P, NB])

        zeroed = sem("zeroed")
        const_ready = sem("const_ready")
        masks_ready = sem("masks_ready")
        head_landed = [sem(f"head_landed{h}") for h in range(HP)]
        v_landed = sem("v_landed")
        z_landed = sem("z_landed")
        s_psum = sem("s_psum")
        s_used = sem("s_used")
        logits_begun = sem("logits_begun")
        max_ready = sem("max_ready")
        exp_ready = sem("exp_ready")
        t_psum = sem("t_psum")
        even_ready = sem("even_ready")
        odd_ready = sem("odd_ready")
        pv_done = sem("pv_done")
        ot_ready = sem("ot_ready")
        fold_psum = sem("fold_psum")
        inv_ready = sem("inv_ready")
        x_used = sem("x_used")
        y_psum = sem("y_psum")
        y_stored = [sem(f"y_stored{i}") for i in range(2)]

        ORDER = [(h, J) for h in range(HP) for J in range(GROUPS)]

        def chunks(J):
            return [(r, c, NB if c < J else (r + 1) * P, c == J) for r in range(QT) for c in range(J + 1)]

        def pairs(J):
            return QT * (J + 1) // 2

        def chunks_before(g, m=0):
            return sum(len(chunks(J)) for _, J in ORDER[:g]) + m

        def pairs_before(g, p=0):
            return sum(pairs(J) for _, J in ORDER[:g]) + p

        ALL_CHUNKS, ALL_PAIRS, ALL_ROWS = chunks_before(len(ORDER)), pairs_before(len(ORDER)), QT * len(ORDER)

        def plan(g):
            n = pairs(ORDER[g][1])
            following = chunks(ORDER[g + 1][1]) if g + 1 < len(ORDER) else []
            slots = max(1, n - 2)
            per = -(-len(following) // slots)
            return [list(enumerate(following))[p * per:(p + 1) * per] for p in range(n)]

        def columns_of(J, kt):
            return max(0, kt - QT * J) * P

        block = ctx.enter_context(nc.Block())

        @block.sync
        def _(sp):
            def load_head(h, pair, row):
                for part in range(2):
                    rows = slice(part * F_DH, (part + 1) * F_DH)
                    sp.dma_start(q_pack[rows, h, :].bitcast(F32), scratch["qkT"][part, bass.ds(row, F_DH), :]
                                 ).then_inc(head_landed[h], 16)
                    sp.dma_start(k_hi2[rows, h, :].bitcast(F32), scratch["qkT"][0, bass.ds(row + F_W, F_DH), :]
                                 ).then_inc(head_landed[h], 16)
                    sp.dma_start(k_lo2[rows, h, :].bitcast(F32), scratch["qkT"][1, bass.ds(row + F_W, F_DH), :]
                                 ).then_inc(head_landed[h], 16)
                sp.dma_start(neg_f[:, h, :], scratch["f_negF"][bass.ds(pair * HP + h, 1), :].broadcast_to([P, SEQ])
                             ).then_inc(head_landed[h], 16)

            def load_v(pair):
                sp.dma_start(v_tok[:, :, :, :].rearrange("p t h d -> p (t h d)"),
                             scratch["arrays"][bass.ds(pair * P + A_FV * P, P), :]).then_inc(v_landed, 16)

            def load_z(pair):
                sp.dma_start(gate_z[:, :], scratch["arrays"][bass.ds(pair * P + A_FZ * P, P), :]).then_inc(z_landed, 16)

            for h in range(HP):
                load_head(h, 0, h * F_DH)
            load_v(0)
            load_z(0)

            def store_y(n, J):
                sp.wait_ge(x_used, n * X_READS + X_Y[J])
                sp.dma_start(scratch["yT"][bass.ds(n * P + M_W, P), J * NB:(J + 1) * NB],
                             y_out[:, J % 2, :]).then_inc(y_stored[J % 2], 16)

            with sp.Fori(0, PAIRS - 1) as n:
                sp.wait_ge(s_used, n * ALL_CHUNKS + 2 + chunks_before(GROUPS))
                load_head(0, n + 1, n * P + P)
                for J in range(GROUPS - 1):
                    store_y(n, J)
                sp.wait_ge(s_used, n * ALL_CHUNKS + 2 + chunks_before(HP * GROUPS))
                load_head(1, n + 1, n * P + P + F_DH)
                sp.wait_ge(pv_done, n * ALL_PAIRS + 2 + ALL_PAIRS)
                load_v(n + 1)
                store_y(n, GROUPS - 1)
                load_z(n + 1)
            for J in range(GROUPS):
                store_y(PAIRS - 1, J)
            for i in range(2):
                sp.wait_ge(y_stored[i], 16 + PAIRS * GROUPS // 2 * 16)

        @block.gpsimd
        def _(pool):
            pool.memset(ident[:, :], 0.0).then_inc(zeroed, 1)
            pool.memset(mask[:, :], 0.0).then_inc(zeroed, 1)
            pool.memset(fold[:, :], 0.0).then_inc(zeroed, 1)
            pool.wait_ge(zeroed, 3)
            pool.affine_select(out=ident[:, :], in_=ident[:, :], compare_op=ALU.not_equal, fill=1.0, base=0,
                               pattern=[[-1, P]], channel_multiplier=1).then_inc(const_ready, 1)
            pool.affine_select(out=mask[:, :], in_=mask[:, :], compare_op=ALU.is_ge, fill=MASKED, base=0,
                               pattern=[[-1, P]], channel_multiplier=1).then_inc(const_ready, 1)
            for h in range(2):
                pool.wait_ge(const_ready, 2 + h)
                pool.affine_select(out=fold[:, :], in_=fold[:, :], compare_op=ALU.not_equal, fill=1.0,
                                   base=-h * F_DH, pattern=[[-1, F_DH]], channel_multiplier=1).then_inc(const_ready, 1)

        @block.tensor
        def _(pe):
            pe.wait_ge(const_ready, 4)
            pe.wait_ge(masks_ready, 2)
            with pe.Fori(0, PAIRS) as n:
                def scores(g, m, r, c, width, last):
                    h, J = ORDER[g]
                    at = chunks_before(g, m)
                    if J == 0 and m == 0:
                        pe.wait_ge(head_landed[h], (n + 1) * 7 * 16)
                    pe.wait_ge(s_used, n * ALL_CHUNKS + at + 1)
                    q = q_pack[:, h, (J * QT + r) * P:(J * QT + r + 1) * P]
                    keys = slice(c * NB, c * NB + width)
                    bank = ps_s[:, at % 2, :]
                    pe.matmul(bank[:, 0:width], q, k_hi2[:, h, keys], start=True, stop=False)
                    ins = pe.matmul(bank[:, 0:width], q, k_lo2[:, h, keys], start=False, stop=not last)
                    if last:
                        ins = pe.matmul(bank[:, width - P:width], ident_r[:, :], mask_r[:, :], start=False, stop=True)
                    ins.then_inc(s_psum, 1)

                def turn(g, p):
                    h, J = ORDER[g]
                    at = pairs_before(g, p)
                    if p == 0:
                        pe.wait_ge(exp_ready, n * ALL_ROWS + (g + 1) * QT)
                    for e in range(2):
                        kt = 2 * p + e
                        for r in range(columns_of(J, kt) // P, QT):
                            ins = pe.transpose(ps_t[:, at % 2, e, r * P:(r + 1) * P],
                                               probs[:, g % 2, r, kt * P:(kt + 1) * P], ident[:, :])
                    ins.then_inc(t_psum, 1)

                def product(g, p):
                    h, J = ORDER[g]
                    at = pairs_before(g, p)
                    pe.wait_ge(even_ready, n * ALL_PAIRS + at + 1)
                    pe.wait_ge(odd_ready, n * ALL_PAIRS + at + 1)
                    if p == 0 and g == 0:
                        pe.wait_ge(v_landed, (n + 1) * 16)
                    if p == 0:
                        pe.wait_ge(ot_ready, n * len(ORDER) + g + 1)
                    for e in range(2):
                        kt = 2 * p + e
                        first = columns_of(J, kt)
                        ins = pe.matmul(ps_o[e * F_DH:(e + 1) * F_DH, first:], v_tok[:, kt, h, :],
                                        probs_t[:, at % 2, e, first:], start=(p == 0), stop=(p == pairs(J) - 1))
                    ins.then_inc(pv_done, 1)

                def finish(g):
                    h, J = ORDER[g]
                    pe.wait_ge(ot_ready, n * len(ORDER) + g + 2)
                    pe.wait_ge(x_used, n * X_READS + X_FOLD[g])
                    for r in range(QT):
                        rows = slice(0, F_DH if J == 0 and r == 0 else P)
                        ins = pe.matmul(ps_x[:, r * F_DH:(r + 1) * F_DH], out_t[rows, r * P:(r + 1) * P],
                                        fold[rows, :], start=True, stop=True)
                    ins.then_inc(fold_psum, 1)
                    if h == HP - 1:
                        pe.wait_ge(x_used, n * X_READS + X_FOLD[g] + 1)
                        for r in range(QT):
                            ins = pe.transpose(ps_x[:, r * P:(r + 1) * P],
                                               out_tok[:, J * QT + r, :, :].rearrange("p h d -> p (h d)"), ident[:, :])
                        ins.then_inc(y_psum, 1)

                for m, chunk in enumerate(chunks(ORDER[0][1])):
                    scores(0, m, *chunk)
                for g, (h, J) in enumerate(ORDER):
                    for p, share in enumerate(plan(g)):
                        turn(g, p)
                        for m, chunk in share:
                            scores(g + 1, m, *chunk)
                        if p:
                            product(g, p - 1)
                        if p == 0 and g:
                            finish(g - 1)
                    product(g, pairs(J) - 1)
                finish(len(ORDER) - 1)

        @block.vector
        def _(dve):
            dve.wait_ge(const_ready, 4)
            dve.tensor_copy(ident_r[:, :], ident[:, :]).then_inc(masks_ready, 1)
            dve.tensor_copy(mask_r[:, :], mask[:, :]).then_inc(masks_ready, 1)
            dve.sem_inc(s_used, 2)
            with dve.Fori(0, PAIRS) as n:
                def logits(g, m, r, c, width, last):
                    h, J = ORDER[g]
                    at = chunks_before(g, m)
                    dve.wait_ge(s_psum, n * ALL_CHUNKS + at + 1)
                    if J == 0 and m == 0:
                        dve.wait_ge(head_landed[h], (n + 1) * 7 * 16)
                    keys = slice(c * NB, c * NB + width)
                    dve.sem_inc(logits_begun, 1)
                    dve.tensor_tensor_reduce(out=probs[:, g % 2, r, keys], in0=ps_s[:, at % 2, 0:width],
                                             in1=neg_f[:, h, keys], scale=1.0, scalar=MASKED, op0=ALU.add,
                                             op1=ALU.max, accum_out=part_max[:, g % 2, r, c:c + 1]
                                             ).then_inc(s_used, 1)
                    if last:
                        dve.wait_ge(s_used, n * ALL_CHUNKS + at + 3)
                        dve.tensor_reduce(neg_max[:, g % 2, r:r + 1], part_max[:, g % 2, r, 0:c + 1], axis=AX_X,
                                          op=ALU.max, negate=True).then_inc(max_ready, 1)

                def odd(g, p):
                    h, J = ORDER[g]
                    at = pairs_before(g, p)
                    first = columns_of(J, 2 * p + 1)
                    dve.wait_ge(t_psum, n * ALL_PAIRS + at + 1)
                    dve.wait_ge(pv_done, n * ALL_PAIRS + at + 1)
                    dve.tensor_copy(probs_t[:, at % 2, 1, first:], ps_t[:, at % 2, 1, first:]).then_inc(odd_ready, 1)

                def finish(g):
                    h, J = ORDER[g]
                    dve.wait_ge(exp_ready, n * ALL_ROWS + (g + 1) * QT)
                    dve.reciprocal(inv_sum[:, g % 4, :], row_sum[:, g % 4, :]).then_inc(inv_ready, 1)
                    dve.wait_ge(inv_ready, n * len(ORDER) + g + 1)
                    dve.wait_ge(fold_psum, n * len(ORDER) + g + 1)
                    dve.tensor_mul(out_tok[:, J * QT:(J + 1) * QT, h, :],
                                   ps_x[:, 0:QT * F_DH].rearrange("p (r d) -> p r d", d=F_DH),
                                   inv_sum[:, g % 4, :].unsqueeze(2).broadcast_to([P, QT, F_DH])).then_inc(x_used, 1)
                    if h == HP - 1:
                        dve.wait_ge(y_psum, n * GROUPS + J + 1)
                        dve.wait_ge(z_landed, (n + 1) * 16)
                        dve.wait_ge(y_stored[J % 2], (n * GROUPS // 2 + J // 2 + 1) * 16)
                        dve.tensor_mul(y_out[:, J % 2, :], ps_x[:, :], gate_z[:, J * NB:(J + 1) * NB]).then_inc(x_used, 1)

                for m, chunk in enumerate(chunks(ORDER[0][1])):
                    logits(0, m, *chunk)
                for g, (h, J) in enumerate(ORDER):
                    for p, share in enumerate(plan(g)):
                        odd(g, p)
                        for m, chunk in share:
                            logits(g + 1, m, *chunk)
                        if p == 0 and g:
                            finish(g - 1)
                finish(len(ORDER) - 1)

        @block.scalar
        def _(act):
            act.preload_act_table(ACT.Exp)
            act.sem_inc(ot_ready, 1)
            act.sem_inc(pv_done, 2)
            act.sem_inc(y_stored[0], 16)
            act.sem_inc(y_stored[1], 16)
            with act.Fori(0, PAIRS) as n:
                def exponential(g, m, r, c, width, last):
                    if not last:
                        return
                    act.wait_ge(max_ready, n * ALL_ROWS + g * QT + r + 1)
                    row = probs[:, g % 2, r, 0:c * NB + width]
                    act.activation(row, row, ACT.Exp, bias=neg_max[:, g % 2, r:r + 1],
                                   accum_out=row_sum[:, g % 4, r:r + 1]).then_inc(exp_ready, 1)

                def even(g, p):
                    h, J = ORDER[g]
                    at = pairs_before(g, p)
                    first = columns_of(J, 2 * p)
                    act.wait_ge(t_psum, n * ALL_PAIRS + at + 1)
                    act.wait_ge(pv_done, n * ALL_PAIRS + at + 1)
                    act.activation(probs_t[:, at % 2, 0, first:], ps_t[:, at % 2, 0, first:], ACT.Copy
                                   ).then_inc(even_ready, 1)

                for m, chunk in enumerate(chunks(ORDER[0][1])):
                    exponential(0, m, *chunk)
                for g, (h, J) in enumerate(ORDER):
                    for p, share in enumerate(plan(g)):
                        even(g, p)
                        for m, chunk in share:
                            exponential(g + 1, m, *chunk)
                    act.wait_ge(pv_done, n * ALL_PAIRS + 2 + pairs_before(g + 1))
                    act.wait_ge(fold_psum, n * len(ORDER) + g)
                    if J == 0:
                        act.activation(out_t[0:F_DH, 0:P], ps_o[0:F_DH, 0:P], ACT.Copy)
                        act.activation(out_t[:, P:], ps_o[:, P:], ACT.Copy).then_inc(ot_ready, 1)
                    else:
                        act.activation(out_t[:, :], ps_o[:, :], ACT.Copy).then_inc(ot_ready, 1)



def memory_heads(nc, a, scratch, keep):
    with ExitStack() as ctx:
        def sb(name, shape, dt=F32):
            return ctx.enter_context(nc.sbuf_tensor("m_" + name, shape, dt))

        def psum(name, shape):
            return ctx.enter_context(nc.psum_tensor("m_" + name, shape, F32))

        def sem(name):
            return ctx.enter_context(nc.semaphore("m_" + name))

        H, W = M_HEADS, M_DH + 1
        HB = H // 2
        q_in = sb("q_in", [P, 2, H, CHUNK])
        k_in = sb("k_in", [P, 2, H, CHUNK])
        v_in = sb("v_in", [P, 2, H, W])
        o_in = sb("o_in", [P, 2, H, M_DH])
        z_in = sb("z_in", [P, 2, H, CHUNK])
        g_max = sb("g_max", [P, 2, H, CHUNK])
        w_in = sb("w_in", [P, 2, H, CHUNK])
        decay = sb("decay", [P, H, CHUNKS])
        diff = sb("diff", [P, 2, H, CHUNK])
        q_w = sb("q_w", [P, 2, H, CHUNK])
        scores = sb("scores", [P, H, CHUNK])
        k_w = sb("k_w", [P, H, M_DH])
        state = sb("state", [P, 2, H, W])
        den = sb("den", [P, 2, H])
        gated = sb("gated", [P, H, M_DH])
        stats = sb("stats", [P, H, nc.vector.BN_STATS_DIM])
        moments = sb("moments", [P, H, 2])
        rstd = sb("rstd", [P, H])
        normed = sb("normed", [P, H, M_DH])
        y_out = sb("y_out", [P, 2, H, CHUNK])
        ident = sb("ident", [P, P])
        future = sb("future", [P, CHUNK])
        ps_s = psum("ps_s", [P, H, CHUNK])
        ps_k = psum("ps_k", [P, H, CHUNK])
        ps_n = psum("ps_n", [P, 2, NB])
        ps_c = psum("ps_c", [P, 2, NB])
        ps_y = psum("ps_y", [P, H, CHUNK])

        def by_head(ps):
            return ps[:, :, 0:HB * W].rearrange("p b (h w) -> p b h w", w=W)

        zeroed = sem("zeroed")
        const_ready = sem("const_ready")
        state_zero = sem("state_zero")
        decay_landed = sem("decay_landed")
        landed = [sem(f"landed{i}") for i in range(2)]
        diff_ready = sem("diff_ready")
        masked = sem("masked")
        weights_ready = sem("weights_ready")
        qw_ready = sem("qw_ready")
        s_psum = sem("s_psum")
        k_psum = sem("k_psum")
        scores_ready = sem("scores_ready")
        kw_ready = sem("kw_ready")
        n_psum = sem("n_psum")
        c_psum = sem("c_psum")
        negative_ready = sem("negative_ready")
        den_ready = sem("den_ready")
        inv_ready = sem("inv_ready")
        hidden_ready = sem("hidden_ready")
        state_ready = sem("state_ready")
        stats_ready = sem("stats_ready")
        stats_seen = sem("stats_seen")
        moments_ready = sem("moments_ready")
        log_ready = sem("log_ready")
        rstd_ready = sem("rstd_ready")
        normed_ready = sem("normed_ready")
        y_psum = sem("y_psum")
        chunk_done = sem("chunk_done")
        stored = [sem(f"stored{i}") for i in range(2)]
        LOADS = 7

        block = ctx.enter_context(nc.Block())

        @block.sync
        def _(sp):
            def tile_rows(first, c):
                return scratch["arrays"][first * P:(first + H) * P, bass.ds(c * CHUNK, CHUNK)].rearrange(
                    "(h p) t -> p h t", p=P)

            def load(par, c):
                for buf, src in ((k_in[:, par], tile_rows(A_MK, c)), (q_in[:, par], tile_rows(A_MQ, c)),
                                 (v_in[:, par, :, 0:M_DH], tile_rows(A_MV, c)), (o_in[:, par], tile_rows(A_MO, c)),
                                 (z_in[:, par], tile_rows(A_MZ, c))):
                    sp.dma_start(buf, src).then_inc(landed[par], 16)
                for buf, rows in ((g_max, "m_G"), (w_in, "m_in")):
                    sp.dma_start(buf[:, par], scratch[rows][:, bass.ds(c * CHUNK, CHUNK)].unsqueeze(0).broadcast_to(
                        [P, H, CHUNK])).then_inc(landed[par], 16)

            def store(par, c):
                sp.wait_ge(chunk_done, c + 1)
                sp.dma_start(scratch["yT"][0:M_W, bass.ds(c * CHUNK, CHUNK)].rearrange("(h p) t -> p h t", p=P),
                             y_out[:, par]).then_inc(stored[par], 16)

            sp.dma_start(decay[:, :, :], scratch["m_decay"].unsqueeze(0).broadcast_to([P, H, CHUNKS])
                         ).then_inc(decay_landed, 16)
            for par in range(2):
                load(par, par)
            with sp.Fori(0, CHUNKS // 2 - 1) as n:
                for par in range(2):
                    store(par, n * 2 + par)
                    load(par, n * 2 + par + 2)
            for par in range(2):
                store(par, CHUNKS - 2 + par)
            for par in range(2):
                sp.wait_ge(stored[par], CHUNKS // 2 * 16)

        @block.gpsimd
        def _(pool):
            pool.memset(ident[:, :], 0.0).then_inc(zeroed, 1)
            pool.memset(future[:, :], 0.0).then_inc(zeroed, 1)
            pool.memset(v_in[:, :, :, M_DH:W], 1.0).then_inc(const_ready, 1)
            pool.wait_ge(zeroed, 2)
            pool.affine_select(out=ident[:, :], in_=ident[:, :], compare_op=ALU.not_equal, fill=1.0, base=0,
                               pattern=[[-1, P]], channel_multiplier=1).then_inc(const_ready, 1)
            pool.affine_select(out=future[:, :], in_=future[:, :], compare_op=ALU.is_ge, fill=MASKED, base=0,
                               pattern=[[1, CHUNK]], channel_multiplier=-1).then_inc(const_ready, 1)
            with pool.Fori(0, CHUNKS // 2) as n:
                for par in range(2):
                    pool.wait_ge(landed[par], (n + 1) * LOADS * 16)
                    pool.tensor_tensor(out=q_w[:, par], in0=q_in[:, par], in1=w_in[:, par], op=ALU.mult
                                       ).then_inc(qw_ready, 1)

        @block.tensor
        def _(pe):
            pe.wait_ge(const_ready, 3)
            pe.wait_ge(state_zero, 2)

            def score(par, n):
                pe.wait_ge(landed[par], (n + 1) * LOADS * 16)
                for h in range(H):
                    ins = pe.matmul(ps_s[:, h, :], k_in[:, par, h, :], q_in[:, par, h, :], start=True, stop=True)
                ins.then_inc(s_psum, 1)
                for h in range(H):
                    ins = pe.transpose(ps_k[:, h, :], k_in[:, par, h, :], ident[:, :])
                ins.then_inc(k_psum, 1)

            def products(par, c):
                num, new = by_head(ps_n), by_head(ps_c)
                pe.wait_ge(scores_ready, c + 1)
                pe.wait_ge(qw_ready, c + 1)
                pe.wait_ge(hidden_ready, c + 1)
                pe.wait_ge(state_ready, c + 1)
                for h in range(H):
                    pe.matmul(num[:, h // HB, h % HB, :], scores[:, h, :], v_in[:, par, h, :], start=True, stop=False)
                    ins = pe.matmul(num[:, h // HB, h % HB, :], q_w[:, par, h, :], state[:, par, h, :],
                                    start=False, stop=True)
                ins.then_inc(n_psum, 1)
                pe.wait_ge(kw_ready, c + 1)
                for h in range(H):
                    ins = pe.matmul(new[:, h // HB, h % HB, :], k_w[:, h, :], v_in[:, par, h, :], start=True, stop=True)
                ins.then_inc(c_psum, 1)

            def turn(c):
                pe.wait_ge(normed_ready, c + 1)
                for h in range(H):
                    ins = pe.transpose(ps_y[:, h, :], normed[:, h, :], ident[:, :])
                ins.then_inc(y_psum, 1)

            score(0, 0)
            with pe.Fori(0, CHUNKS // 2 - 1) as n:
                for par in range(2):
                    products(par, n * 2 + par)
                    score(1 - par, n + par)
                    turn(n * 2 + par)
            products(0, CHUNKS - 2)
            score(1, CHUNKS // 2 - 1)
            turn(CHUNKS - 2)
            products(1, CHUNKS - 1)
            turn(CHUNKS - 1)

        @block.vector
        def _(dve):
            dve.memset(state[:, 0], 0.0).then_inc(state_zero, 1)
            dve.memset(keep["eps"][:, :], EPS).then_inc(state_zero, 1)
            dve.sem_inc(hidden_ready, 1)
            dve.sem_inc(state_ready, 1)
            dve.wait_ge(const_ready, 3)
            dve.wait_ge(decay_landed, 16)

            def prepare(par, n, c):
                dve.wait_ge(landed[par], (n + 1) * LOADS * 16)
                cols = keep["gate_cols"][:, bass.ds(c, 1), :]
                g_col = cols[:, 0, COL_G:COL_G + H].unsqueeze(2).broadcast_to([P, H, CHUNK])
                dve.tensor_sub(diff[:, par], g_col, g_max[:, par]).then_inc(diff_ready, 1)
                dve.wait_ge(diff_ready, c + 1)
                dve.scalar_tensor_tensor(out=diff[:, par], in0=diff[:, par], scalar=0.0,
                                         in1=future[:, :].unsqueeze(1).broadcast_to([P, H, CHUNK]),
                                         op0=ALU.min, op1=ALU.add).then_inc(masked, 1)
                dve.wait_ge(k_psum, c + 1)
                ws_col = cols[:, 0, COL_WS:COL_WS + H].unsqueeze(2).broadcast_to([P, H, CHUNK])
                dve.tensor_mul(k_w[:, :, :], ps_k[:, :, :], ws_col).then_inc(kw_ready, 1)
                dve.wait_ge(weights_ready, c + 1)
                dve.wait_ge(s_psum, c + 1)
                dve.tensor_mul(scores[:, :, :], ps_s[:, :, :], diff[:, par]).then_inc(scores_ready, 1)

            def divide(par, c):
                num = by_head(ps_n)
                em = keep["gate_cols"][:, bass.ds(c, 1), :][:, 0, COL_EM:COL_EM + H].rearrange("p (b h) -> p b h", b=2)
                dve.wait_ge(n_psum, c + 1)
                bound = den[:, 0, :].rearrange("p (b h) -> p b h", b=2)
                dve.scalar_tensor_tensor(out=bound, in0=num[:, :, :, M_DH], scalar=-1.0, in1=em,
                                         op0=ALU.mult, op1=ALU.max).then_inc(negative_ready, 1)
                dve.wait_ge(negative_ready, c + 1)
                dve.tensor_max(bound, num[:, :, :, M_DH], bound).then_inc(den_ready, 1)
                dve.wait_ge(den_ready, c + 1)
                dve.reciprocal(den[:, 1, :], den[:, 0, :]).then_inc(inv_ready, 1)
                dve.wait_ge(inv_ready, c + 1)
                for h in range(H):
                    ins = dve.scalar_tensor_tensor(out=gated[:, h, :], in0=num[:, h // HB, h % HB, 0:M_DH],
                                                   scalar=den[:, 1, h:h + 1], in1=o_in[:, par, h, :],
                                                   op0=ALU.mult, op1=ALU.mult)
                ins.then_inc(hidden_ready, 1)

            def carry(par, c):
                new = by_head(ps_c)
                dve.wait_ge(c_psum, c + 1)
                for h in range(H):
                    ins = dve.scalar_tensor_tensor(out=state[:, 1 - par, h, :], in0=state[:, par, h, :],
                                                   scalar=decay[:, h, bass.ds(c, 1)],
                                                   in1=new[:, h // HB, h % HB, :], op0=ALU.mult, op1=ALU.add)
                ins.then_inc(state_ready, 1)

            def moments_of(c):
                dve.wait_ge(hidden_ready, c + 2)
                for h in range(H):
                    ins = dve.bn_stats(stats[:, h, :], gated[:, h, :])
                ins.then_inc(stats_ready, 1)
                dve.wait_ge(stats_ready, c + 1)
                dve.sem_inc(stats_seen, 1)
                for h in range(H):
                    ins = dve.bn_aggr(moments[:, h, :], stats[:, h, :])
                ins.then_inc(moments_ready, 1)

            def output(par, n, c):
                dve.wait_ge(rstd_ready, c + 1)
                for h in range(H):
                    ins = dve.tensor_scalar(normed[:, h, :], gated[:, h, :], moments[:, h, 0:1], rstd[:, h:h + 1],
                                            ALU.subtract, ALU.mult)
                ins.then_inc(normed_ready, 1)

            def leave(par, n, c):
                dve.wait_ge(y_psum, c + 1)
                dve.wait_ge(stored[par], n * 16)
                for h in range(H):
                    ins = dve.scalar_tensor_tensor(out=y_out[:, par, h, :], in0=ps_y[:, h, :],
                                                   scalar=keep["params"][:, NORM_GAIN + h:NORM_GAIN + h + 1],
                                                   in1=z_in[:, par, h, :], op0=ALU.mult, op1=ALU.mult)
                ins.then_inc(chunk_done, 1)

            prepare(0, 0, 0)
            with dve.Fori(0, CHUNKS // 2 - 1) as n:
                for par in range(2):
                    c = n * 2 + par
                    divide(par, c)
                    carry(par, c)
                    moments_of(c)
                    prepare(1 - par, n + par, c + 1)
                    output(par, n, c)
                    leave(par, n, c)
            for par in range(2):
                n, c = CHUNKS // 2 - 1, CHUNKS - 2 + par
                divide(par, c)
                carry(par, c)
                moments_of(c)
                if par == 0:
                    prepare(1, n, c + 1)
                output(par, n, c)
                leave(par, n, c)

        @block.scalar
        def _(act):
            act.preload_act_table_set("natural_log_exp_and_others")

            def weights(par, c):
                act.wait_ge(masked, c + 1)
                act.activation(diff[:, par], diff[:, par], ACT.Exp).then_inc(weights_ready, 1)

            act.wait_ge(state_zero, 2)

            def root(c):
                act.wait_ge(moments_ready, c + 1)
                act.activation(rstd[:, :], moments[:, :, 1], ACT.Ln, bias=keep["eps"][:, 0:1]).then_inc(log_ready, 1)
                act.wait_ge(log_ready, c + 1)
                act.activation(rstd[:, :], rstd[:, :], ACT.Exp, scale=-0.5).then_inc(rstd_ready, 1)

            weights(0, 0)
            with act.Fori(0, CHUNKS // 2 - 1) as n:
                for par in range(2):
                    root(n * 2 + par)
                    weights(1 - par, n * 2 + par + 1)
            root(CHUNKS - 2)
            weights(1, CHUNKS - 1)
            root(CHUNKS - 1)


def project_out(nc, a, scratch, out):
    with ExitStack() as ctx:
        def sb(name, shape, dt=F32):
            return ctx.enter_context(nc.sbuf_tensor("o_" + name, shape, dt))

        def sem(name):
            return ctx.enter_context(nc.semaphore("o_" + name))

        ON = D_MODEL // NB
        w_land = sb("w_land", [P, KT, D_MODEL])
        w_hi = sb("w_hi", [P, KT, D_MODEL], F32R)
        w_lo = sb("w_lo", [P, KT, D_MODEL], F32R)
        gate = sb("gate", [P, D_MODEL])
        y_land = sb("y_land", [P, 2, KT, P])
        y_hi = sb("y_hi", [P, 2, KT, P], F32R)
        y_lo = sb("y_lo", [P, 2, KT, P], F32R)
        x_land = sb("x_land", [P, 2, D_MODEL])
        update = sb("update", [P, 2, D_MODEL])
        result = sb("result", [P, 2, D_MODEL])
        ps = ctx.enter_context(nc.psum_tensor("o_ps", [P, 2, ON, NB], F32))

        w_landed = [sem(f"w_landed{k}") for k in range(KT)]
        gate_landed = sem("gate_landed")
        y_landed = [sem(f"y_landed{i}") for i in range(2)]
        x_landed = [sem(f"x_landed{i}") for i in range(2)]
        w_hi_ready = sem("w_hi_ready")
        w_ready = sem("w_ready")
        y_hi_ready = sem("y_hi_ready")
        y_ready = sem("y_ready")
        projected = sem("projected")
        gated = sem("gated")
        added = sem("added")
        stored = [sem(f"stored{i}") for i in range(2)]

        block = ctx.enter_context(nc.Block())

        @block.sync
        def _(sp):
            def load_y(par, t):
                sp.dma_start(y_land[:, par], scratch["yT"][:, bass.ds(t * P, P)].rearrange("(k p) t -> p k t", p=P)
                             ).then_inc(y_landed[par], 16)

            load_y(0, 0)
            for k in range(KT):
                sp.dma_start(w_land[:, k, :], a["w_out"][0, k * P:(k + 1) * P, :]).then_inc(w_landed[k], 16)
            load_y(1, 1)
            with sp.Fori(0, TT // 2 - 1) as n:
                for par in range(2):
                    sp.wait_ge(y_ready, n * 2 + par + 1)
                    load_y(par, n * 2 + par + 2)

        @block.gpsimd
        def _(pool):
            def load_x(par, t):
                pool.dma_start(x_land[:, par, :], a["x"][0, bass.ds(t * P, P), :]).then_inc(x_landed[par], 16)

            def store(par, t):
                pool.wait_ge(added, t + 1)
                pool.dma_start(out[0, bass.ds(t * P, P), :], result[:, par, :]).then_inc(stored[par], 16)

            pool.dma_start(gate[:, :], scratch["gate"]).then_inc(gate_landed, 16)
            for par in range(2):
                load_x(par, par)
            with pool.Fori(0, TT // 2 - 1) as n:
                for par in range(2):
                    store(par, n * 2 + par)
                    load_x(par, n * 2 + par + 2)
            for par in range(2):
                store(par, TT - 2 + par)
            for par in range(2):
                pool.wait_ge(stored[par], TT // 2 * 16)

        @block.scalar
        def _(act):
            for k in range(KT):
                act.wait_ge(w_landed[k], 16)
                act.activation(w_hi[:, k, :], w_land[:, k, :], ACT.Copy).then_inc(w_hi_ready, 1)

        @block.vector
        def _(dve):
            def split(par, n, t):
                dve.wait_ge(y_landed[par], (n + 1) * 16)
                dve.wait_ge(projected, t + 1)
                dve.tensor_copy(y_hi[:, par], y_land[:, par]).then_inc(y_hi_ready, 1)
                dve.wait_ge(y_hi_ready, t + 1)
                dve.tensor_sub(y_lo[:, par], y_land[:, par], y_hi[:, par].bitcast(F32)).then_inc(y_ready, 1)

            def residual(par, n, t):
                dve.wait_ge(projected, t + 3)
                dve.tensor_mul(update[:, par, :], ps[:, par].rearrange("p b n -> p (b n)"), gate[:, :]).then_inc(gated, 1)
                dve.wait_ge(gated, t + 1)
                dve.wait_ge(x_landed[par], (n + 1) * 16)
                dve.wait_ge(stored[par], n * 16)
                dve.tensor_add(result[:, par, :], update[:, par, :], x_land[:, par, :]).then_inc(added, 1)

            split(0, 0, 0)
            for k in range(KT):
                dve.wait_ge(w_hi_ready, k + 1)
                dve.tensor_sub(w_lo[:, k, :], w_land[:, k, :], w_hi[:, k, :].bitcast(F32)).then_inc(w_ready, 1)
            dve.wait_ge(gate_landed, 16)
            with dve.Fori(0, TT // 2 - 1) as n:
                for par in range(2):
                    split(1 - par, n + par, n * 2 + par + 1)
                    residual(par, n, n * 2 + par)
            split(1, TT // 2 - 1, TT - 1)
            residual(0, TT // 2 - 1, TT - 2)
            residual(1, TT // 2 - 1, TT - 1)

        @block.tensor
        def _(pe):
            pe.sem_inc(projected, 2)

            def project(par, t, first):
                pe.wait_ge(y_ready, t + 1)
                if not first:
                    pe.wait_ge(gated, t - 1)
                for k in range(KT):
                    pe.wait_ge(w_ready, k + 1)
                    for y, w in ((y_hi, w_hi), (y_hi, w_lo), (y_lo, w_hi)):
                        for b in range(ON):
                            ins = pe.matmul(ps[:, par, b, :], y[:, par, k, :], w[:, k, b * NB:(b + 1) * NB],
                                            start=(k == 0 and y is y_hi and w is w_hi),
                                            stop=(k == KT - 1 and y is y_lo))
                ins.then_inc(projected, 1)

            project(0, 0, True)
            project(1, 1, True)
            with pe.Fori(1, TT // 2) as n:
                for par in range(2):
                    project(par, n * 2 + par, False)


_INS = ["x", "c", "norm_g", "w_ada", "b_ada", "w_in", "conv_w", "conv_b", "b_igate", "b_fgate_m",
        "mlstm_norm_g", "b_fgate_f", "fox_qnorm_g", "fox_knorm_g", "w_out"]


def layer(nc, a, out):
    def dram(name, shape):
        return nc.dram_tensor("scratch_" + name, shape, F32).ap()

    scratch = {
        "gate": dram("gate", (P, D_MODEL)),
        "gate_rows": dram("gate_rows", (ROW_FF + F_HEADS, SEQ)),
        "qkT": dram("qkT", (2, 2 * F_W, SEQ)),
        "arrays": dram("arrays", (7 * M_W, SEQ)),
        "f_negF": dram("f_negF", (F_HEADS, SEQ)),
        "m_G": dram("m_G", (M_HEADS, SEQ)),
        "m_in": dram("m_in", (M_HEADS, SEQ)),
        "m_decay": dram("m_decay", (M_HEADS, CHUNKS)),
        "yT": dram("yT", (M_W + F_W, SEQ)),
    }
    with ExitStack() as ctx:
        keep = {
            "params": ctx.enter_context(nc.sbuf_tensor("params", [P, PARAM_ROWS], F32)),
            "gate_cols": ctx.enter_context(nc.sbuf_tensor("gate_cols", [P, CHUNKS, GATE_COLS], F32)),
            "eps": ctx.enter_context(nc.sbuf_tensor("eps", [P, 1], F32)),
            "qk_gain": ctx.enter_context(nc.sbuf_tensor("qk_gain", [P, 2 * M_HEADS], F32)),
        }
        modulate_and_project(nc, a, scratch, keep)
        gate_rows(nc, a, scratch, keep)
        forgetting_heads(nc, a, scratch)
        memory_heads(nc, a, scratch, keep)
        project_out(nc, a, scratch, out)


def kernel(**inputs):
    import numpy as _np
    import concourse.bacc as _bacc
    from concourse import mybir as _mybir
    from concourse.bass_utils import run_bass_kernel_spmd as _run

    nc = _bacc.Bacc("TRN2", target_bir_lowering=False, num_devices=1)
    arrays, aps = {}, {}
    for name in _INS:
        arr = _np.ascontiguousarray(inputs[name])
        arrays["in_" + name] = arr
        aps[name] = nc.dram_tensor("in_" + name, arr.shape, _mybir.dt.from_np(arr.dtype), kind="ExternalInput").ap()
    out = nc.dram_tensor("out_0", (1, SEQ, D_MODEL), F32, kind="ExternalOutput").ap()
    layer(nc, aps, out)
    r = _run(nc, [arrays], core_ids=[0])
    return r.results[0]["out_0"]
```

```python
import math
from contextlib import ExitStack

import concourse.bass as bass
from concourse import mybir

F32 = mybir.dt.float32
F32R = mybir.dt.float32r
ALU = mybir.AluOpType
ACT = mybir.ActivationFunctionType
AX_X = mybir.AxisListType.X

P = 128
D_MODEL = 1024
SEQ = 2048
EPS = 1e-6
KT = D_MODEL // P
TT = SEQ // P
NB = 512
TB = SEQ // NB

M_HEADS, M_DH = 4, 128
F_HEADS, F_DH = 8, 64
M_W, F_W = M_HEADS * M_DH, F_HEADS * F_DH
CONV_K = 4

M_GATES = 5 * M_W
F_Q = M_GATES + 2 * M_HEADS
F_GATES = F_Q + 4 * F_W
D_IN = F_GATES + F_HEADS
M_TILES = 5 * M_W // P
F_TILES = 4 * F_W // P
U_TILES = M_TILES + F_TILES
HEADS_IN_TILE = P // F_DH
PARAM_ROWS = (CONV_K + 1) * 2 * M_HEADS + 2 + M_HEADS
CHUNK = 128
CHUNKS = SEQ // CHUNK
A_FV, A_MV, A_MO, A_MQ, A_MK, A_MZ, A_FZ = (i * M_HEADS for i in range(7))
COL_G, COL_WS, COL_EM, GATE_COLS = 0, 32, 64, 64 + M_HEADS
NORM_GAIN = (CONV_K + 1) * 2 * M_HEADS + 2
EXP_MAX = 88.0
MASKED = -1e30
ROW_I, ROW_F, ROW_FF = 0, 32, 64


def modulate_and_project(nc, a, scratch, keep):
    with ExitStack() as ctx:
        def sb(name, shape, dt=F32):
            return ctx.enter_context(nc.sbuf_tensor("a_" + name, shape, dt))

        def sem(name):
            return ctx.enter_context(nc.semaphore("a_" + name))

        UN = 4
        WP = 256
        AR = 4
        PIECES = 3 * D_MODEL // WP
        COL_PIECES = 2 * D_MODEL // WP
        assert PIECES % AR == 0 and COL_PIECES % AR == 0

        H_SLOTS = 2
        params, qk_gain = keep["params"], keep["qk_gain"]
        h_hi = sb("h_hi", [P, KT, SEQ], F32R)
        h_lo = sb("h_lo", [P, KT, SEQ], F32R)

        with ExitStack() as early:
            def esb(name, shape, dt=F32):
                return early.enter_context(nc.sbuf_tensor("a0_" + name, shape, dt))

            x_ring = esb("x_ring", [P, UN, D_MODEL])
            w_ring = esb("w_ring", [P, AR, KT, WP])
            h_part = esb("h_part", [P, 2, KT, P])
            vec_rows = esb("vec_rows", [4 * KT, P])
            vec_cols = esb("vec_cols", [P, 4 * KT])
            c_wide = esb("c_wide", [P, KT, P])
            ident = esb("ident", [P, P])
            mod_a = esb("mod_a", [P, KT])
            mod_b = esb("mod_b", [P, KT])
            scale1 = esb("scale1", [P, KT])
            b_gate = esb("b_gate", [P, D_MODEL])
            sumsq = esb("sumsq", [P, TT])
            meansq = esb("meansq", [P, TT])
            inv_ms = esb("inv_ms", [P, TT])
            rstd = esb("rstd", [P, TT])
            junk = esb("junk", [P, D_MODEL])
            ps_t = early.enter_context(nc.psum_tensor("a0_ps_t", [P, 2, KT, P], F32))
            ps_v = early.enter_context(nc.psum_tensor("a0_ps_v", [P, NB], F32))
            ps_m = early.enter_context(nc.psum_tensor("a0_ps_m", [P, NB], F32))
            ps_g = early.enter_context(nc.psum_tensor("a0_ps_g", [P, NB], F32))

            vec_landed = sem("vec_landed")
            bgate_landed = sem("bgate_landed")
            x_landed = [sem(f"x_landed{u}") for u in range(UN)]
            w_landed = [sem(f"w_landed{u}") for u in range(AR)]
            w_used = sem("w_used")
            zeroed = sem("zeroed")
            ident_ready = sem("ident_ready")
            vec_transposed = sem("vec_transposed")
            vec_ready = sem("vec_ready")
            cwide_ready = sem("cwide_ready")
            scale1_done = sem("scale1_done")
            mod_ready = sem("mod_ready")
            gate_psum = sem("gate_psum")
            gate_taken = sem("gate_taken")
            gate_stored = sem("gate_stored")
            sumsq_ready = sem("sumsq_ready")
            meansq_ready = sem("meansq_ready")
            inv_ready = sem("inv_ready")
            rstd_ready = sem("rstd_ready")
            x_scaled = sem("x_scaled")
            xt_psum = sem("xt_psum")
            xt_taken = sem("xt_taken")
            hi_ready = sem("hi_ready")
            split_done = sem("split_done")

            block = early.enter_context(nc.Block())

            @block.sync
            def _(sp):
                sp.dma_start(vec_rows[0:KT, :], a["c"].rearrange("b (k p) -> (b k) p", p=P)).then_inc(vec_landed, 16)
                sp.dma_start(vec_rows[KT:2 * KT, :],
                             a["norm_g"].rearrange("b (k p) -> (b k) p", p=P)).then_inc(vec_landed, 16)
                sp.dma_start(vec_rows[2 * KT:4 * KT, :],
                             a["b_ada"].rearrange("b (k p) -> (b k) p", p=P)[0:2 * KT, :]).then_inc(vec_landed, 16)
                with sp.Fori(0, TT // UN) as n:
                    for u in range(UN):
                        sp.wait_ge(xt_psum, n * UN + u + 1)
                        sp.dma_start(x_ring[:, u, :],
                                     a["x"][0, bass.ds((n * UN + u) * P, P), :]).then_inc(x_landed[u], 16)
                sp.dma_start(b_gate[:, :],
                             a["b_ada"][0:1, 2 * D_MODEL:3 * D_MODEL].broadcast_to([P, D_MODEL])).then_inc(bgate_landed, 16)
                sp.wait_ge(gate_taken, PIECES - COL_PIECES)
                sp.dma_start(scratch["gate"], b_gate[:, :]).then_inc(gate_stored, 16)
                sp.wait_ge(gate_stored, 16)

            @block.gpsimd
            def _(pool):
                w_view = a["w_ada"][0].rearrange("(k p) n -> p k n", p=P)
                pool.memset(ident[:, :], 0.0).then_inc(zeroed, 1)
                pool.wait_ge(zeroed, 1)
                pool.affine_select(out=ident[:, :], in_=ident[:, :], compare_op=ALU.not_equal, fill=1.0, base=0,
                                   pattern=[[-1, P]], channel_multiplier=1).then_inc(ident_ready, 1)
                with pool.Fori(0, PIECES // AR) as n:
                    for u in range(AR):
                        pool.wait_ge(w_used, n * AR + u + 1)
                        pool.dma_start(w_ring[:, u], w_view[:, :, bass.ds((n * AR + u) * WP, WP)]).then_inc(w_landed[u], 16)

            @block.scalar
            def _(act):
                act.preload_act_table(ACT.Sqrt)
                act.sem_inc(xt_taken, H_SLOTS)

                def rms(n, u, t):
                    act.wait_ge(x_landed[u], (n + 1) * 16)
                    act.activation(junk[:, :], x_ring[:, u, :], ACT.Square,
                                   accum_out=sumsq[:, bass.ds(t, 1)]).then_inc(sumsq_ready, 1)
                    act.wait_ge(inv_ready, t + 1)
                    act.activation(rstd[:, bass.ds(t, 1)], inv_ms[:, bass.ds(t, 1)], ACT.Sqrt).then_inc(rstd_ready, 1)

                def modulated(u, t):
                    act.wait_ge(xt_psum, t + 1 + UN)
                    act.wait_ge(split_done, t + 1)
                    for k in range(KT):
                        ins = act.activation(h_part[:, u % 2, k, :], ps_t[:, u % 2, k, :], ACT.Identity,
                                             bias=mod_b[:, k:k + 1], scale=mod_a[:, k:k + 1])
                    ins.then_inc(xt_taken, 1)

                rms(0, 0, 0)
                act.wait_ge(mod_ready, 2)
                with act.Fori(0, TT // UN - 1) as n:
                    for u in range(UN):
                        rms(n + (u + 1) // UN, (u + 1) % UN, n * UN + u + 1)
                        modulated(u, n * UN + u)
                for u in range(UN):
                    if u + 1 < UN:
                        rms(TT // UN - 1, u + 1, TT - UN + u + 1)
                    modulated(u, TT - UN + u)

            @block.vector
            def _(dve):
                dve.sem_inc(split_done, H_SLOTS)
                dve.wait_ge(vec_transposed, 1)
                dve.tensor_copy(vec_cols[:, :], ps_v[:, 0:4 * KT]).then_inc(vec_ready, 1)
                dve.wait_ge(vec_ready, 1)
                dve.tensor_copy(c_wide[:, :, :],
                                vec_cols[:, 0:KT].unsqueeze(2).broadcast_to([P, KT, P])).then_inc(cwide_ready, 1)

                def normalised(u, t):
                    dve.wait_ge(sumsq_ready, t + 1)
                    dve.tensor_scalar(meansq[:, bass.ds(t, 1)], sumsq[:, bass.ds(t, 1)], 1.0 / D_MODEL, EPS,
                                      ALU.mult, ALU.add).then_inc(meansq_ready, 1)
                    dve.wait_ge(meansq_ready, t + 1)
                    dve.reciprocal(inv_ms[:, bass.ds(t, 1)], meansq[:, bass.ds(t, 1)]).then_inc(inv_ready, 1)
                    dve.wait_ge(rstd_ready, t + 1)
                    dve.tensor_scalar(x_ring[:, u, :], x_ring[:, u, :], rstd[:, bass.ds(t, 1)], None,
                                      ALU.mult).then_inc(x_scaled, 1)

                def split(u, t):
                    dve.wait_ge(xt_taken, t + 1 + H_SLOTS)
                    dve.tensor_copy(h_hi[:, :, bass.ds(t * P, P)], h_part[:, u % 2]).then_inc(hi_ready, 1)
                    dve.wait_ge(hi_ready, t + 1)
                    dve.tensor_sub(h_lo[:, :, bass.ds(t * P, P)], h_part[:, u % 2],
                                   h_hi[:, :, bass.ds(t * P, P)].bitcast(F32)).then_inc(split_done, 1)

                normalised(0, 0)
                dve.wait_ge(w_used, AR + COL_PIECES)
                dve.tensor_scalar(scale1[:, :], ps_m[:, KT:2 * KT], 1.0, None, ALU.add).then_inc(scale1_done, 1)
                dve.wait_ge(scale1_done, 1)
                dve.tensor_add(scale1[:, :], scale1[:, :], vec_cols[:, 3 * KT:4 * KT]).then_inc(scale1_done, 1)
                dve.wait_ge(scale1_done, 2)
                dve.tensor_mul(mod_a[:, :], scale1[:, :], vec_cols[:, KT:2 * KT]).then_inc(mod_ready, 1)
                dve.tensor_add(mod_b[:, :], ps_m[:, 0:KT], vec_cols[:, 2 * KT:3 * KT]).then_inc(mod_ready, 1)
                with dve.Fori(0, TT // UN - 1) as n:
                    for u in range(UN):
                        normalised((u + 1) % UN, n * UN + u + 1)
                        split(u, n * UN + u)
                for u in range(UN):
                    if u + 1 < UN:
                        normalised(u + 1, TT - UN + u + 1)
                    split(u, TT - UN + u)
                dve.wait_ge(bgate_landed, 16)
                for q in range(PIECES - COL_PIECES):
                    dve.wait_ge(gate_psum, q + 1)
                    part = b_gate[:, q * WP:(q + 1) * WP]
                    dve.tensor_add(part, ps_g[:, 0:WP], part).then_inc(gate_taken, 1)

            @block.tensor
            def _(pe):
                pe.sem_inc(xt_psum, UN)
                pe.sem_inc(w_used, AR)
                pe.wait_ge(vec_landed, 48)
                pe.wait_ge(ident_ready, 1)
                pe.transpose(ps_v[:, 0:4 * KT], vec_rows[:, :], ident[0:4 * KT, 0:4 * KT]).then_inc(vec_transposed, 1)
                pe.wait_ge(vec_ready, 1)
                for q in range(COL_PIECES):
                    pe.wait_ge(w_landed[q % AR], (q // AR + 1) * 16)
                    for j in range(WP // P):
                        col = q * (WP // P) + j
                        for k in range(KT):
                            ins = pe.matmul(ps_m[:, col:col + 1], w_ring[:, q % AR, k, j * P:(j + 1) * P],
                                            vec_cols[:, k:k + 1], start=(k == 0), stop=(k == KT - 1))
                    ins.then_inc(w_used, 1)
                with pe.Fori(0, TT // UN) as n:
                    for u in range(UN):
                        t = n * UN + u
                        pe.wait_ge(x_scaled, t + 1)
                        pe.wait_ge(xt_taken, t + 1)
                        for k in range(KT):
                            ins = pe.transpose(ps_t[:, u % 2, k, :], x_ring[:, u, k * P:(k + 1) * P], ident[:, :])
                        ins.then_inc(xt_psum, 1)
                pe.wait_ge(cwide_ready, 1)
                for q in range(COL_PIECES, PIECES):
                    pe.wait_ge(w_landed[q % AR], (q // AR + 1) * 16)
                    if q > COL_PIECES:
                        pe.wait_ge(gate_taken, q - COL_PIECES)
                    for k in range(KT):
                        ins = pe.matmul(ps_g[:, 0:WP], c_wide[:, k, :], w_ring[:, q % AR, k, :],
                                        start=(k == 0), stop=(k == KT - 1))
                    ins.then_inc(gate_psum, 1)

        with ExitStack() as late:
            def lsb(name, shape, dt=F32):
                return late.enter_context(nc.sbuf_tensor("a1_" + name, shape, dt))

            w_land = lsb("w_land", [P, 2, KT, P])
            w_hi = lsb("w_hi", [P, 2, KT, P], F32R)
            w_lo = lsb("w_lo", [P, 2, KT, P], F32R)
            wg_land = lsb("wg_land", [P, KT, 2 * M_HEADS + F_HEADS])
            wg_hi = lsb("wg_hi", [P, KT, P], F32R)
            wg_lo = lsb("wg_lo", [P, KT, P], F32R)
            u_copy = lsb("u_copy", [P, 2, SEQ])
            work = lsb("work", [P, SEQ])
            stage = lsb("stage", [P, 2, SEQ])
            head_mean = lsb("head_mean", [P, HEADS_IN_TILE])
            inv_rms = lsb("inv_rms", [P, TT * HEADS_IN_TILE])
            ident = lsb("ident", [P, P])
            par_rows = lsb("par_rows", [PARAM_ROWS, P])
            ps_u = late.enter_context(nc.psum_tensor("a1_ps_u", [P, 2, TB, NB], F32))

            w_landed = [sem(f"wi_landed{u}") for u in range(2)]
            wg_landed = sem("wg_landed")
            param_landed = sem("param_landed")
            const_zeroed = sem("const_zeroed")
            const_ready = sem("const_ready")
            hi_ready = sem("w_hi_ready")
            w_split = sem("w_split")
            wg_split = sem("wg_split")
            u_psum = sem("u_psum")
            half_free = sem("half_free")
            param_psum = sem("param_psum")
            gain_ready = sem("gain_ready")
            u_copied = sem("u_copied")
            squared = sem("squared")
            means_psum = sem("means_psum")
            spread = sem("spread")
            post_psum = sem("post_psum")
            mean_ready = sem("mean_ready")
            inverse_ready = sem("inverse_ready")
            root_ready = sem("root_ready")
            stage_hi = sem("stage_hi")
            sigmoid_ready = sem("sigmoid_ready")
            conv_started = sem("conv_started")
            tap_done = sem("tap_done")
            finished = sem("finished")
            stored = sem("stored")

            w_view = a["w_in"][0].rearrange("(k p) n -> p k n", p=P)
            G = M_HEADS
            LOADS = ((0, 3 * G, F_Q), (3 * G, 2 * G, 2 * M_W), (5 * G, 2 * G, 0), (7 * G, G, 4 * M_W),
                     (8 * G, G, F_Q + 3 * F_W))
            NORM, TURN, CONV, SILU = 0, 2 * G, 5 * G, 7 * G
            END = 9 * G
            assert END == U_TILES and G % 2 == 0
            block = late.enter_context(nc.Block())

            @block.sync
            def _(sp):
                sp.dma_start(wg_land[:, :, 0:2 * M_HEADS], w_view[:, :, M_GATES:F_Q]).then_inc(wg_landed, 16)
                sp.dma_start(wg_land[:, :, 2 * M_HEADS:], w_view[:, :, F_GATES:D_IN]).then_inc(wg_landed, 16)
                for first, count, column in LOADS:
                    with sp.Fori(0, count // 2) as n:
                        for par in range(2):
                            sp.wait_ge(w_split, n * 2 + par + first + 1)
                            sp.dma_start(w_land[:, par],
                                         w_view[:, :, bass.ds((n * 2 + par) * P + column, P)]).then_inc(w_landed[par], 16)

            @block.gpsimd
            def _(pool):
                pool.memset(ident[:, :], 0.0).then_inc(const_zeroed, 1)
                pool.memset(head_mean[:, :], 0.0).then_inc(const_zeroed, 1)
                pool.wait_ge(const_zeroed, 2)
                pool.affine_select(out=ident[:, :], in_=ident[:, :], compare_op=ALU.not_equal, fill=1.0, base=0,
                                   pattern=[[-1, P]], channel_multiplier=1).then_inc(const_ready, 1)
                for h in range(HEADS_IN_TILE):
                    part = slice(h * F_DH, (h + 1) * F_DH)
                    pool.wait_ge(const_ready, h + 1)
                    pool.memset(head_mean[part, h:h + 1], 1.0 / F_DH).then_inc(const_ready, 1)
                pool.dma_start(par_rows[0:32, :], a["conv_w"][0].rearrange("k (j p) -> (k j) p", p=P)).then_inc(param_landed, 16)
                pool.dma_start(par_rows[32:40, :], a["conv_b"].rearrange("b (j p) -> (b j) p", p=P)).then_inc(param_landed, 16)
                for h in range(HEADS_IN_TILE):
                    part = slice(h * F_DH, (h + 1) * F_DH)
                    pool.dma_start(par_rows[40:41, part], a["fox_qnorm_g"][:, :]).then_inc(param_landed, 16)
                    pool.dma_start(par_rows[41:42, part], a["fox_knorm_g"][:, :]).then_inc(param_landed, 16)
                pool.dma_start(par_rows[42:46, :],
                               a["mlstm_norm_g"].rearrange("b (j p) -> (b j) p", p=P)).then_inc(param_landed, 16)
                pool.wait_ge(finished, 1 + 2)
                pool.dma_start(scratch["gate_rows"], stage[0:ROW_FF + F_HEADS, 0, :]).then_inc(stored, 16)

                def store(out, j, sb_view):
                    pool.wait_ge(finished, j + 4)
                    pool.dma_start(out, sb_view).then_inc(stored, 16)

                with pool.Fori(0, (TURN - NORM)) as n:
                    store(scratch["qkT"][:, bass.ds(n * P, P), :].rearrange("s p c -> p s c"), n + NORM, stage[:, :, :])
                with pool.Fori(0, END - TURN) as n:
                    store(scratch["arrays"][bass.ds(n * P, P), :], n + TURN, stage[:, 0, :])
                pool.wait_ge(stored, (END + 1) * 16)

            @block.vector
            def _(dve):
                dve.sem_inc(w_split, 2)
                dve.sem_inc(finished, 2)

                def split_w(par, n, j):
                    dve.wait_ge(w_landed[par], (n + 1) * 16)
                    dve.tensor_copy(w_hi[:, par], w_land[:, par]).then_inc(hi_ready, 1)
                    dve.wait_ge(hi_ready, j + 1)
                    dve.tensor_sub(w_lo[:, par], w_land[:, par], w_hi[:, par].bitcast(F32)).then_inc(w_split, 1)

                dve.memset(wg_hi[:, :, :].bitcast(F32), 0.0).then_inc(wg_split, 1)
                dve.memset(wg_lo[:, :, :].bitcast(F32), 0.0).then_inc(wg_split, 1)
                dve.wait_ge(wg_landed, 32)
                dve.wait_ge(wg_split, 2)
                for n, (row, first, count) in enumerate(((ROW_I, 0, M_HEADS), (ROW_F, M_HEADS, M_HEADS),
                                                         (ROW_FF, 2 * M_HEADS, F_HEADS))):
                    part = wg_land[:, :, first:first + count]
                    hi = wg_hi[:, :, row:row + count]
                    dve.tensor_copy(hi, part).then_inc(wg_split, 1)
                    dve.wait_ge(wg_split, 3 + 2 * n)
                    dve.tensor_sub(wg_lo[:, :, row:row + count], part, hi.bitcast(F32)).then_inc(wg_split, 1)
                split_w(0, 0, 0)
                split_w(1, 0, 1)
                dve.wait_ge(param_psum, 1)
                dve.tensor_copy(params[:, :], ps_u[:, 0, 0, 0:PARAM_ROWS]).then_inc(half_free, 1)
                dve.wait_ge(u_psum, 1)
                dve.tensor_copy(stage[0:ROW_FF + F_HEADS, 0, :],
                                ps_u[0:ROW_FF + F_HEADS, 1].rearrange("p b n -> p (b n)")).then_inc(half_free, 1)
                dve.wait_ge(half_free, 2)
                dve.sem_inc(finished, 1)

                def begin(par, n, j, split=True):
                    dve.wait_ge(u_psum, j + 2)
                    if split:
                        split_w(par, n + 1, j + 2)

                def flat(par):
                    return ps_u[:, par].rearrange("p b n -> p (b n)")

                dve.wait_ge(gain_ready, 1)
                with dve.Fori(0, (TURN - NORM) // 2) as n:
                    for par in range(2):
                        j = n * 2 + par
                        begin(par, n, j)
                        dve.wait_ge(means_psum, j + 1)
                        dve.tensor_scalar(inv_rms[:, :], ps_u[:, par, 0, 0:TT * HEADS_IN_TILE], EPS, None,
                                          ALU.add).then_inc(mean_ready, 1)
                        dve.wait_ge(mean_ready, j + 1)
                        dve.reciprocal(inv_rms[:, :], inv_rms[:, :]).then_inc(inverse_ready, 1)
                        dve.wait_ge(root_ready, j + 1)
                        dve.tensor_copy(work[:, :].rearrange("p (t d) -> p t d", d=F_DH),
                                        inv_rms[:, :].unsqueeze(2).broadcast_to([P, TT * HEADS_IN_TILE, F_DH])
                                        ).then_inc(spread, 1)
                        dve.wait_ge(post_psum, j + 1)
                        dve.scalar_tensor_tensor(out=u_copy[:, par, :], in0=u_copy[:, par, :],
                                                 scalar=qk_gain[:, bass.ds(j, 1)], in1=flat(par),
                                                 op0=ALU.mult, op1=ALU.mult).then_inc(half_free, 1)
                        dve.wait_ge(half_free, j + 3)
                        dve.wait_ge(stored, (j + 1) * 16)
                        dve.tensor_copy(stage[:, 0, :].bitcast(F32R), u_copy[:, par, :]).then_inc(stage_hi, 1)
                        dve.wait_ge(stage_hi, j + 1)
                        dve.tensor_sub(stage[:, 1, :].bitcast(F32R), u_copy[:, par, :],
                                       stage[:, 0, :]).then_inc(finished, 1)
                with dve.Fori(0, (CONV - TURN) // 2) as n:
                    for par in range(2):
                        j = n * 2 + par + TURN
                        begin(par, n + TURN // 2, j)
                        dve.wait_ge(post_psum, j + 1)
                        dve.wait_ge(stored, (j + 1) * 16)
                        dve.tensor_copy(stage[:, 0, :], flat(par)).then_inc(finished, 1)
                        dve.wait_ge(finished, j + 4)
                        dve.sem_inc(half_free, 1)
                for kind, factor in ((0, 1.0), (1, float(M_DH) ** -0.5)):
                    with dve.Fori(0, G // 2) as n:
                        for par in range(2):
                            i = n * 2 + par + kind * G
                            j = i + CONV
                            begin(par, n + (CONV + kind * G) // 2, j)
                            dve.wait_ge(conv_started, i + 1)
                            for s in range(1, CONV_K):
                                dve.scalar_tensor_tensor(
                                    out=work[:, s:], in0=u_copy[:, par, 0:SEQ - s],
                                    scalar=params[:, bass.ds(i + (CONV_K - 1 - s) * 2 * G, 1)],
                                    in1=work[:, s:], op0=ALU.mult, op1=ALU.add).then_inc(tap_done, 1)
                                dve.wait_ge(tap_done, i * (CONV_K - 1) + s)
                                if s == 1:
                                    dve.sem_inc(half_free, 1)
                            dve.wait_ge(sigmoid_ready, i + 1)
                            dve.wait_ge(stored, (j + 1) * 16)
                            dve.scalar_tensor_tensor(out=stage[:, 0, :], in0=work[:, :], scalar=factor,
                                                     in1=stage[:, 1, :], op0=ALU.mult, op1=ALU.mult).then_inc(finished, 1)

                def silu(par, n, j, split):
                    begin(par, n, j, split)
                    dve.wait_ge(sigmoid_ready, j - CONV + 1)
                    dve.wait_ge(stored, (j + 1) * 16)
                    dve.tensor_mul(stage[:, 0, :], flat(par), work[:, :]).then_inc(finished, 1)
                    dve.wait_ge(finished, j + 4)
                    dve.sem_inc(half_free, 1)

                with dve.Fori(0, (END - SILU) // 2 - 1) as n:
                    for par in range(2):
                        silu(par, n + SILU // 2, n * 2 + par + SILU, True)
                for par in range(2):
                    silu(par, 0, END - 2 + par, False)

            @block.tensor
            def _(pe):
                def project(par, j, hi, lo, post=()):
                    for k in range(KT):
                        for b in range(TB):
                            cols = slice(b * NB, (b + 1) * NB)
                            pe.matmul(ps_u[:, par, b, :], hi[:, k, :], h_hi[:, k, cols], start=(k == 0), stop=False)
                            pe.matmul(ps_u[:, par, b, :], hi[:, k, :], h_lo[:, k, cols], start=False, stop=False)
                        for b in range(TB):
                            cols = slice(b * NB, (b + 1) * NB)
                            ins = pe.matmul(ps_u[:, par, b, :], lo[:, k, :], h_hi[:, k, cols],
                                            start=False, stop=(k == KT - 1))
                        for at, step in post:
                            if k == at:
                                step(1 - par, j - 1)
                    ins.then_inc(u_psum, 1)

                def tile(par, j, post=()):
                    pe.wait_ge(w_split, j + 3)
                    pe.wait_ge(half_free, j + 1)
                    project(par, j, w_hi[:, par], w_lo[:, par], post)

                def head_means(par, j):
                    pe.wait_ge(squared, j + 1)
                    for t in range(TT):
                        ins = pe.matmul(ps_u[:, par, 0, t * HEADS_IN_TILE:(t + 1) * HEADS_IN_TILE],
                                        work[:, t * P:(t + 1) * P], head_mean[:, :], start=True, stop=True)
                    ins.then_inc(means_psum, 1)

                def turn(par, source):
                    view = ps_u[:, par].rearrange("p b (t n) -> p (b t) n", n=P)
                    for t in range(TT):
                        ins = pe.transpose(view[:, t, :], source[:, t * P:(t + 1) * P], ident[:, :])
                    ins.then_inc(post_psum, 1)

                def turned_norms(par, j):
                    pe.wait_ge(spread, j + 1)
                    turn(par, work)

                def turned(par, j):
                    pe.wait_ge(u_copied, j + 1)
                    turn(par, u_copy[:, par])

                pe.wait_ge(const_ready, 3)
                pe.wait_ge(param_landed, 7 * 16)
                pe.transpose(ps_u[:, 0, 0, 0:PARAM_ROWS], par_rows[:, :],
                             ident[0:PARAM_ROWS, 0:PARAM_ROWS]).then_inc(param_psum, 1)
                pe.wait_ge(wg_split, 8)
                project(1, 0, wg_hi[:, :, :], wg_lo[:, :, :])
                tile(0, 0)
                with pe.Fori(0, (TURN - NORM) // 2) as n:
                    tile(1, n * 2 + 1, ((2, head_means), (5, turned_norms)))
                    tile(0, n * 2 + 2, ((2, head_means), (5, turned_norms)))
                with pe.Fori(0, (CONV - TURN) // 2) as n:
                    tile(1, n * 2 + 1 + TURN, ((2, turned),))
                    tile(0, n * 2 + 2 + TURN, ((2, turned),))
                with pe.Fori(0, (END - CONV) // 2 - 1) as n:
                    tile(1, n * 2 + 1 + CONV)
                    tile(0, n * 2 + 2 + CONV)
                tile(1, END - 1)

            @block.scalar
            def _(act):
                def copy(par, j, func=ACT.Copy):
                    act.wait_ge(u_psum, j + 2)
                    act.wait_ge(finished, j + 2)
                    return act.activation(u_copy[:, par, :], flat(par), func)

                def flat(par):
                    return ps_u[:, par].rearrange("p b n -> p (b n)")

                act.preload_act_table(ACT.Sqrt)
                act.wait_ge(half_free, 1)
                act.activation(qk_gain[:, 0:G], params[:, 40:41].broadcast_to([P, G]), ACT.Copy,
                               scale=float(F_DH) ** -0.5)
                act.activation(qk_gain[:, G:2 * G], params[:, 41:42].broadcast_to([P, G]), ACT.Copy).then_inc(gain_ready, 1)
                with act.Fori(0, (TURN - NORM) // 2) as n:
                    for par in range(2):
                        j = n * 2 + par
                        copy(par, j).then_inc(u_copied, 1)
                        act.wait_ge(finished, j + 3)
                        act.activation(work[:, :], flat(par), ACT.Square).then_inc(squared, 1)
                        act.wait_ge(inverse_ready, j + 1)
                        act.activation(inv_rms[:, :], inv_rms[:, :], ACT.Sqrt).then_inc(root_ready, 1)
                with act.Fori(0, G) as n:
                    for par in range(2):
                        copy(par, n * 2 + par + TURN).then_inc(u_copied, 1)
                act.preload_act_table(ACT.Sigmoid)
                with act.Fori(0, G // 2) as n:
                    for par in range(2):
                        copy(par, n * 2 + par + TURN + 2 * G, ACT.Sigmoid).then_inc(u_copied, 1)
                with act.Fori(0, G) as n:
                    for par in range(2):
                        i = n * 2 + par
                        copy(par, i + CONV)
                        act.wait_ge(finished, i + CONV + 3)
                        act.activation(work[:, :], flat(par), ACT.Identity,
                                       bias=params[:, bass.ds(i + CONV_K * 2 * G, 1)],
                                       scale=params[:, bass.ds(i + (CONV_K - 1) * 2 * G, 1)]).then_inc(conv_started, 1)
                        act.wait_ge(tap_done, (i + 1) * (CONV_K - 1))
                        act.activation(stage[:, 1, :], work[:, :], ACT.Sigmoid).then_inc(sigmoid_ready, 1)
                with act.Fori(0, (END - SILU) // 2) as n:
                    for par in range(2):
                        j = n * 2 + par + SILU
                        act.wait_ge(u_psum, j + 2)
                        act.wait_ge(finished, j + 3)
                        act.activation(work[:, :], flat(par), ACT.Sigmoid).then_inc(sigmoid_ready, 1)




def gate_rows(nc, a, scratch, keep):
    with ExitStack() as ctx:
        def sb(name, shape, dt=F32):
            return ctx.enter_context(nc.sbuf_tensor("g_" + name, shape, dt))

        def sem(name):
            return ctx.enter_context(nc.semaphore("g_" + name))

        R = ROW_FF + F_HEADS
        I, F, FF = slice(ROW_I, ROW_I + M_HEADS), slice(ROW_F, ROW_F + M_HEADS), slice(ROW_FF, ROW_FF + F_HEADS)
        LOGS = slice(0, R)
        pre = sb("pre", [R, SEQ])
        bias = sb("bias", [R, 1])
        log_f = sb("log_f", [R, SEQ])
        keep_on = sb("keep_on", [R, SEQ])
        neg_sum = sb("neg_sum", [R, SEQ])
        chunk_sum = sb("chunk_sum", [R, SEQ])
        b_row = sb("b_row", [M_HEADS, SEQ])
        carried = sb("carried", [M_HEADS, SEQ])
        g_max = sb("g_max", [M_HEADS, SEQ])
        m_prev = sb("m_prev", [M_HEADS, CHUNKS])
        last_b = sb("last_b", [M_HEADS, CHUNKS])
        decay = sb("decay", [M_HEADS, CHUNKS])
        columns = sb("columns", [GATE_COLS, SEQ])
        ident = sb("ident", [P, P])
        ps = ctx.enter_context(nc.psum_tensor("g_ps", [P, CHUNKS, P], F32))

        landed = sem("landed")
        zeroed = sem("zeroed")
        ident_ready = sem("ident_ready")
        reset_ready = sem("reset_ready")
        step = {name: sem(name) for name in (
            "bias_zero", "biased", "magnitude", "exp_neg", "log1p", "log_ready", "neg_sum_ready", "chunk_ready",
            "b_ready", "g_ready", "last_ready", "carried_ready", "g_max_ready", "m_prev_ready", "differences",
            "exponentials", "turned", "stored")}

        def chunked(row):
            return row.rearrange("h (c t) -> h c t", t=CHUNK)

        block = ctx.enter_context(nc.Block())

        @block.sync
        def _(sp):
            sp.dma_start(pre[:, :], scratch["gate_rows"]).then_inc(landed, 16)
            sp.wait_ge(step["bias_zero"], 1)
            for rows, name in ((I, "b_igate"), (F, "b_fgate_m"), (FF, "b_fgate_f")):
                sp.dma_start(bias[rows, :], a[name].rearrange("b h -> h b")).then_inc(landed, 16)
            sp.wait_ge(step["neg_sum_ready"], 1)
            sp.dma_start(scratch["f_negF"], neg_sum[FF, :]).then_inc(step["stored"], 16)
            sp.wait_ge(step["g_max_ready"], 1)
            sp.dma_start(scratch["m_G"], g_max[:, :]).then_inc(step["stored"], 16)
            sp.wait_ge(step["m_prev_ready"], 1)
            sp.dma_start(scratch["m_prev"], m_prev[:, :]).then_inc(step["stored"], 16)
            sp.wait_ge(step["exponentials"], 3)
            sp.dma_start(scratch["m_decay"], decay[:, :]).then_inc(step["stored"], 16)
            sp.wait_ge(step["stored"], 4 * 16)

        @block.gpsimd
        def _(pool):
            pool.memset(ident[:, :], 0.0).then_inc(zeroed, 1)
            pool.wait_ge(zeroed, 1)
            pool.affine_select(out=ident[:, :], in_=ident[:, :], compare_op=ALU.not_equal, fill=1.0, base=0,
                               pattern=[[-1, P]], channel_multiplier=1).then_inc(ident_ready, 1)
            pool.memset(columns[:, :], 0.0).then_inc(zeroed, 1)
            pool.memset(carried[:, :], 0.0).then_inc(zeroed, 1)
            pool.memset(keep_on[:, :], 1.0).then_inc(zeroed, 1)
            pool.wait_ge(zeroed, 4)
            pool.memset(chunked(keep_on[F, :])[:, :, 0:1], 0.0).then_inc(reset_ready, 1)

        @block.scalar
        def _(act):
            act.preload_act_table_set("natural_log_exp_and_others")
            act.wait_ge(step["biased"], 1)
            act.activation(log_f[LOGS, :], pre[LOGS, :], ACT.Abs).then_inc(step["magnitude"], 1)
            act.wait_ge(step["magnitude"], 1)
            act.activation(log_f[LOGS, :], log_f[LOGS, :], ACT.Exp, scale=-1.0).then_inc(step["exp_neg"], 1)
            act.wait_ge(step["exp_neg"], 1)
            act.activation(log_f[LOGS, :], log_f[LOGS, :], ACT.Ln, bias=1.0).then_inc(step["log1p"], 1)
            act.wait_ge(step["differences"], 3)
            act.activation(columns[COL_WS:COL_WS + M_HEADS, :], columns[COL_WS:COL_WS + M_HEADS, :],
                           ACT.Exp).then_inc(step["exponentials"], 1)
            act.activation(columns[COL_EM:COL_EM + M_HEADS, :], columns[COL_EM:COL_EM + M_HEADS, :],
                           ACT.Exp).then_inc(step["exponentials"], 1)
            act.activation(decay[:, :], decay[:, :], ACT.Exp).then_inc(step["exponentials"], 1)

        @block.vector
        def _(dve):
            def done(name, count=1):
                dve.wait_ge(step[name], count)

            dve.memset(bias[:, :], 0.0).then_inc(step["bias_zero"], 1)
            dve.memset(keep["eps"][:, :], EPS)
            dve.wait_ge(landed, 64)
            dve.tensor_scalar(pre[:, :], pre[:, :], bias[:, 0:1], None, ALU.add).then_inc(step["biased"], 1)
            dve.wait_ge(step["log1p"], 1)
            dve.scalar_tensor_tensor(out=log_f[LOGS, :], in0=pre[LOGS, :], scalar=0.0, in1=log_f[LOGS, :],
                                     op0=ALU.min, op1=ALU.subtract).then_inc(step["log_ready"], 1)
            done("log_ready")
            dve.wait_ge(reset_ready, 1)
            dve.tensor_tensor_scan(out=neg_sum[FF, :], data0=keep_on[FF, :], data1=log_f[FF, :], initial=0.0,
                                   op0=ALU.mult, op1=ALU.subtract).then_inc(step["neg_sum_ready"], 1)
            dve.tensor_tensor_scan(out=chunk_sum[F, :], data0=keep_on[F, :], data1=log_f[F, :], initial=0.0,
                                   op0=ALU.mult, op1=ALU.add).then_inc(step["chunk_ready"], 1)
            done("chunk_ready")
            dve.tensor_copy(b_row[:, :], chunk_sum[F, :]).then_inc(step["b_ready"], 1)
            done("b_ready")
            g_row = columns[COL_G:COL_G + M_HEADS, :]
            dve.tensor_sub(g_row, pre[I, :], b_row[:, :]).then_inc(step["g_ready"], 1)
            dve.tensor_copy(chunked(carried[:, :])[:, 1:, 0], chunked(b_row[:, :])[:, :-1, CHUNK - 1]
                            ).then_inc(step["carried_ready"], 1)
            done("g_ready")
            done("carried_ready")
            dve.tensor_tensor_scan(out=g_max[:, :], data0=carried[:, :], data1=g_row, initial=0.0,
                                   op0=ALU.add, op1=ALU.max).then_inc(step["g_max_ready"], 1)
            dve.memset(m_prev[:, 0:1], 0.0)
            done("g_max_ready")
            last_G = chunked(g_max[:, :])[:, :, CHUNK - 1]
            dve.tensor_add(m_prev[:, 1:], chunked(carried[:, :])[:, 1:, 0], last_G[:, :-1]).then_inc(step["m_prev_ready"], 1)
            dve.tensor_sub(chunked(columns[COL_WS:COL_WS + M_HEADS, :]), chunked(g_row),
                           last_G.unsqueeze(2).broadcast_to([M_HEADS, CHUNKS, CHUNK])).then_inc(step["differences"], 1)
            em_row = columns[COL_EM:COL_EM + M_HEADS, :]
            dve.tensor_add(em_row, b_row[:, :], g_max[:, :]).then_inc(step["last_ready"], 1)
            done("last_ready")
            dve.tensor_scalar(em_row, em_row, -1.0, EXP_MAX, ALU.mult, ALU.min).then_inc(step["differences"], 1)
            done("m_prev_ready")
            dve.tensor_sub(decay[:, :], m_prev[:, :], last_G).then_inc(step["differences"], 1)
            dve.wait_ge(step["turned"], 1)
            dve.tensor_copy(keep["gate_cols"][:, :, :], ps[:, :, 0:GATE_COLS])

        @block.tensor
        def _(pe):
            pe.wait_ge(ident_ready, 1)
            pe.wait_ge(step["exponentials"], 3)
            for c in range(CHUNKS):
                ins = pe.transpose(ps[:, c, 0:GATE_COLS], columns[:, c * CHUNK:(c + 1) * CHUNK],
                                   ident[0:GATE_COLS, 0:GATE_COLS])
            ins.then_inc(step["turned"], 1)


def forgetting_heads(nc, a, scratch, w_land):
    with ExitStack() as ctx:
        def sb(name, shape, dt=F32):
            return ctx.enter_context(nc.sbuf_tensor("f_" + name, shape, dt))

        def psum(name, shape):
            return ctx.enter_context(nc.psum_tensor("f_" + name, shape, F32))

        def sem(name):
            return ctx.enter_context(nc.semaphore("f_" + name))

        QT = NB // P
        GROUPS = TT // QT
        HP = HEADS_IN_TILE
        PAIRS = F_HEADS // HP
        q_pack = sb("q_pack", [P, HP, SEQ], F32R)
        k_hi2 = sb("k_hi2", [P, HP, SEQ], F32R)
        k_lo2 = sb("k_lo2", [P, HP, SEQ], F32R)
        neg_f = sb("neg_f", [P, HP, SEQ])
        v_tok = sb("v_tok", [P, TT, HP, F_DH])
        gate_z = sb("gate_z", [P, SEQ])
        probs = sb("probs", [P, 2, QT, SEQ])
        probs_t = sb("probs_t", [P, 2, 2, NB])
        out_t = sb("out_t", [P, NB])
        out_tok = sb("out_tok", [P, 2, QT, HP, F_DH])
        y_out = sb("y_out", [P, 2, NB])
        part_max = sb("part_max", [P, 2, QT, GROUPS])
        neg_max = sb("neg_max", [P, 2, QT])
        row_sum = sb("row_sum", [P, 4, QT])
        inv_sum = sb("inv_sum", [P, 4, QT])
        ident = sb("ident", [P, P])
        mask = sb("mask", [P, P])
        ident_r = sb("ident_r", [P, P], F32R)
        mask_r = sb("mask_r", [P, P], F32R)
        fold = sb("fold", [P, F_DH])
        ps_s = psum("ps_s", [P, 2, NB])
        ps_t = psum("ps_t", [P, 2, 2, NB])
        ps_o = psum("ps_o", [P, NB])
        ps_x = psum("ps_x", [P, NB])

        zeroed = sem("zeroed")
        const_ready = sem("const_ready")
        masks_ready = sem("masks_ready")
        head_landed = [sem(f"head_landed{h}") for h in range(HP)]
        v_landed = [sem(f"v_landed{i}") for i in range(2)]
        z_landed = sem("z_landed")
        s_psum = sem("s_psum")
        s_used = sem("s_used")
        logits_begun = sem("logits_begun")
        max_ready = sem("max_ready")
        exp_ready = sem("exp_ready")
        t_psum = sem("t_psum")
        even_ready = sem("even_ready")
        odd_ready = sem("odd_ready")
        pv_done = sem("pv_done")
        ot_ready = sem("ot_ready")
        fold_psum = sem("fold_psum")
        inv_ready = sem("inv_ready")
        x_used = sem("x_used")
        y_psum = sem("y_psum")
        y_stored = [sem(f"y_stored{i}") for i in range(2)]
        w_landed = sem("w_landed")

        ORDER = [(h, J) for J in range(GROUPS) for h in range(HP)]
        assert HP == 2
        X_READS = (HP + 1) * GROUPS

        def x_reads_before(g):
            return (HP + 1) * (g // HP) + g % HP

        def chunks(J):
            return [(r, c, NB if c < J else (r + 1) * P, c == J) for r in range(QT) for c in range(J + 1)]

        def pairs(J):
            return QT * (J + 1) // 2

        def chunks_before(g, m=0):
            return sum(len(chunks(J)) for _, J in ORDER[:g]) + m

        def pairs_before(g, p=0):
            return sum(pairs(J) for _, J in ORDER[:g]) + p

        ALL_CHUNKS, ALL_PAIRS, ALL_ROWS = chunks_before(len(ORDER)), pairs_before(len(ORDER)), QT * len(ORDER)

        LAST = len(ORDER)

        def plan(g, last):
            n = pairs(ORDER[g][1])
            following = [] if g + 1 == LAST and last else chunks(ORDER[(g + 1) % LAST][1])
            steps = max(1, n - 1.5)
            cuts = [min(len(following), math.ceil(len(following) * p / steps)) for p in range(n + 1)]
            return [list(enumerate(following))[cuts[p]:cuts[p + 1]] for p in range(n)]

        def columns_of(J, kt):
            return max(0, kt - QT * J) * P

        block = ctx.enter_context(nc.Block())

        @block.sync
        def _(sp):
            def load_head(h, pair, row):
                for part in range(2):
                    rows = slice(part * F_DH, (part + 1) * F_DH)
                    sp.dma_start(q_pack[rows, h, :].bitcast(F32), scratch["qkT"][part, bass.ds(row, F_DH), :]
                                 ).then_inc(head_landed[h], 16)
                    sp.dma_start(k_hi2[rows, h, :].bitcast(F32), scratch["qkT"][0, bass.ds(row + F_W, F_DH), :]
                                 ).then_inc(head_landed[h], 16)
                    sp.dma_start(k_lo2[rows, h, :].bitcast(F32), scratch["qkT"][1, bass.ds(row + F_W, F_DH), :]
                                 ).then_inc(head_landed[h], 16)
                sp.dma_start(neg_f[:, h, :], scratch["f_negF"][bass.ds(pair * HP + h, 1), :].broadcast_to([P, SEQ])
                             ).then_inc(head_landed[h], 16)

            def load_v(half, pair):
                cols = slice(half * SEQ // 2, (half + 1) * SEQ // 2)
                sp.dma_start(v_tok[:, :, :, :].rearrange("p t h d -> p (t h d)")[:, cols],
                             scratch["arrays"][bass.ds(pair * P + A_FV * P, P), cols]).then_inc(v_landed[half], 16)

            def load_z(pair):
                sp.dma_start(gate_z[:, :], scratch["arrays"][bass.ds(pair * P + A_FZ * P, P), :]).then_inc(z_landed, 16)

            for h in range(HP):
                load_head(h, 0, h * F_DH)
            for half in range(2):
                load_v(half, 0)
            load_z(0)
            sp.dma_start(w_land[:, :, :], a["w_out"][0].rearrange("(k p) n -> p k n", p=P)).then_inc(w_landed, 16)

            def store_y(n, J):
                sp.wait_ge(x_used, n * X_READS + (HP + 1) * (J + 1) + 1)
                sp.dma_start(scratch["yT"][bass.ds(n * P, P), J * NB:(J + 1) * NB],
                             y_out[:, J % 2, :]).then_inc(y_stored[J % 2], 16)

            with sp.Fori(0, PAIRS - 1) as n:
                for J in range(GROUPS - 2):
                    store_y(n, J)
                sp.wait_ge(s_used, n * ALL_CHUNKS + 2 + chunks_before(LAST - 1))
                load_head(0, n + 1, n * P + P)
                store_y(n, GROUPS - 2)
                sp.wait_ge(s_used, n * ALL_CHUNKS + 2 + chunks_before(LAST))
                load_head(1, n + 1, n * P + P + F_DH)
                for half in range(2):
                    sp.wait_ge(pv_done, n * ALL_PAIRS + 2 + pairs_before(LAST - 1, (half + 1) * TT // 4))
                    load_v(half, n + 1)
                store_y(n, GROUPS - 1)
                load_z(n + 1)
            for J in range(GROUPS):
                store_y(PAIRS - 1, J)
            for i in range(2):
                sp.wait_ge(y_stored[i], 16 + PAIRS * GROUPS // 2 * 16)
            sp.wait_ge(w_landed, 16)

        @block.gpsimd
        def _(pool):
            pool.memset(ident[:, :], 0.0).then_inc(zeroed, 1)
            pool.memset(mask[:, :], 0.0).then_inc(zeroed, 1)
            pool.memset(fold[:, :], 0.0).then_inc(zeroed, 1)
            pool.wait_ge(zeroed, 3)
            pool.affine_select(out=ident[:, :], in_=ident[:, :], compare_op=ALU.not_equal, fill=1.0, base=0,
                               pattern=[[-1, P]], channel_multiplier=1).then_inc(const_ready, 1)
            pool.affine_select(out=mask[:, :], in_=mask[:, :], compare_op=ALU.is_ge, fill=MASKED, base=0,
                               pattern=[[-1, P]], channel_multiplier=1).then_inc(const_ready, 1)
            for h in range(2):
                pool.wait_ge(const_ready, 2 + h)
                pool.affine_select(out=fold[:, :], in_=fold[:, :], compare_op=ALU.not_equal, fill=1.0,
                                   base=-h * F_DH, pattern=[[-1, F_DH]], channel_multiplier=1).then_inc(const_ready, 1)

        @block.tensor
        def _(pe):
            pe.sem_inc(fold_psum, 1)
            pe.wait_ge(const_ready, 4)
            pe.wait_ge(masks_ready, 2)
            def pair_of_heads(n, last_pair):
                def scores(g, m, r, c, width, last):
                    h, J = ORDER[g % LAST]
                    at = chunks_before(g, m)
                    if J == 0 and m == 0:
                        pe.wait_ge(head_landed[h], (n + 1 + g // LAST) * 7 * 16)
                    pe.wait_ge(s_used, n * ALL_CHUNKS + at + 1)
                    q = q_pack[:, h, (J * QT + r) * P:(J * QT + r + 1) * P]
                    keys = slice(c * NB, c * NB + width)
                    bank = ps_s[:, at % 2, :]
                    pe.matmul(bank[:, 0:width], q, k_hi2[:, h, keys], start=True, stop=False)
                    ins = pe.matmul(bank[:, 0:width], q, k_lo2[:, h, keys], start=False, stop=not last)
                    if last:
                        ins = pe.matmul(bank[:, width - P:width], ident_r[:, :], mask_r[:, :], start=False, stop=True)
                    ins.then_inc(s_psum, 1)

                def turn(g, p):
                    h, J = ORDER[g % LAST]
                    at = pairs_before(g, p)
                    for r in range(QT):
                        if p == 0:
                            pe.wait_ge(exp_ready, n * ALL_ROWS + g * QT + r + 1)
                        for e in range(2):
                            kt = 2 * p + e
                            if r * P >= columns_of(J, kt):
                                ins = pe.transpose(ps_t[:, at % 2, e, r * P:(r + 1) * P],
                                                   probs[:, g % 2, r, kt * P:(kt + 1) * P], ident[:, :])
                    ins.then_inc(t_psum, 1)

                def product(g, p):
                    h, J = ORDER[g % LAST]
                    at = pairs_before(g, p)
                    pe.wait_ge(even_ready, n * ALL_PAIRS + at + 1)
                    pe.wait_ge(odd_ready, n * ALL_PAIRS + at + 1)
                    for half in range(2):
                        if h == 0 and 2 * p == half * TT // 2 and J == half * TT // 2 // QT:
                            pe.wait_ge(v_landed[half], (n + 1) * 16)
                    if p == 0:
                        pe.wait_ge(ot_ready, n * LAST + g + 1)
                    for e in range(2):
                        kt = 2 * p + e
                        first = columns_of(J, kt)
                        ins = pe.matmul(ps_o[e * F_DH:(e + 1) * F_DH, first:], v_tok[:, kt, h, :],
                                        probs_t[:, at % 2, e, first:], start=(p == 0), stop=(p == pairs(J) - 1))
                    ins.then_inc(pv_done, 1)

                def finish(g):
                    h, J = ORDER[g % LAST]
                    pe.wait_ge(ot_ready, n * LAST + g + 2)
                    pe.wait_ge(x_used, n * X_READS + x_reads_before(g) + 1)
                    for r in range(QT):
                        rows = slice(0, F_DH if J == 0 and r == 0 else P)
                        ins = pe.matmul(ps_x[:, r * F_DH:(r + 1) * F_DH], out_t[rows, r * P:(r + 1) * P],
                                        fold[rows, :], start=True, stop=True)
                    ins.then_inc(fold_psum, 1)

                def turn_back(g):
                    h, J = ORDER[g % LAST]
                    if h == HP - 1:
                        pe.wait_ge(x_used, n * X_READS + x_reads_before(g) + 2)
                        for r in range(QT):
                            ins = pe.transpose(ps_x[:, r * P:(r + 1) * P],
                                               out_tok[:, J % 2, r, :, :].rearrange("p h d -> p (h d)"), ident[:, :])
                        ins.then_inc(y_psum, 1)

                if n is None:
                    n = 0
                    for m, chunk in enumerate(chunks(ORDER[0][1])):
                        scores(0, m, *chunk)
                    turn(0, 0)
                    return
                for g, (h, J) in enumerate(ORDER):
                    for p, share in enumerate(plan(g, last_pair)):
                        for m, chunk in share[:1]:
                            scores(g + 1, m, *chunk)
                        if g or p:
                            turn(g, p)
                        for m, chunk in share[1:2]:
                            scores(g + 1, m, *chunk)
                        if p:
                            product(g, p - 1)
                        for m, chunk in share[2:]:
                            scores(g + 1, m, *chunk)
                        if p == 0 and g:
                            finish(g - 1)
                        if p == 1 and g:
                            turn_back(g - 1)
                    product(g, pairs(J) - 1)
                if not last_pair:
                    turn(LAST, 0)
                finish(LAST - 1)
                turn_back(LAST - 1)

            pair_of_heads(None, False)
            with pe.Fori(0, PAIRS - 1) as n:
                pair_of_heads(n, False)
            pair_of_heads(PAIRS - 1, True)

        @block.vector
        def _(dve):
            dve.wait_ge(const_ready, 4)
            dve.tensor_copy(ident_r[:, :], ident[:, :]).then_inc(masks_ready, 1)
            dve.tensor_copy(mask_r[:, :], mask[:, :]).then_inc(masks_ready, 1)
            dve.sem_inc(s_used, 2)
            dve.sem_inc(x_used, 1)
            def pair_of_heads(n, last_pair):
                def logits(g, m, r, c, width, last):
                    h, J = ORDER[g % LAST]
                    at = chunks_before(g, m)
                    dve.wait_ge(s_psum, n * ALL_CHUNKS + at + 1)
                    if J == 0 and m == 0:
                        dve.wait_ge(head_landed[h], (n + 1 + g // LAST) * 7 * 16)
                    keys = slice(c * NB, c * NB + width)
                    dve.sem_inc(logits_begun, 1)
                    dve.tensor_tensor_reduce(out=probs[:, g % 2, r, keys], in0=ps_s[:, at % 2, 0:width],
                                             in1=neg_f[:, h, keys], scale=1.0, scalar=MASKED, op0=ALU.add,
                                             op1=ALU.max, accum_out=part_max[:, g % 2, r, c:c + 1]
                                             ).then_inc(s_used, 1)
                    if last:
                        dve.wait_ge(s_used, n * ALL_CHUNKS + at + 3)
                        dve.tensor_reduce(neg_max[:, g % 2, r:r + 1], part_max[:, g % 2, r, 0:c + 1], axis=AX_X,
                                          op=ALU.max, negate=True).then_inc(max_ready, 1)

                def odd(g, p):
                    h, J = ORDER[g % LAST]
                    at = pairs_before(g, p)
                    first = columns_of(J, 2 * p + 1)
                    dve.wait_ge(t_psum, n * ALL_PAIRS + at + 1)
                    dve.wait_ge(pv_done, n * ALL_PAIRS + at + 1)
                    dve.tensor_copy(probs_t[:, at % 2, 1, first:], ps_t[:, at % 2, 1, first:]).then_inc(odd_ready, 1)

                def finish(g):
                    h, J = ORDER[g % LAST]
                    dve.wait_ge(exp_ready, n * ALL_ROWS + (g + 1) * QT)
                    dve.reciprocal(inv_sum[:, g % 4, :], row_sum[:, g % 4, :]).then_inc(inv_ready, 1)
                    dve.wait_ge(inv_ready, n * LAST + g + 1)
                    dve.wait_ge(fold_psum, n * LAST + g + 2)
                    dve.tensor_mul(out_tok[:, J % 2, :, h, :],
                                   ps_x[:, 0:QT * F_DH].rearrange("p (r d) -> p r d", d=F_DH),
                                   inv_sum[:, g % 4, :].unsqueeze(2).broadcast_to([P, QT, F_DH])).then_inc(x_used, 1)

                def output(g):
                    h, J = ORDER[g % LAST]
                    if h == HP - 1:
                        dve.wait_ge(y_psum, n * GROUPS + J + 1)
                        dve.wait_ge(z_landed, (n + 1) * 16)
                        dve.wait_ge(y_stored[J % 2], (n * GROUPS // 2 + J // 2 + 1) * 16)
                        dve.tensor_mul(y_out[:, J % 2, :], ps_x[:, :], gate_z[:, J * NB:(J + 1) * NB]).then_inc(x_used, 1)

                if n is None:
                    n = 0
                    for m, chunk in enumerate(chunks(ORDER[0][1])):
                        logits(0, m, *chunk)
                    odd(0, 0)
                    return
                for g, (h, J) in enumerate(ORDER):
                    for p, share in enumerate(plan(g, last_pair)):
                        for m, chunk in share[:1]:
                            logits(g + 1, m, *chunk)
                        if g or p:
                            odd(g, p)
                        for m, chunk in share[1:]:
                            logits(g + 1, m, *chunk)
                        if p == 0 and g:
                            finish(g - 1)
                        if p == 1 and g:
                            output(g - 1)
                if not last_pair:
                    odd(LAST, 0)
                finish(LAST - 1)
                output(LAST - 1)

            pair_of_heads(None, False)
            with dve.Fori(0, PAIRS - 1) as n:
                pair_of_heads(n, False)
            pair_of_heads(PAIRS - 1, True)

        @block.scalar
        def _(act):
            act.preload_act_table(ACT.Exp)
            act.sem_inc(ot_ready, 1)
            act.sem_inc(pv_done, 2)
            act.sem_inc(y_stored[0], 16)
            act.sem_inc(y_stored[1], 16)
            def pair_of_heads(n, last_pair):
                def exponential(g, m, r, c, width, last):
                    if not last:
                        return
                    act.wait_ge(max_ready, n * ALL_ROWS + g * QT + r + 1)
                    row = probs[:, g % 2, r, 0:c * NB + width]
                    act.activation(row, row, ACT.Exp, bias=neg_max[:, g % 2, r:r + 1],
                                   accum_out=row_sum[:, g % 4, r:r + 1]).then_inc(exp_ready, 1)

                def even(g, p):
                    h, J = ORDER[g % LAST]
                    at = pairs_before(g, p)
                    first = columns_of(J, 2 * p)
                    act.wait_ge(t_psum, n * ALL_PAIRS + at + 1)
                    act.wait_ge(pv_done, n * ALL_PAIRS + at + 1)
                    act.activation(probs_t[:, at % 2, 0, first:], ps_t[:, at % 2, 0, first:], ACT.Copy
                                   ).then_inc(even_ready, 1)

                if n is None:
                    n = 0
                    for m, chunk in enumerate(chunks(ORDER[0][1])):
                        exponential(0, m, *chunk)
                    even(0, 0)
                    return
                for g, (h, J) in enumerate(ORDER):
                    for p, share in enumerate(plan(g, last_pair)):
                        if g or p:
                            even(g, p)
                        for m, chunk in share:
                            exponential(g + 1, m, *chunk)
                    act.wait_ge(pv_done, n * ALL_PAIRS + 2 + pairs_before(g + 1))
                    act.wait_ge(fold_psum, n * LAST + g + 1)
                    if J == 0:
                        act.activation(out_t[0:F_DH, 0:P], ps_o[0:F_DH, 0:P], ACT.Copy)
                        act.activation(out_t[:, P:], ps_o[:, P:], ACT.Copy).then_inc(ot_ready, 1)
                    else:
                        act.activation(out_t[:, :], ps_o[:, :], ACT.Copy).then_inc(ot_ready, 1)
                if not last_pair:
                    even(LAST, 0)

            pair_of_heads(None, False)
            with act.Fori(0, PAIRS - 1) as n:
                pair_of_heads(n, False)
            pair_of_heads(PAIRS - 1, True)



def memory_heads_and_output(nc, a, scratch, keep, w_land, out):
    with ExitStack() as ctx:
        def sb(name, shape, dt=F32):
            return ctx.enter_context(nc.sbuf_tensor("m_" + name, shape, dt))

        def psum(name, shape):
            return ctx.enter_context(nc.psum_tensor("m_" + name, shape, F32))

        def sem(name):
            return ctx.enter_context(nc.semaphore("m_" + name))

        H, W = M_HEADS, M_DH + 1
        FT = F_W // P
        ON = D_MODEL // NB
        q_in = sb("q_in", [P, 2, H, CHUNK])
        k_in = sb("k_in", [P, 2, H, CHUNK])
        v_in = sb("v_in", [P, 2, H, W])
        o_in = sb("o_in", [P, 2, H, M_DH])
        z_in = sb("z_in", [P, 2, H, CHUNK])
        g_max = sb("g_max", [P, 2, H, CHUNK])
        w_in = sb("w_in", [P, 2, H, CHUNK])
        decay = sb("decay", [P, H, CHUNKS])
        m_prev = sb("m_prev", [P, H, CHUNKS])
        diff = sb("diff", [P, 2, H, CHUNK])
        q_w = sb("q_w", [P, 2, H, CHUNK])
        scores = sb("scores", [P, H, CHUNK])
        k_w = sb("k_w", [P, H, M_DH])
        state = sb("state", [P, 2, H, W])
        den = sb("den", [P, 2, H])
        gated = sb("gated", [P, H, M_DH])
        stats = sb("stats", [P, H, nc.vector.BN_STATS_DIM])
        moments = sb("moments", [P, H, 2])
        rstd = sb("rstd", [P, H])
        normed = sb("normed", [P, H, M_DH])
        ident = sb("ident", [P, P])
        future = sb("future", [P, CHUNK])
        w_hi = sb("w_hi", [P, KT, D_MODEL], F32R)
        w_lo = sb("w_lo", [P, KT, D_MODEL], F32R)
        gate = sb("gate", [P, D_MODEL])
        y = sb("y", [P, 2, KT, CHUNK])
        y_hi = sb("y_hi", [P, 2, KT, CHUNK], F32R)
        y_lo = sb("y_lo", [P, 2, KT, CHUNK], F32R)
        x_in = sb("x_in", [P, 2, D_MODEL])
        update = sb("update", [P, 2, D_MODEL])
        result = sb("result", [P, 2, D_MODEL])
        ps_s = psum("ps_s", [P, H, CHUNK])
        ps_k = psum("ps_k", [P, H, CHUNK])
        ps_m = psum("ps_m", [P, 3, NB])
        ps_y = psum("ps_y", [P, H, CHUNK])
        ps_out = psum("ps_out", [P, ON, NB])

        def at(i):
            return slice(i * W, (i + 1) * W)

        numerators = ps_m[:, 0:2, 0:2 * W].rearrange("p b (h w) -> p b h w", w=W)
        num = [ps_m[:, h // 2, at(h % 2)] for h in range(H)]
        new = [ps_m[:, 0, at(2)], ps_m[:, 1, at(2)], ps_m[:, 2, at(0)], ps_m[:, 2, at(1)]]

        zeroed = sem("zeroed")
        const_ready = sem("const_ready")
        state_zero = sem("state_zero")
        rows_landed = sem("rows_landed")
        landed = [sem(f"landed{i}") for i in range(2)]
        late_landed = [sem(f"late_landed{i}") for i in range(2)]
        x_landed = [sem(f"x_landed{i}") for i in range(2)]
        diff_ready = sem("diff_ready")
        masked = sem("masked")
        weights_ready = sem("weights_ready")
        win_ready = sem("win_ready")
        qw_ready = sem("qw_ready")
        s_psum = sem("s_psum")
        k_psum = sem("k_psum")
        scores_ready = sem("scores_ready")
        kw_ready = sem("kw_ready")
        products_done = sem("products_done")
        negative_ready = sem("negative_ready")
        den_ready = sem("den_ready")
        inv_ready = sem("inv_ready")
        hidden_ready = sem("hidden_ready")
        state_ready = sem("state_ready")
        stats_ready = sem("stats_ready")
        stats_seen = sem("stats_seen")
        moments_ready = sem("moments_ready")
        log_ready = sem("log_ready")
        rstd_ready = sem("rstd_ready")
        normed_ready = sem("normed_ready")
        y_psum = sem("y_psum")
        y_ready = sem("y_ready")
        yhi_ready = sem("yhi_ready")
        y_split = sem("y_split")
        w_hi_ready = sem("w_hi_ready")
        w_ready = sem("w_ready")
        projected = sem("projected")
        out_taken = sem("out_taken")
        added = sem("added")
        stored = [sem(f"stored{i}") for i in range(2)]
        LOADS, LATE_LOADS, ROW_LOADS = 5, 2, 3

        block = ctx.enter_context(nc.Block())

        @block.sync
        def _(sp):
            def tile_rows(first, c):
                return scratch["arrays"][first * P:(first + H) * P, bass.ds(c * CHUNK, CHUNK)].rearrange(
                    "(h p) t -> p h t", p=P)

            def load(par, c):
                for buf, src in ((k_in[:, par], tile_rows(A_MK, c)), (q_in[:, par], tile_rows(A_MQ, c)),
                                 (g_max[:, par], scratch["m_G"][:, bass.ds(c * CHUNK, CHUNK)].unsqueeze(0).broadcast_to(
                                     [P, H, CHUNK])),
                                 (v_in[:, par, :, 0:M_DH], tile_rows(A_MV, c)), (o_in[:, par], tile_rows(A_MO, c))):
                    sp.dma_start(buf, src).then_inc(landed[par], 16)

            def load_late(par, c):
                sp.dma_start(z_in[:, par], tile_rows(A_MZ, c)).then_inc(late_landed[par], 16)
                sp.dma_start(y[:, par, H:KT, :], scratch["yT"][:, bass.ds(c * CHUNK, CHUNK)].rearrange(
                    "(k p) t -> p k t", p=P)).then_inc(late_landed[par], 16)

            def load_x(par, c):
                sp.dma_start(x_in[:, par, :], a["x"][0, bass.ds(c * CHUNK, CHUNK), :]).then_inc(x_landed[par], 16)

            def store(par, c):
                sp.wait_ge(added, c + 3)
                sp.dma_start(out[0, bass.ds(c * CHUNK, CHUNK), :], result[:, par, :]).then_inc(stored[par], 16)

            for row, buf in (("m_decay", decay), ("m_prev", m_prev)):
                sp.dma_start(buf[:, :, :], scratch[row].unsqueeze(0).broadcast_to([P, H, CHUNKS])
                             ).then_inc(rows_landed, 16)
            load(0, 0)
            load(1, 1)
            load_late(0, 0)
            sp.dma_start(gate[:, :], scratch["gate"]).then_inc(rows_landed, 16)
            load_late(1, 1)
            for par in range(2):
                load_x(par, par)

            def reload(par, c):
                sp.wait_ge(state_ready, c)
                sp.wait_ge(hidden_ready, c)
                load(par, c)
                sp.wait_ge(y_split, c - 1)
                load_late(par, c)

            reload(0, 2)
            with sp.Fori(0, CHUNKS // 2 - 2) as n:
                for par in range(2):
                    reload(1 - par, n * 2 + par + 3)
                    store(par, n * 2 + par)
                    load_x(par, n * 2 + par + 2)
            reload(1, CHUNKS - 1)
            for par in range(2):
                store(par, CHUNKS - 4 + par)
                load_x(par, CHUNKS - 2 + par)
            for par in range(2):
                store(par, CHUNKS - 2 + par)
            for par in range(2):
                sp.wait_ge(stored[par], 16 + CHUNKS // 2 * 16)

        @block.gpsimd
        def _(pool):
            pool.memset(ident[:, :], 0.0).then_inc(zeroed, 1)
            pool.memset(future[:, :], 0.0).then_inc(zeroed, 1)
            pool.memset(v_in[:, :, :, M_DH:W], 1.0).then_inc(const_ready, 1)
            pool.wait_ge(zeroed, 2)
            pool.affine_select(out=ident[:, :], in_=ident[:, :], compare_op=ALU.not_equal, fill=1.0, base=0,
                               pattern=[[-1, P]], channel_multiplier=1).then_inc(const_ready, 1)
            pool.affine_select(out=future[:, :], in_=future[:, :], compare_op=ALU.is_ge, fill=MASKED, base=0,
                               pattern=[[1, CHUNK]], channel_multiplier=-1).then_inc(const_ready, 1)
            for par in range(2):
                pool.sem_inc(stored[par], 16)

            def weigh(par, c):
                pool.wait_ge(win_ready, c + 1)
                pool.tensor_tensor(out=q_w[:, par], in0=q_in[:, par], in1=w_in[:, par], op=ALU.mult
                                   ).then_inc(qw_ready, 1)

            def add(par, n, c):
                pool.wait_ge(out_taken, c + 2)
                pool.wait_ge(x_landed[par], (n + 1) * 16)
                pool.wait_ge(stored[par], (n + 1) * 16)
                pool.tensor_tensor(out=result[:, par, :], in0=update[:, par, :], in1=x_in[:, par, :], op=ALU.add
                                   ).then_inc(added, 1)

            weigh(0, 0)
            weigh(1, 1)
            with pool.Fori(0, CHUNKS // 2 - 1) as n:
                for par in range(2):
                    weigh(par, n * 2 + par + 2)
                    add(par, n, n * 2 + par)
            for par in range(2):
                add(par, CHUNKS // 2 - 1, CHUNKS - 2 + par)

        @block.tensor
        def _(pe):
            pe.wait_ge(const_ready, 3)
            pe.wait_ge(state_zero, 1)

            def score(par, n):
                pe.wait_ge(landed[par], (n + 1) * LOADS * 16)
                for h in range(H):
                    ins = pe.matmul(ps_s[:, h, :], k_in[:, par, h, :], q_in[:, par, h, :], start=True, stop=True)
                ins.then_inc(s_psum, 1)
                for h in range(H):
                    ins = pe.transpose(ps_k[:, h, :], k_in[:, par, h, :], ident[:, :])
                ins.then_inc(k_psum, 1)

            def products(par, c):
                pe.wait_ge(scores_ready, c + 1)
                pe.wait_ge(qw_ready, c + 1)
                pe.wait_ge(hidden_ready, c + 1)
                pe.wait_ge(state_ready, c + 1)
                for h in range(H):
                    pe.matmul(num[h], scores[:, h, :], v_in[:, par, h, :], start=True, stop=False)
                    pe.matmul(num[h], q_w[:, par, h, :], state[:, par, h, :], start=False, stop=True)
                pe.wait_ge(kw_ready, c + 1)
                for h in range(H):
                    ins = pe.matmul(new[h], k_w[:, h, :], v_in[:, par, h, :], start=True, stop=True)
                ins.then_inc(products_done, 1)

            def turn(c):
                pe.wait_ge(normed_ready, c + 1)
                for h in range(H):
                    ins = pe.transpose(ps_y[:, h, :], normed[:, h, :], ident[:, :])
                ins.then_inc(y_psum, 1)

            def project(par, c, between):
                pe.wait_ge(y_split, c + 1)
                pe.wait_ge(out_taken, c + 1)
                for k in range(KT):
                    for part, w in ((y_hi, w_hi), (y_hi, w_lo), (y_lo, w_hi)):
                        for b in range(ON):
                            ins = pe.matmul(ps_out[:, b, :], part[:, par, k, :], w[:, k, b * NB:(b + 1) * NB],
                                            start=(k == 0 and part is y_hi and w is w_hi),
                                            stop=(k == KT - 1 and part is y_lo))
                    if k == KT - 1:
                        ins.then_inc(projected, 1)
                    if k in between:
                        between[k]()

            score(0, 0)
            products(0, 0)
            score(1, 0)
            turn(0)
            pe.wait_ge(w_ready, KT)
            with pe.Fori(0, CHUNKS // 2 - 1) as n:
                for par in (1, 0):
                    c = n * 2 + 2 - par
                    products(par, c)
                    project(1 - par, c - 1, {1: lambda: score(1 - par, n + 1), 5: lambda: turn(c)})
            products(1, CHUNKS - 1)
            project(0, CHUNKS - 2, {5: lambda: turn(CHUNKS - 1)})
            project(1, CHUNKS - 1, {})

        @block.vector
        def _(dve):
            dve.memset(state[:, 0], 0.0).then_inc(state_zero, 1)
            dve.sem_inc(hidden_ready, 1)
            dve.sem_inc(state_ready, 1)
            dve.sem_inc(out_taken, 1)
            dve.sem_inc(added, 2)
            for k in range(KT):
                dve.wait_ge(w_hi_ready, k + 1)
                dve.tensor_sub(w_lo[:, k, :], w_land[:, k, :], w_hi[:, k, :].bitcast(F32)).then_inc(w_ready, 1)
            dve.wait_ge(const_ready, 3)
            dve.wait_ge(rows_landed, ROW_LOADS * 16)

            def prepare(par, n, c):
                dve.wait_ge(landed[par], (n + 1) * LOADS * 16)
                cols = keep["gate_cols"][:, bass.ds(c, 1), :]
                g_col = cols[:, 0, COL_G:COL_G + H].unsqueeze(2).broadcast_to([P, H, CHUNK])
                dve.tensor_sub(diff[:, par], g_col, g_max[:, par]).then_inc(diff_ready, 1)
                dve.wait_ge(diff_ready, c + 1)
                dve.scalar_tensor_tensor(out=diff[:, par], in0=diff[:, par], scalar=0.0,
                                         in1=future[:, :].unsqueeze(1).broadcast_to([P, H, CHUNK]),
                                         op0=ALU.min, op1=ALU.add).then_inc(masked, 1)
                dve.wait_ge(k_psum, c + 1)
                ws_col = cols[:, 0, COL_WS:COL_WS + H].unsqueeze(2).broadcast_to([P, H, CHUNK])
                dve.tensor_mul(k_w[:, :, :], ps_k[:, :, :], ws_col).then_inc(kw_ready, 1)
                dve.wait_ge(weights_ready, c + 1)
                dve.wait_ge(s_psum, c + 1)
                dve.tensor_mul(scores[:, :, :], ps_s[:, :, :], diff[:, par]).then_inc(scores_ready, 1)

            def divide(par, c):
                em = keep["gate_cols"][:, bass.ds(c, 1), :][:, 0, COL_EM:COL_EM + H].rearrange("p (b h) -> p b h", b=2)
                bound = den[:, 0, :].rearrange("p (b h) -> p b h", b=2)
                dve.wait_ge(products_done, c + 1)
                dve.scalar_tensor_tensor(out=bound, in0=numerators[:, :, :, M_DH], scalar=-1.0, in1=em,
                                         op0=ALU.mult, op1=ALU.max).then_inc(negative_ready, 1)
                dve.wait_ge(negative_ready, c + 1)
                dve.tensor_max(bound, numerators[:, :, :, M_DH], bound).then_inc(den_ready, 1)
                dve.wait_ge(den_ready, c + 1)
                dve.reciprocal(den[:, 1, :], den[:, 0, :]).then_inc(inv_ready, 1)
                dve.wait_ge(inv_ready, c + 1)
                for h in range(H):
                    ins = dve.scalar_tensor_tensor(out=gated[:, h, :], in0=num[h][:, 0:M_DH],
                                                   scalar=den[:, 1, h:h + 1], in1=o_in[:, par, h, :],
                                                   op0=ALU.mult, op1=ALU.mult)
                ins.then_inc(hidden_ready, 1)

            def carry(par, c):
                for h in range(H):
                    ins = dve.scalar_tensor_tensor(out=state[:, 1 - par, h, :], in0=state[:, par, h, :],
                                                   scalar=decay[:, h, bass.ds(c, 1)],
                                                   in1=new[h], op0=ALU.mult, op1=ALU.add)
                ins.then_inc(state_ready, 1)

            def moments_of(c):
                dve.wait_ge(hidden_ready, c + 2)
                for h in range(H):
                    ins = dve.bn_stats(stats[:, h, :], gated[:, h, :])
                ins.then_inc(stats_ready, 1)
                dve.wait_ge(stats_ready, c + 1)
                dve.sem_inc(stats_seen, 1)
                for h in range(H):
                    ins = dve.bn_aggr(moments[:, h, :], stats[:, h, :])
                ins.then_inc(moments_ready, 1)

            def output(par, n, c):
                dve.wait_ge(rstd_ready, c + 1)
                for h in range(H):
                    ins = dve.tensor_scalar(normed[:, h, :], gated[:, h, :], moments[:, h, 0:1], rstd[:, h:h + 1],
                                            ALU.subtract, ALU.mult)
                ins.then_inc(normed_ready, 1)
                dve.wait_ge(y_psum, c + 1)
                dve.wait_ge(late_landed[par], (n + 1) * LATE_LOADS * 16)
                for h in range(H):
                    ins = dve.scalar_tensor_tensor(out=y[:, par, h, :], in0=ps_y[:, h, :],
                                                   scalar=keep["params"][:, NORM_GAIN + h:NORM_GAIN + h + 1],
                                                   in1=z_in[:, par, h, :], op0=ALU.mult, op1=ALU.mult)
                ins.then_inc(y_ready, 1)
                dve.wait_ge(yhi_ready, c + 1)
                dve.tensor_sub(y_lo[:, par], y[:, par], y_hi[:, par].bitcast(F32)).then_inc(y_split, 1)

            def residual(par, c):
                dve.wait_ge(projected, c + 1)
                dve.wait_ge(added, c + 1)
                dve.tensor_mul(update[:, par, :], ps_out[:, :, :].rearrange("p b n -> p (b n)"), gate[:, :]
                               ).then_inc(out_taken, 1)

            def chunk(par, c, n, following):
                divide(par, c)
                carry(par, c)
                moments_of(c)
                if following:
                    prepare(1 - par, *following)
                output(par, n, c)

            prepare(0, 0, 0)
            chunk(0, 0, 0, (0, 1))
            with dve.Fori(0, CHUNKS // 2 - 1) as n:
                for par in (1, 0):
                    c = n * 2 + 2 - par
                    chunk(par, c, n + 1 - par, (n + 1, c + 1))
                    residual(1 - par, c - 1)
            chunk(1, CHUNKS - 1, CHUNKS // 2 - 1, None)
            residual(0, CHUNKS - 2)
            residual(1, CHUNKS - 1)

        @block.scalar
        def _(act):
            act.preload_act_table_set("natural_log_exp_and_others")
            for k in range(KT):
                act.activation(w_hi[:, k, :], w_land[:, k, :], ACT.Copy).then_inc(w_hi_ready, 1)
            act.wait_ge(rows_landed, ROW_LOADS * 16)

            def carried_weight(par, n, c):
                act.wait_ge(landed[par], (n + 1) * LOADS * 16)
                for h in range(H):
                    ins = act.activation(w_in[:, par, h, :], g_max[:, par, h, :], ACT.Exp,
                                         bias=m_prev[:, h, bass.ds(c, 1)], scale=-1.0)
                ins.then_inc(win_ready, 1)

            def weights(par, c):
                act.wait_ge(masked, c + 1)
                act.activation(diff[:, par], diff[:, par], ACT.Exp).then_inc(weights_ready, 1)

            def root(c):
                act.wait_ge(moments_ready, c + 1)
                act.activation(rstd[:, :], moments[:, :, 1], ACT.Ln, bias=keep["eps"][:, 0:1]).then_inc(log_ready, 1)
                act.wait_ge(log_ready, c + 1)
                act.activation(rstd[:, :], rstd[:, :], ACT.Exp, scale=-0.5).then_inc(rstd_ready, 1)

            def high(par, n, c):
                act.wait_ge(y_ready, c + 1)
                act.wait_ge(late_landed[par], (n + 1) * LATE_LOADS * 16)
                act.activation(y_hi[:, par], y[:, par], ACT.Copy).then_inc(yhi_ready, 1)

            carried_weight(0, 0, 0)
            weights(0, 0)
            carried_weight(1, 0, 1)
            root(0)
            weights(1, 1)
            high(0, 0, 0)
            with act.Fori(0, CHUNKS // 2 - 1) as n:
                for par in (1, 0):
                    c = n * 2 + 2 - par
                    carried_weight(1 - par, n + 1, c + 1)
                    root(c)
                    weights(1 - par, c + 1)
                    high(par, n + 1 - par, c)
            root(CHUNKS - 1)
            high(1, CHUNKS // 2 - 1, CHUNKS - 1)


_INS = ["x", "c", "norm_g", "w_ada", "b_ada", "w_in", "conv_w", "conv_b", "b_igate", "b_fgate_m",
        "mlstm_norm_g", "b_fgate_f", "fox_qnorm_g", "fox_knorm_g", "w_out"]


def layer(nc, a, out):
    def dram(name, shape):
        return nc.dram_tensor("scratch_" + name, shape, F32).ap()

    scratch = {
        "gate": dram("gate", (P, D_MODEL)),
        "gate_rows": dram("gate_rows", (ROW_FF + F_HEADS, SEQ)),
        "qkT": dram("qkT", (2, 2 * F_W, SEQ)),
        "arrays": dram("arrays", (7 * M_W, SEQ)),
        "f_negF": dram("f_negF", (F_HEADS, SEQ)),
        "m_G": dram("m_G", (M_HEADS, SEQ)),
        "m_prev": dram("m_prev", (M_HEADS, CHUNKS)),
        "m_decay": dram("m_decay", (M_HEADS, CHUNKS)),
        "yT": dram("yT", (F_W, SEQ)),
    }
    with ExitStack() as ctx:
        keep = {
            "params": ctx.enter_context(nc.sbuf_tensor("params", [P, PARAM_ROWS], F32)),
            "gate_cols": ctx.enter_context(nc.sbuf_tensor("gate_cols", [P, CHUNKS, GATE_COLS], F32)),
            "eps": ctx.enter_context(nc.sbuf_tensor("eps", [P, 1], F32)),
            "qk_gain": ctx.enter_context(nc.sbuf_tensor("qk_gain", [P, 2 * M_HEADS], F32)),
        }
        modulate_and_project(nc, a, scratch, keep)
        gate_rows(nc, a, scratch, keep)
        w_land = ctx.enter_context(nc.sbuf_tensor("w_land", [P, KT, D_MODEL], F32))
        forgetting_heads(nc, a, scratch, w_land)
        memory_heads_and_output(nc, a, scratch, keep, w_land, out)


def kernel(**inputs):
    import numpy as _np
    import concourse.bacc as _bacc
    from concourse import mybir as _mybir
    from concourse.bass_utils import run_bass_kernel_spmd as _run

    nc = _bacc.Bacc("TRN2", target_bir_lowering=False, num_devices=1)
    arrays, aps = {}, {}
    for name in _INS:
        arr = _np.ascontiguousarray(inputs[name])
        arrays["in_" + name] = arr
        aps[name] = nc.dram_tensor("in_" + name, arr.shape, _mybir.dt.from_np(arr.dtype), kind="ExternalInput").ap()
    out = nc.dram_tensor("out_0", (1, SEQ, D_MODEL), F32, kind="ExternalOutput").ap()
    layer(nc, aps, out)
    r = _run(nc, [arrays], core_ids=[0])
    return r.results[0]["out_0"]
```

```python
import math
from contextlib import ExitStack

import concourse.bass as bass
from concourse import mybir

F32 = mybir.dt.float32
F32R = mybir.dt.float32r
ALU = mybir.AluOpType
ACT = mybir.ActivationFunctionType
AX_X = mybir.AxisListType.X

P = 128
D_MODEL = 1024
SEQ = 2048
EPS = 1e-6
KT = D_MODEL // P
TT = SEQ // P
NB = 512
TB = SEQ // NB

M_HEADS, M_DH = 4, 128
F_HEADS, F_DH = 8, 64
M_W, F_W = M_HEADS * M_DH, F_HEADS * F_DH
CONV_K = 4

M_GATES = 5 * M_W
F_Q = M_GATES + 2 * M_HEADS
F_GATES = F_Q + 4 * F_W
D_IN = F_GATES + F_HEADS
M_TILES = 5 * M_W // P
F_TILES = 4 * F_W // P
U_TILES = M_TILES + F_TILES
HEADS_IN_TILE = P // F_DH
PARAM_ROWS = (CONV_K + 1) * 2 * M_HEADS + 2 + M_HEADS
CHUNK = 128
CHUNKS = SEQ // CHUNK
A_FV, A_MV, A_MO, A_MQ, A_MK, A_MZ, A_FZ = (i * M_HEADS for i in range(7))
COL_G, COL_WS, COL_EM = range(3)
NORM_GAIN = (CONV_K + 1) * 2 * M_HEADS + 2
EXP_MAX = 88.0
MASKED = -1e30
ROW_I, ROW_F, ROW_FF = 0, 32, 64
ROW_LOW = 16
GATE_ROWS = ROW_FF + ROW_LOW + F_HEADS


def modulate_and_project(nc, a, scratch, keep):
    with ExitStack() as ctx:
        def sb(name, shape, dt=F32):
            return ctx.enter_context(nc.sbuf_tensor("a_" + name, shape, dt))

        def sem(name):
            return ctx.enter_context(nc.semaphore("a_" + name))

        UN = 4
        WP = 256
        AR = 4
        PIECES = 3 * D_MODEL // WP
        ROW_PIECES = 2 * D_MODEL // WP
        HALF = NB // WP
        T_SLOTS = 2
        params, qk_gain = keep["params"], keep["qk_gain"]
        h_hi = sb("h_hi", [P, KT, SEQ], F32R)
        h_lo = sb("h_lo", [P, KT, SEQ], F32R)
        ident = sb("ident", [P, P])
        head_mean = sb("head_mean", [P, HEADS_IN_TILE])
        par_rows = sb("par_rows", [PARAM_ROWS, P])
        gate_bias = sb("gate_bias", [GATE_ROWS, 1])
        w_land = sb("w_land", [P, 2, KT, P])
        wg_land = sb("wg_land", [P, KT, 2 * M_HEADS + F_HEADS])
        w_view = a["w_in"][0].rearrange("(k p) n -> p k n", p=P)
        param_landed = sem("param_landed")

        with ExitStack() as early:
            def esb(name, shape, dt=F32):
                return early.enter_context(nc.sbuf_tensor("a0_" + name, shape, dt))

            x_ring = esb("x_ring", [P, UN, D_MODEL])
            w_ring = esb("w_ring", [P, AR, KT, WP])
            mod = esb("mod", [P, 2, D_MODEL])
            gain = esb("gain", [P, D_MODEL])
            c_rows = esb("c_rows", [KT, P])
            c_cols = esb("c_cols", [P, KT])
            c_wide = esb("c_wide", [P, KT, P])
            sumsq = esb("sumsq", [P, TT])
            rms = esb("rms", [P, TT])
            rstd = esb("rstd", [P, TT])
            junk = esb("junk", [P, D_MODEL])
            ps_t = early.enter_context(nc.psum_tensor("a0_ps_t", [P, T_SLOTS, KT, P], F32))
            ps_v = early.enter_context(nc.psum_tensor("a0_ps_v", [P, NB], F32))
            ps_m = early.enter_context(nc.psum_tensor("a0_ps_m", [P, 2, NB], F32))

            c_landed = sem("c_landed")
            rows_landed = sem("rows_landed")
            gate_row_landed = sem("gate_row_landed")
            x_landed = [sem(f"x_landed{u}") for u in range(UN)]
            w_landed = [sem(f"w_landed{u}") for u in range(AR)]
            prefetched = sem("prefetched")
            w_used = sem("w_used")
            zeroed = sem("zeroed")
            eps_ready = sem("eps_ready")
            ident_ready = sem("ident_ready")
            c_transposed = sem("c_transposed")
            c_ready = sem("c_ready")
            c_wide_ready = sem("c_wide_ready")
            mod_ready = sem("mod_ready")
            gain_done = sem("gain_done")
            gate_stored = sem("gate_stored")
            sumsq_ready = sem("sumsq_ready")
            rms_ready = sem("rms_ready")
            rstd_ready = sem("rstd_ready")
            x_scaled = sem("x_scaled")
            x_shifted = sem("x_shifted")
            xt_psum = sem("xt_psum")
            h_hi_ready = sem("h_hi_ready")
            split_done = sem("split_done")

            block = early.enter_context(nc.Block())

            @block.sync
            def _(sp):
                ada_view = a["w_ada"][0].rearrange("(k p) n -> p k n", p=P)

                def load_piece(u, q):
                    sp.dma_start(w_ring[:, u], ada_view[:, :, bass.ds(q * WP, WP)]).then_inc(w_landed[u], 16)

                def load_x(u, t):
                    sp.dma_start(x_ring[:, u, :], a["x"][0, bass.ds(t * P, P), :]).then_inc(x_landed[u], 16)

                sp.dma_start(c_rows[:, :], a["c"].rearrange("b (k p) -> (b k) p", p=P)).then_inc(c_landed, 16)
                for u in range(AR):
                    load_piece(u, u)

                def reload_piece(u, q):
                    sp.wait_ge(w_used, q - AR + 1)
                    load_piece(u, q)

                def load_row(buf, row, landed):
                    sp.dma_start(buf, row.broadcast_to([P, D_MODEL])).then_inc(landed, 16)

                load_row(mod[:, 0, :], a["b_ada"][0:1, 0:D_MODEL], rows_landed)
                reload_piece(0, AR)
                load_row(mod[:, 1, :], a["b_ada"][0:1, D_MODEL:2 * D_MODEL], rows_landed)
                reload_piece(1, AR + 1)
                load_row(gain[:, :], a["norm_g"][0:1, :], rows_landed)
                reload_piece(2, AR + 2)
                load_x(0, 0)
                reload_piece(3, AR + 3)
                load_x(1, 1)
                reload_piece(0, 2 * AR)
                load_x(2, 2)
                reload_piece(1, 2 * AR + 1)
                load_x(3, 3)
                for u in range(2, AR):
                    reload_piece(u, 2 * AR + u)
                sp.wait_ge(gain_done, 1)
                load_row(mod[:, 1, :], a["b_ada"][0:1, 2 * D_MODEL:], gate_row_landed)
                with sp.Fori(0, TT // UN - 1) as n:
                    for u in range(UN):
                        sp.wait_ge(xt_psum, n * UN + u + 1)
                        load_x(u, n * UN + u + UN)
                sp.dma_start(wg_land[:, :, 0:2 * M_HEADS], w_view[:, :, M_GATES:F_Q]).then_inc(prefetched, 16)
                sp.dma_start(wg_land[:, :, 2 * M_HEADS:], w_view[:, :, F_GATES:D_IN]).then_inc(prefetched, 16)
                for par in range(2):
                    sp.dma_start(w_land[:, par], w_view[:, :, F_Q + par * P:F_Q + (par + 1) * P]).then_inc(prefetched, 16)
                sp.wait_ge(mod_ready, 6)
                sp.dma_start(scratch["gate"], mod[:, 1, :]).then_inc(gate_stored, 16)
                sp.wait_ge(gate_stored, 16)
                sp.wait_ge(prefetched, 64)

            @block.gpsimd
            def _(pool):
                pool.memset(ident[:, :], 0.0).then_inc(zeroed, 1)
                pool.memset(head_mean[:, :], 0.0).then_inc(zeroed, 1)
                pool.memset(gate_bias[:, :], 0.0).then_inc(zeroed, 1)
                pool.wait_ge(zeroed, 3)
                pool.affine_select(out=ident[:, :], in_=ident[:, :], compare_op=ALU.not_equal, fill=1.0, base=0,
                                   pattern=[[-1, P]], channel_multiplier=1).then_inc(ident_ready, 1)
                for h in range(HEADS_IN_TILE):
                    part = slice(h * F_DH, (h + 1) * F_DH)
                    pool.wait_ge(ident_ready, h + 1)
                    pool.memset(head_mean[part, h:h + 1], 1.0 / F_DH).then_inc(ident_ready, 1)
                pool.dma_start(par_rows[0:32, :], a["conv_w"][0].rearrange("k (j p) -> (k j) p", p=P)).then_inc(param_landed, 16)
                pool.dma_start(par_rows[32:40, :], a["conv_b"].rearrange("b (j p) -> (b j) p", p=P)).then_inc(param_landed, 16)
                for h in range(HEADS_IN_TILE):
                    part = slice(h * F_DH, (h + 1) * F_DH)
                    pool.dma_start(par_rows[40:41, part], a["fox_qnorm_g"][:, :]).then_inc(param_landed, 16)
                    pool.dma_start(par_rows[41:42, part], a["fox_knorm_g"][:, :]).then_inc(param_landed, 16)
                pool.dma_start(par_rows[42:46, :],
                               a["mlstm_norm_g"].rearrange("b (j p) -> (b j) p", p=P)).then_inc(param_landed, 16)
                for row, heads, name in ((ROW_I, M_HEADS, "b_igate"), (ROW_F, M_HEADS, "b_fgate_m"),
                                         (ROW_FF, F_HEADS, "b_fgate_f")):
                    pool.dma_start(gate_bias[row:row + heads, :], a[name].rearrange("b h -> h b")).then_inc(param_landed, 16)
                pool.wait_ge(ident_ready, 1 + HEADS_IN_TILE)
                pool.wait_ge(mod_ready, 2)
                with pool.Fori(0, TT // UN) as n:
                    for u in range(UN):
                        pool.wait_ge(x_scaled, n * UN + u + 1)
                        pool.tensor_tensor(out=x_ring[:, u, :], in0=x_ring[:, u, :], in1=mod[:, 0, :], op=ALU.add
                                           ).then_inc(x_shifted, 1)
                pool.wait_ge(param_landed, 10 * 16)

            @block.scalar
            def _(act):
                act.preload_act_table(ACT.Sqrt)
                act.wait_ge(eps_ready, 1)

                def root_mean_square(n, u, t):
                    act.wait_ge(x_landed[u], (n + 1) * 16)
                    act.activation(junk[:, :], x_ring[:, u, :], ACT.Square,
                                   accum_out=sumsq[:, bass.ds(t, 1)]).then_inc(sumsq_ready, 1)
                    act.wait_ge(sumsq_ready, t + 1)
                    act.activation(rms[:, bass.ds(t, 1)], sumsq[:, bass.ds(t, 1)], ACT.Sqrt,
                                   bias=keep["eps"][:, 0:1], scale=1.0 / D_MODEL).then_inc(rms_ready, 1)

                def high(u, t):
                    act.wait_ge(xt_psum, t + 1)
                    act.activation(h_hi[:, :, bass.ds(t * P, P)], ps_t[:, u % 2], ACT.Copy).then_inc(h_hi_ready, 1)

                for t in range(3):
                    root_mean_square(0, t, t)
                with act.Fori(0, TT // UN - 1) as n:
                    for u in range(UN):
                        high(u, n * UN + u)
                        root_mean_square(n + (u + 3) // UN, (u + 3) % UN, n * UN + u + 3)
                for u in range(UN):
                    high(u, TT - UN + u)
                    if u + 3 < UN:
                        root_mean_square(TT // UN - 1, u + 3, TT - UN + u + 3)

            @block.vector
            def _(dve):
                dve.memset(keep["eps"][:, :], EPS).then_inc(eps_ready, 1)
                dve.sem_inc(split_done, T_SLOTS)
                dve.wait_ge(c_transposed, 1)
                dve.tensor_copy(c_cols[:, :], ps_v[:, 0:KT]).then_inc(c_ready, 1)
                dve.wait_ge(c_ready, 1)
                dve.tensor_copy(c_wide[:, :, :], c_cols[:, :].unsqueeze(2).broadcast_to([P, KT, P])
                                ).then_inc(c_wide_ready, 1)

                def add_bias(i):
                    dve.wait_ge(w_used, (i + 1) * HALF)
                    part = mod[:, min(i // 2, 1), (i % 2) * NB:(i % 2 + 1) * NB]
                    dve.tensor_add(part, ps_m[:, i % 2, :], part).then_inc(mod_ready, 1)

                def scale(u, t):
                    dve.wait_ge(rms_ready, t + 1)
                    dve.reciprocal(rstd[:, bass.ds(t, 1)], rms[:, bass.ds(t, 1)]).then_inc(rstd_ready, 1)
                    dve.wait_ge(rstd_ready, t + 1)
                    dve.scalar_tensor_tensor(out=x_ring[:, u, :], in0=x_ring[:, u, :], scalar=rstd[:, bass.ds(t, 1)],
                                             in1=gain[:, :], op0=ALU.mult, op1=ALU.mult).then_inc(x_scaled, 1)

                def low(u, t):
                    dve.wait_ge(h_hi_ready, t + 1)
                    dve.tensor_sub(h_lo[:, :, bass.ds(t * P, P)], ps_t[:, u % 2],
                                   h_hi[:, :, bass.ds(t * P, P)].bitcast(F32)).then_inc(split_done, 1)

                dve.wait_ge(rows_landed, 48)
                for i in range(4):
                    add_bias(i)
                dve.wait_ge(mod_ready, 4)
                dve.scalar_tensor_tensor(out=gain[:, :], in0=mod[:, 1, :], scalar=1.0, in1=gain[:, :],
                                         op0=ALU.add, op1=ALU.mult).then_inc(gain_done, 1)
                dve.wait_ge(gain_done, 1)
                scale(0, 0)
                scale(1, 1)
                dve.wait_ge(gate_row_landed, 16)
                with dve.Fori(0, TT // UN - 1) as n:
                    for u in range(UN):
                        scale((u + 2) % UN, n * UN + u + 2)
                        low(u, n * UN + u)
                for u in range(UN):
                    if u < 2:
                        scale(u + 2, TT - UN + u + 2)
                        add_bias(4 + u)
                    low(u, TT - UN + u)

            @block.tensor
            def _(pe):
                pe.wait_ge(c_landed, 16)
                pe.wait_ge(ident_ready, 1)
                pe.transpose(ps_v[:, 0:KT], c_rows[:, :], ident[0:KT, 0:KT]).then_inc(c_transposed, 1)
                pe.wait_ge(c_wide_ready, 1)

                def multiply(q, ks):
                    if ks[0] == 0:
                        pe.wait_ge(w_landed[q % AR], (q // AR + 1) * 16)
                        if q % HALF == 0 and q >= 2 * HALF:
                            pe.wait_ge(mod_ready, q // HALF - 1)
                    for k in ks:
                        ins = pe.matmul(ps_m[:, q // HALF % 2, q % HALF * WP:(q % HALF + 1) * WP], c_wide[:, k, :],
                                        w_ring[:, q % AR, k, :], start=(k == 0), stop=(k == KT - 1))
                    if ks[-1] == KT - 1:
                        ins.then_inc(w_used, 1)

                def turn(u, t):
                    pe.wait_ge(x_shifted, t + 1)
                    pe.wait_ge(split_done, t + 1)
                    for k in range(KT):
                        ins = pe.transpose(ps_t[:, u % 2, k, :], x_ring[:, u, k * P:(k + 1) * P], ident[:, :])
                    ins.then_inc(xt_psum, 1)

                for q in range(ROW_PIECES):
                    multiply(q, range(KT))
                for t in range(2 * (PIECES - ROW_PIECES)):
                    multiply(ROW_PIECES + t // 2, range(t % 2 * KT // 2, (t % 2 + 1) * KT // 2))
                    turn(t % UN, t)
                with pe.Fori(2 * (PIECES - ROW_PIECES) // UN, TT // UN) as n:
                    for u in range(UN):
                        turn(u, n * UN + u)

        with ExitStack() as late:
            def lsb(name, shape, dt=F32):
                return late.enter_context(nc.sbuf_tensor("a1_" + name, shape, dt))

            w_hi = lsb("w_hi", [P, 2, KT, P], F32R)
            w_lo = lsb("w_lo", [P, 2, KT, P], F32R)
            w_gates = lsb("w_gates", [P, KT, GATE_ROWS], F32R)
            u_copy = lsb("u_copy", [P, 2, SEQ])
            work = lsb("work", [P, SEQ])
            stage = lsb("stage", [P, 2, SEQ])
            inv_rms = lsb("inv_rms", [P, TT * HEADS_IN_TILE])
            ps_u = late.enter_context(nc.psum_tensor("a1_ps_u", [P, 2, TB, NB], F32))

            w_landed = [sem(f"wi_landed{u}") for u in range(2)]
            hi_ready = sem("w_hi_ready")
            w_split = sem("w_split")
            wg_split = sem("wg_split")
            u_psum = sem("u_psum")
            half_free = sem("half_free")
            param_psum = sem("param_psum")
            gain_ready = sem("gain_ready")
            u_copied = sem("u_copied")
            squared = sem("squared")
            means_psum = sem("means_psum")
            spread = sem("spread")
            post_psum = sem("post_psum")
            mean_ready = sem("mean_ready")
            inverse_ready = sem("inverse_ready")
            root_ready = sem("root_ready")
            stage_hi = sem("stage_hi")
            sigmoid_ready = sem("sigmoid_ready")
            conv_started = sem("conv_started")
            tap_done = sem("tap_done")
            finished = sem("finished")
            stored = sem("stored")

            G = M_HEADS
            LOADS = ((2, 3 * G - 2, F_Q + 2 * P), (3 * G, 2 * G, 2 * M_W), (5 * G, 2 * G, 0), (7 * G, G, 4 * M_W),
                     (8 * G, G, F_Q + 3 * F_W))
            NORM, TURN, CONV, SILU = 0, 2 * G, 5 * G, 7 * G
            END = 9 * G
            assert END == U_TILES and G % 2 == 0
            block = late.enter_context(nc.Block())

            @block.sync
            def _(sp):
                for first, count, column in LOADS:
                    with sp.Fori(0, count // 2) as n:
                        for par in range(2):
                            sp.wait_ge(w_split, n * 2 + par + first - 1)
                            sp.dma_start(w_land[:, par],
                                         w_view[:, :, bass.ds((n * 2 + par) * P + column, P)]).then_inc(w_landed[par], 16)

            @block.gpsimd
            def _(pool):
                pool.wait_ge(finished, 1 + 2)
                pool.dma_start(scratch["gate_rows"], stage[0:GATE_ROWS, 0, :]).then_inc(stored, 16)

                def store(out, j, sb_view):
                    pool.wait_ge(finished, j + 4)
                    pool.dma_start(out, sb_view).then_inc(stored, 16)

                with pool.Fori(0, (TURN - NORM)) as n:
                    store(scratch["qkT"][:, bass.ds(n * P, P), :].rearrange("s p c -> p s c"), n + NORM, stage[:, :, :])
                with pool.Fori(0, END - TURN) as n:
                    store(scratch["arrays"][bass.ds(n * P, P), :], n + TURN, stage[:, 0, :])
                pool.wait_ge(stored, (END + 1) * 16)

            @block.vector
            def _(dve):
                dve.sem_inc(finished, 2)

                def split_w(par, n, j):
                    if n is not None:
                        dve.wait_ge(w_landed[par], n * 16)
                    dve.tensor_copy(w_hi[:, par], w_land[:, par]).then_inc(hi_ready, 1)
                    dve.wait_ge(hi_ready, j + 1)
                    dve.tensor_sub(w_lo[:, par], w_land[:, par], w_hi[:, par].bitcast(F32)).then_inc(w_split, 1)

                dve.memset(w_gates[:, :, :].bitcast(F32), 0.0).then_inc(wg_split, 1)
                dve.wait_ge(wg_split, 1)
                for n, (row, first, count) in enumerate(((ROW_I, 0, M_HEADS), (ROW_F, M_HEADS, M_HEADS),
                                                         (ROW_FF, 2 * M_HEADS, F_HEADS))):
                    part = wg_land[:, :, first:first + count]
                    hi = w_gates[:, :, row:row + count]
                    dve.tensor_copy(hi, part).then_inc(wg_split, 1)
                    dve.wait_ge(wg_split, 2 + 2 * n)
                    dve.tensor_sub(w_gates[:, :, row + ROW_LOW:row + ROW_LOW + count], part, hi.bitcast(F32)
                                   ).then_inc(wg_split, 1)
                split_w(0, None, 0)
                split_w(1, None, 1)
                dve.wait_ge(param_psum, 1)
                dve.tensor_copy(params[:, :], ps_u[:, 0, 0, 0:PARAM_ROWS]).then_inc(half_free, 1)
                dve.wait_ge(u_psum, 1)
                dve.tensor_scalar(stage[0:GATE_ROWS, 0, :],
                                  ps_u[0:GATE_ROWS, 1].rearrange("p b n -> p (b n)"), gate_bias[:, 0:1], None,
                                  ALU.add).then_inc(half_free, 1)
                dve.wait_ge(half_free, 2)
                dve.sem_inc(finished, 1)

                def begin(par, n, j, split=True):
                    dve.wait_ge(u_psum, j + 2)
                    if split:
                        split_w(par, n + 1, j + 2)

                def flat(par):
                    return ps_u[:, par].rearrange("p b n -> p (b n)")

                dve.wait_ge(gain_ready, 1)
                with dve.Fori(0, (TURN - NORM) // 2) as n:
                    for par in range(2):
                        j = n * 2 + par
                        begin(par, n, j)
                        dve.wait_ge(means_psum, j + 1)
                        dve.tensor_scalar(inv_rms[:, :], ps_u[:, par, 0, 0:TT * HEADS_IN_TILE], EPS, None,
                                          ALU.add).then_inc(mean_ready, 1)
                        dve.wait_ge(mean_ready, j + 1)
                        dve.reciprocal(inv_rms[:, :], inv_rms[:, :]).then_inc(inverse_ready, 1)
                        dve.wait_ge(root_ready, j + 1)
                        dve.tensor_copy(work[:, :].rearrange("p (t d) -> p t d", d=F_DH),
                                        inv_rms[:, :].unsqueeze(2).broadcast_to([P, TT * HEADS_IN_TILE, F_DH])
                                        ).then_inc(spread, 1)
                        dve.wait_ge(post_psum, j + 1)
                        dve.scalar_tensor_tensor(out=u_copy[:, par, :], in0=u_copy[:, par, :],
                                                 scalar=qk_gain[:, bass.ds(j, 1)], in1=flat(par),
                                                 op0=ALU.mult, op1=ALU.mult).then_inc(half_free, 1)
                        dve.wait_ge(half_free, j + 3)
                        dve.wait_ge(stored, (j + 1) * 16)
                        dve.tensor_copy(stage[:, 0, :].bitcast(F32R), u_copy[:, par, :]).then_inc(stage_hi, 1)
                        dve.wait_ge(stage_hi, j + 1)
                        dve.tensor_sub(stage[:, 1, :].bitcast(F32R), u_copy[:, par, :],
                                       stage[:, 0, :]).then_inc(finished, 1)
                with dve.Fori(0, (CONV - TURN) // 2) as n:
                    for par in range(2):
                        j = n * 2 + par + TURN
                        begin(par, n + TURN // 2, j)
                        dve.wait_ge(post_psum, j + 1)
                        dve.wait_ge(stored, (j + 1) * 16)
                        dve.tensor_copy(stage[:, 0, :], flat(par)).then_inc(finished, 1)
                        dve.wait_ge(finished, j + 4)
                        dve.sem_inc(half_free, 1)
                for kind, factor in ((0, 1.0), (1, float(M_DH) ** -0.5)):
                    with dve.Fori(0, G // 2) as n:
                        for par in range(2):
                            i = n * 2 + par + kind * G
                            j = i + CONV
                            begin(par, n + (CONV + kind * G) // 2, j)
                            dve.wait_ge(conv_started, i + 1)
                            for s in range(1, CONV_K):
                                dve.scalar_tensor_tensor(
                                    out=work[:, s:], in0=u_copy[:, par, 0:SEQ - s],
                                    scalar=params[:, bass.ds(i + (CONV_K - 1 - s) * 2 * G, 1)],
                                    in1=work[:, s:], op0=ALU.mult, op1=ALU.add).then_inc(tap_done, 1)
                                dve.wait_ge(tap_done, i * (CONV_K - 1) + s)
                                if s == 1:
                                    dve.sem_inc(half_free, 1)
                            dve.wait_ge(sigmoid_ready, i + 1)
                            dve.wait_ge(stored, (j + 1) * 16)
                            dve.scalar_tensor_tensor(out=stage[:, 0, :], in0=work[:, :], scalar=factor,
                                                     in1=stage[:, 1, :], op0=ALU.mult, op1=ALU.mult).then_inc(finished, 1)

                def silu(par, n, j, split):
                    begin(par, n, j, split)
                    dve.wait_ge(sigmoid_ready, j - CONV + 1)
                    dve.wait_ge(stored, (j + 1) * 16)
                    dve.tensor_mul(stage[:, 0, :], flat(par), work[:, :]).then_inc(finished, 1)
                    dve.wait_ge(finished, j + 4)
                    dve.sem_inc(half_free, 1)

                with dve.Fori(0, (END - SILU) // 2 - 1) as n:
                    for par in range(2):
                        silu(par, n + SILU // 2, n * 2 + par + SILU, True)
                for par in range(2):
                    silu(par, 0, END - 2 + par, False)

            @block.tensor
            def _(pe):
                def project(par, j, hi, lo, post=()):
                    for k in range(KT):
                        for b in range(TB):
                            cols = slice(b * NB, (b + 1) * NB)
                            pe.matmul(ps_u[:, par, b, :], hi[:, k, :], h_hi[:, k, cols], start=(k == 0), stop=False)
                            pe.matmul(ps_u[:, par, b, :], hi[:, k, :], h_lo[:, k, cols], start=False, stop=False)
                        for b in range(TB):
                            cols = slice(b * NB, (b + 1) * NB)
                            ins = pe.matmul(ps_u[:, par, b, :], lo[:, k, :], h_hi[:, k, cols],
                                            start=False, stop=(k == KT - 1))
                        for at, step in post:
                            if k == at:
                                step(1 - par, j - 1)
                    ins.then_inc(u_psum, 1)

                def tile(par, j, post=()):
                    pe.wait_ge(w_split, j + 1)
                    pe.wait_ge(half_free, j + 1)
                    project(par, j, w_hi[:, par], w_lo[:, par], post)

                def head_means(par, j):
                    pe.wait_ge(squared, j + 1)
                    for t in range(TT):
                        ins = pe.matmul(ps_u[:, par, 0, t * HEADS_IN_TILE:(t + 1) * HEADS_IN_TILE],
                                        work[:, t * P:(t + 1) * P], head_mean[:, :], start=True, stop=True)
                    ins.then_inc(means_psum, 1)

                def turn(par, source):
                    view = ps_u[:, par].rearrange("p b (t n) -> p (b t) n", n=P)
                    for t in range(TT):
                        ins = pe.transpose(view[:, t, :], source[:, t * P:(t + 1) * P], ident[:, :])
                    ins.then_inc(post_psum, 1)

                def turned_norms(par, j):
                    pe.wait_ge(spread, j + 1)
                    turn(par, work)

                def turned(par, j):
                    pe.wait_ge(u_copied, j + 1)
                    turn(par, u_copy[:, par])

                pe.transpose(ps_u[:, 0, 0, 0:PARAM_ROWS], par_rows[:, :],
                             ident[0:PARAM_ROWS, 0:PARAM_ROWS]).then_inc(param_psum, 1)
                pe.wait_ge(wg_split, 7)
                for k in range(KT):
                    for b in range(TB):
                        cols = slice(b * NB, (b + 1) * NB)
                        pe.matmul(ps_u[0:GATE_ROWS, 1, b, :], w_gates[:, k, :], h_hi[:, k, cols], start=(k == 0), stop=False)
                        ins = pe.matmul(ps_u[0:GATE_ROWS, 1, b, :], w_gates[:, k, :], h_lo[:, k, cols],
                                        start=False, stop=(k == KT - 1))
                ins.then_inc(u_psum, 1)
                tile(0, 0)
                with pe.Fori(0, (TURN - NORM) // 2) as n:
                    tile(1, n * 2 + 1, ((2, head_means), (5, turned_norms)))
                    tile(0, n * 2 + 2, ((2, head_means), (5, turned_norms)))
                with pe.Fori(0, (CONV - TURN) // 2) as n:
                    tile(1, n * 2 + 1 + TURN, ((2, turned),))
                    tile(0, n * 2 + 2 + TURN, ((2, turned),))
                with pe.Fori(0, (END - CONV) // 2 - 1) as n:
                    tile(1, n * 2 + 1 + CONV)
                    tile(0, n * 2 + 2 + CONV)
                tile(1, END - 1)

            @block.scalar
            def _(act):
                def copy(par, j, func=ACT.Copy):
                    act.wait_ge(u_psum, j + 2)
                    act.wait_ge(finished, j + 2)
                    return act.activation(u_copy[:, par, :], flat(par), func)

                def flat(par):
                    return ps_u[:, par].rearrange("p b n -> p (b n)")

                act.preload_act_table(ACT.Sqrt)
                act.wait_ge(half_free, 1)
                act.activation(qk_gain[:, 0:G], params[:, 40:41].broadcast_to([P, G]), ACT.Copy,
                               scale=float(F_DH) ** -0.5)
                act.activation(qk_gain[:, G:2 * G], params[:, 41:42].broadcast_to([P, G]), ACT.Copy).then_inc(gain_ready, 1)
                with act.Fori(0, (TURN - NORM) // 2) as n:
                    for par in range(2):
                        j = n * 2 + par
                        copy(par, j).then_inc(u_copied, 1)
                        act.wait_ge(finished, j + 3)
                        act.activation(work[:, :], flat(par), ACT.Square).then_inc(squared, 1)
                        act.wait_ge(inverse_ready, j + 1)
                        act.activation(inv_rms[:, :], inv_rms[:, :], ACT.Sqrt).then_inc(root_ready, 1)
                with act.Fori(0, G) as n:
                    for par in range(2):
                        copy(par, n * 2 + par + TURN).then_inc(u_copied, 1)
                act.preload_act_table(ACT.Sigmoid)
                with act.Fori(0, G // 2) as n:
                    for par in range(2):
                        copy(par, n * 2 + par + TURN + 2 * G, ACT.Sigmoid).then_inc(u_copied, 1)
                with act.Fori(0, G) as n:
                    for par in range(2):
                        i = n * 2 + par
                        copy(par, i + CONV)
                        act.wait_ge(finished, i + CONV + 3)
                        act.activation(work[:, :], flat(par), ACT.Identity,
                                       bias=params[:, bass.ds(i + CONV_K * 2 * G, 1)],
                                       scale=params[:, bass.ds(i + (CONV_K - 1) * 2 * G, 1)]).then_inc(conv_started, 1)
                        act.wait_ge(tap_done, (i + 1) * (CONV_K - 1))
                        act.activation(stage[:, 1, :], work[:, :], ACT.Sigmoid).then_inc(sigmoid_ready, 1)
                with act.Fori(0, (END - SILU) // 2) as n:
                    for par in range(2):
                        j = n * 2 + par + SILU
                        act.wait_ge(u_psum, j + 2)
                        act.wait_ge(finished, j + 3)
                        act.activation(work[:, :], flat(par), ACT.Sigmoid).then_inc(sigmoid_ready, 1)




def load_fox_head(sp, scratch, fox, h, row, half):
    cols = slice(half * SEQ // 2, (half + 1) * SEQ // 2)
    for part in range(2):
        rows = slice(part * F_DH, (part + 1) * F_DH)
        for name, source, first in (("q_pack", part, row), ("k_hi2", 0, row + F_W), ("k_lo2", 1, row + F_W)):
            sp.dma_start(fox[name][rows, h, cols].bitcast(F32), scratch["qkT"][source, bass.ds(first, F_DH), cols]
                         ).then_inc(fox["head_landed"][h][half], 16)


def load_fox_v(sp, scratch, fox, half, pair):
    cols = slice(half * SEQ // 2, (half + 1) * SEQ // 2)
    sp.dma_start(fox["v_tok"][:, :, :, :].rearrange("p t h d -> p (t h d)")[:, cols],
                 scratch["arrays"][bass.ds(pair * P + A_FV * P, P), cols]).then_inc(fox["v_landed"][half], 16)


def load_fox_z(sp, scratch, fox, pair):
    sp.dma_start(fox["gate_z"][:, :], scratch["arrays"][bass.ds(pair * P + A_FZ * P, P), :]
                 ).then_inc(fox["z_landed"], 16)


def gate_rows(nc, a, scratch, keep, fox):
    with ExitStack() as ctx:
        def sb(name, shape):
            return ctx.enter_context(nc.sbuf_tensor("g_" + name, shape, F32))

        def sem(name):
            return ctx.enter_context(nc.semaphore("g_" + name))

        HC = M_HEADS * CHUNKS
        assert F_HEADS * CHUNKS == P and CHUNK == P
        FF, F, I = range(3)
        pre = sb("pre", [P, 3, CHUNK])
        pre_low = sb("pre_low", [P, 3, CHUNK])
        log_f = sb("log_f", [P, 2, CHUNK])
        ones = sb("ones", [P, CHUNK])
        zeros = sb("zeros", [HC, CHUNK])
        neg_sum = sb("neg_sum", [P, CHUNK])
        neg_before = sb("neg_before", [P, 1])
        neg_all = sb("neg_all", [P, CHUNK])
        before = sb("before", [P, F_HEADS, CHUNKS])
        b_sum = sb("b_sum", [HC, CHUNK])
        g_local = sb("g_local", [HC, CHUNK])
        g_max = sb("g_max", [HC, CHUNK])
        ends = sb("ends", [HC, 2])
        end_rows = sb("end_rows", [1, 2, HC])
        m_next = sb("m_next", [1, M_HEADS, CHUNKS + 1])
        m_prev = sb("m_prev", [1, HC])
        decay = sb("decay", [1, HC])
        m_col = sb("m_col", [HC, 1])
        to_turn = sb("to_turn", [HC, 3, CHUNK])
        ident = sb("ident", [P, P])
        ps_before = ctx.enter_context(nc.psum_tensor("g_ps_before", [P, NB], F32))
        ps_ends = ctx.enter_context(nc.psum_tensor("g_ps_ends", [P, NB], F32))
        ps_m = ctx.enter_context(nc.psum_tensor("g_ps_m", [P, NB], F32))
        ps_cols = ctx.enter_context(nc.psum_tensor("g_ps_cols", [P, NB], F32))

        landed = sem("landed")
        cleared = sem("cleared")
        filled = sem("filled")
        selected = sem("selected")
        step = {name: sem(name) for name in (
            "added", "magnitude", "exp_neg", "log1p", "log_ready", "neg_sum_ready", "before_psum", "before_ready",
            "neg_all_ready", "b_ready", "g_ready", "local_ready", "ends_ready", "ends_psum", "end_rows_ready",
            "m_next_ready", "m_prev_ready", "last_ready", "decay_log", "m_psum", "m_col_ready", "g_max_ready",
            "m_sum", "exponents", "exponentials", "turned", "stored")}

        block = ctx.enter_context(nc.Block())

        @block.sync
        def _(sp):
            sp.wait_ge(cleared, 2)
            for kind, row, heads in ((FF, ROW_FF, F_HEADS), (F, ROW_F, M_HEADS), (I, ROW_I, M_HEADS)):
                for buf, first in ((pre, row), (pre_low, row + ROW_LOW)):
                    sp.dma_start(buf[0:heads * CHUNKS, kind, :], scratch["gate_rows"][first:first + heads, :].rearrange(
                        "h (c t) -> (h c) t", t=CHUNK)).then_inc(landed, 16)
            for h in range(HEADS_IN_TILE):
                load_fox_head(sp, scratch, fox, h, h * F_DH, 0)
            load_fox_v(sp, scratch, fox, 0, 0)
            sp.wait_ge(step["neg_all_ready"], 1)
            sp.dma_start(scratch["f_negF"].rearrange("h (c t) -> (h c) t", t=CHUNK), neg_all[:, :]
                         ).then_inc(step["stored"], 16)
            sp.wait_ge(step["m_prev_ready"], 1)
            sp.dma_start(scratch["m_prev"].rearrange("h c -> (h c)").unsqueeze(0), m_prev[:, :]).then_inc(step["stored"], 16)
            sp.wait_ge(step["g_max_ready"], 1)
            sp.dma_start(scratch["m_G"].rearrange("h (c t) -> (h c) t", t=CHUNK), g_max[:, :]).then_inc(step["stored"], 16)
            sp.wait_ge(step["exponentials"], 1)
            sp.dma_start(scratch["m_decay"].rearrange("h c -> (h c)").unsqueeze(0), decay[:, :]).then_inc(step["stored"], 16)
            sp.wait_ge(step["stored"], 4 * 16)

        @block.gpsimd
        def _(pool):
            pool.memset(ident[:, :], 0.0).then_inc(filled, 1)
            pool.memset(before[:, :, :], 1.0).then_inc(filled, 1)
            pool.wait_ge(filled, 2)
            pool.affine_select(out=ident[:, :], in_=ident[:, :], compare_op=ALU.not_equal, fill=1.0, base=0,
                               pattern=[[-1, P]], channel_multiplier=1).then_inc(selected, 1)
            flat = before[:, :, :].rearrange("p h c -> p (h c)")
            pool.affine_select(out=flat, in_=flat, compare_op=ALU.is_ge, fill=0.0, base=-1,
                               pattern=[[1, P]], channel_multiplier=-1).then_inc(selected, 1)
            pool.wait_ge(selected, 2)
            pool.affine_select(out=before[:, :, :], in_=before[:, :, :], compare_op=ALU.is_ge, fill=0.0, base=0,
                               pattern=[[-CHUNKS, F_HEADS], [0, CHUNKS]], channel_multiplier=1).then_inc(selected, 1)

        @block.scalar
        def _(act):
            act.preload_act_table_set("natural_log_exp_and_others")
            act.wait_ge(step["added"], 1)
            act.activation(log_f[:, :, :], pre[:, 0:2, :], ACT.Abs).then_inc(step["magnitude"], 1)
            act.wait_ge(step["magnitude"], 1)
            act.activation(log_f[:, :, :], log_f[:, :, :], ACT.Exp, scale=-1.0).then_inc(step["exp_neg"], 1)
            act.wait_ge(step["exp_neg"], 1)
            act.activation(log_f[:, :, :], log_f[:, :, :], ACT.Ln, bias=1.0).then_inc(step["log1p"], 1)
            act.wait_ge(step["decay_log"], 1)
            act.activation(decay[:, :], decay[:, :], ACT.Exp).then_inc(step["exponentials"], 1)
            act.wait_ge(step["exponents"], 2)
            act.activation(to_turn[:, 1:3, :], to_turn[:, 1:3, :], ACT.Exp).then_inc(step["exponentials"], 1)

        @block.vector
        def _(dve):
            def done(name, count=1):
                dve.wait_ge(step[name], count)

            dve.memset(pre[:, :, :], 0.0).then_inc(cleared, 1)
            dve.memset(pre_low[:, :, :], 0.0).then_inc(cleared, 1)
            dve.memset(ones[:, :], 1.0).then_inc(cleared, 1)
            dve.memset(zeros[:, :], 0.0).then_inc(cleared, 1)
            dve.memset(m_next[:, :, :], 0.0).then_inc(cleared, 1)
            dve.wait_ge(cleared, 5)
            dve.wait_ge(landed, 6 * 16)
            dve.tensor_add(pre[:, :, :], pre[:, :, :], pre_low[:, :, :]).then_inc(step["added"], 1)
            done("log1p")
            dve.scalar_tensor_tensor(out=log_f[:, :, :], in0=pre[:, 0:2, :], scalar=0.0, in1=log_f[:, :, :],
                                     op0=ALU.min, op1=ALU.subtract).then_inc(step["log_ready"], 1)
            done("log_ready")
            dve.tensor_tensor_scan(out=neg_sum[:, :], data0=ones[:, :], data1=log_f[:, FF, :], initial=0.0,
                                   op0=ALU.mult, op1=ALU.subtract).then_inc(step["neg_sum_ready"], 1)
            dve.tensor_tensor_scan(out=b_sum[:, :], data0=ones[0:HC, :], data1=log_f[0:HC, F, :], initial=0.0,
                                   op0=ALU.mult, op1=ALU.add).then_inc(step["b_ready"], 1)
            done("b_ready")
            g_row = to_turn[:, 0, :]
            dve.tensor_sub(g_row, pre[0:HC, I, :], b_sum[:, :]).then_inc(step["g_ready"], 1)
            done("before_psum")
            dve.tensor_copy(neg_before[:, :], ps_before[:, 0:1]).then_inc(step["before_ready"], 1)
            done("g_ready")
            dve.tensor_tensor_scan(out=g_local[:, :], data0=zeros[:, :], data1=g_row, initial=MASKED,
                                   op0=ALU.add, op1=ALU.max).then_inc(step["local_ready"], 1)
            done("before_ready")
            dve.tensor_scalar(neg_all[:, :], neg_sum[:, :], neg_before[:, 0:1], None, ALU.add
                              ).then_inc(step["neg_all_ready"], 1)
            done("local_ready")
            dve.tensor_copy(ends[:, 0:1], b_sum[:, CHUNK - 1:]).then_inc(step["ends_ready"], 1)
            dve.tensor_copy(ends[:, 1:2], g_local[:, CHUNK - 1:]).then_inc(step["ends_ready"], 1)
            done("ends_psum", 2)
            dve.tensor_copy(end_rows[:, :, :].rearrange("o s n -> o (s n)"), ps_ends[0:1, 0:2 * HC]
                            ).then_inc(step["end_rows_ready"], 1)
            done("end_rows_ready")
            for h in range(M_HEADS):
                cols = slice(h * CHUNKS, (h + 1) * CHUNKS)
                dve.tensor_tensor_scan(out=m_next[:, h, 1:], data0=end_rows[:, 1, cols], data1=end_rows[:, 0, cols],
                                       initial=0.0, op0=ALU.max, op1=ALU.add).then_inc(step["m_next_ready"], 1)
            done("m_next_ready", M_HEADS)
            dve.tensor_copy(m_prev[:, :].rearrange("o (h c) -> o h c", c=CHUNKS), m_next[:, :, 0:CHUNKS]
                            ).then_inc(step["m_prev_ready"], 1)
            done("m_prev_ready")
            dve.tensor_max(decay[:, :], m_prev[:, :], end_rows[:, 1, :]).then_inc(step["last_ready"], 1)
            done("last_ready")
            dve.tensor_sub(decay[:, :], m_prev[:, :], decay[:, :]).then_inc(step["decay_log"], 1)
            done("m_psum")
            dve.tensor_copy(m_col[:, :], ps_m[0:HC, 0:1]).then_inc(step["m_col_ready"], 1)
            done("m_col_ready")
            dve.tensor_scalar(g_max[:, :], g_local[:, :], m_col[:, 0:1], None, ALU.max).then_inc(step["g_max_ready"], 1)
            done("g_max_ready")
            dve.tensor_add(to_turn[:, 2, :], b_sum[:, :], g_max[:, :]).then_inc(step["m_sum"], 1)
            dve.tensor_scalar(to_turn[:, 1, :], g_row, g_max[:, CHUNK - 1:], None, ALU.subtract
                              ).then_inc(step["exponents"], 1)
            done("m_sum")
            dve.tensor_scalar(to_turn[:, 2, :], to_turn[:, 2, :], -1.0, EXP_MAX, ALU.mult, ALU.min
                              ).then_inc(step["exponents"], 1)
            done("turned")
            dve.tensor_copy(keep["gate_cols"][:, :, :, :].rearrange("p s h c -> p (s h c)"), ps_cols[:, 0:3 * HC])

        @block.tensor
        def _(pe):
            pe.wait_ge(selected, 3)
            pe.wait_ge(step["neg_sum_ready"], 1)
            pe.matmul(ps_before[:, 0:1], before[:, :, :].rearrange("p h c -> p (h c)"), neg_sum[:, CHUNK - 1:],
                      start=True, stop=True).then_inc(step["before_psum"], 1)
            pe.wait_ge(step["ends_ready"], 2)
            for i in range(2):
                pe.transpose(ps_ends[0:1, i * HC:(i + 1) * HC], ends[:, i:i + 1], ident[0:HC, 0:HC]
                             ).then_inc(step["ends_psum"], 1)
            pe.wait_ge(step["m_prev_ready"], 1)
            pe.transpose(ps_m[0:HC, 0:1], m_prev[:, :], ident[0:1, 0:1]).then_inc(step["m_psum"], 1)
            pe.wait_ge(step["exponentials"], 2)
            for i in range(3):
                ins = pe.transpose(ps_cols[:, i * HC:(i + 1) * HC], to_turn[:, i, :], ident[0:HC, 0:HC])
            ins.then_inc(step["turned"], 1)


def forgetting_heads(nc, a, scratch, fox, w_land):
    with ExitStack() as ctx:
        def sb(name, shape, dt=F32):
            return ctx.enter_context(nc.sbuf_tensor("f_" + name, shape, dt))

        def psum(name, shape):
            return ctx.enter_context(nc.psum_tensor("f_" + name, shape, F32))

        def sem(name):
            return ctx.enter_context(nc.semaphore("f_" + name))

        QT = NB // P
        GROUPS = TT // QT
        HP = HEADS_IN_TILE
        PAIRS = F_HEADS // HP
        q_pack, k_hi2, k_lo2, v_tok, gate_z = (fox[name] for name in ("q_pack", "k_hi2", "k_lo2", "v_tok", "gate_z"))
        head_landed, v_landed, z_landed = fox["head_landed"], fox["v_landed"], fox["z_landed"]
        neg_f = sb("neg_f", [P, HP, SEQ])
        probs = sb("probs", [P, 2, QT, SEQ])
        probs_t = sb("probs_t", [P, 2, 2, NB])
        out_t = sb("out_t", [P, NB])
        out_tok = sb("out_tok", [P, 2, QT, HP, F_DH])
        y_out = sb("y_out", [P, 2, NB])
        part_max = sb("part_max", [P, 2, QT, GROUPS])
        neg_max = sb("neg_max", [P, 2, QT])
        row_sum = sb("row_sum", [P, 4, QT])
        inv_sum = sb("inv_sum", [P, 4, QT])
        ident = sb("ident", [P, P])
        mask = sb("mask", [P, P])
        ident_r = sb("ident_r", [P, P], F32R)
        mask_r = sb("mask_r", [P, P], F32R)
        fold = sb("fold", [P, F_DH])
        ps_s = psum("ps_s", [P, 2, NB])
        ps_t = psum("ps_t", [P, 2, 2, NB])
        ps_o = psum("ps_o", [P, NB])
        ps_x = psum("ps_x", [P, NB])

        zeroed = sem("zeroed")
        const_ready = sem("const_ready")
        masks_ready = sem("masks_ready")
        s_psum = sem("s_psum")
        s_used = sem("s_used")
        logits_begun = sem("logits_begun")
        max_ready = sem("max_ready")
        exp_ready = sem("exp_ready")
        t_psum = sem("t_psum")
        even_ready = sem("even_ready")
        odd_ready = sem("odd_ready")
        pv_done = sem("pv_done")
        ot_ready = sem("ot_ready")
        fold_psum = sem("fold_psum")
        inv_ready = sem("inv_ready")
        x_used = sem("x_used")
        y_psum = sem("y_psum")
        y_stored = [sem(f"y_stored{i}") for i in range(2)]
        w_landed = sem("w_landed")

        ORDER = [(h, J) for J in range(GROUPS) for h in range(HP)]
        assert HP == 2
        X_READS = (HP + 1) * GROUPS

        def x_reads_before(g):
            return (HP + 1) * (g // HP) + g % HP

        def chunks(J):
            return [(r, c, NB if c < J else (r + 1) * P, c == J) for r in range(QT) for c in range(J + 1)]

        def pairs(J):
            return QT * (J + 1) // 2

        def chunks_before(g, m=0):
            return sum(len(chunks(J)) for _, J in ORDER[:g]) + m

        def pairs_before(g, p=0):
            return sum(pairs(J) for _, J in ORDER[:g]) + p

        ALL_CHUNKS, ALL_PAIRS, ALL_ROWS = chunks_before(len(ORDER)), pairs_before(len(ORDER)), QT * len(ORDER)

        LAST = len(ORDER)

        def plan(g, last):
            n = pairs(ORDER[g][1])
            following = [] if g + 1 == LAST and last else chunks(ORDER[(g + 1) % LAST][1])
            steps = max(1, n - 1.5)
            cuts = [min(len(following), math.ceil(len(following) * p / steps)) for p in range(n + 1)]
            return [list(enumerate(following))[cuts[p]:cuts[p + 1]] for p in range(n)]

        def columns_of(J, kt):
            return max(0, kt - QT * J) * P

        block = ctx.enter_context(nc.Block())

        @block.sync
        def _(sp):
            def load_neg_f(h, pair, half):
                cols = slice(half * SEQ // 2, (half + 1) * SEQ // 2)
                sp.dma_start(neg_f[:, h, cols], scratch["f_negF"][bass.ds(pair * HP + h, 1), cols].broadcast_to(
                    [P, SEQ // 2])).then_inc(head_landed[h][half], 16)

            def load_head(h, pair):
                for half in range(2):
                    load_fox_head(sp, scratch, fox, h, pair * P + h * F_DH, half)
                    load_neg_f(h, pair, half)

            for h in range(HP):
                load_neg_f(h, 0, 0)
            load_fox_z(sp, scratch, fox, 0)
            for h in range(HP):
                load_fox_head(sp, scratch, fox, h, h * F_DH, 1)
                load_neg_f(h, 0, 1)
            load_fox_v(sp, scratch, fox, 1, 0)
            sp.dma_start(w_land[:, :, :], a["w_out"][0].rearrange("(k p) n -> p k n", p=P)).then_inc(w_landed, 16)

            def store_y(n, J):
                sp.wait_ge(x_used, n * X_READS + (HP + 1) * (J + 1) + 1)
                sp.dma_start(scratch["yT"][bass.ds(n * P, P), J * NB:(J + 1) * NB],
                             y_out[:, J % 2, :]).then_inc(y_stored[J % 2], 16)

            with sp.Fori(0, PAIRS - 1) as n:
                for J in range(GROUPS - 2):
                    store_y(n, J)
                sp.wait_ge(s_used, n * ALL_CHUNKS + 2 + chunks_before(LAST - 1))
                load_head(0, n + 1)
                store_y(n, GROUPS - 2)
                sp.wait_ge(s_used, n * ALL_CHUNKS + 2 + chunks_before(LAST))
                load_head(1, n + 1)
                for half in range(2):
                    sp.wait_ge(pv_done, n * ALL_PAIRS + 2 + pairs_before(LAST - 1, (half + 1) * TT // 4))
                    load_fox_v(sp, scratch, fox, half, n + 1)
                store_y(n, GROUPS - 1)
                load_fox_z(sp, scratch, fox, n + 1)
            for J in range(GROUPS):
                store_y(PAIRS - 1, J)
            for i in range(2):
                sp.wait_ge(y_stored[i], 16 + PAIRS * GROUPS // 2 * 16)
            sp.wait_ge(w_landed, 16)

        @block.gpsimd
        def _(pool):
            pool.memset(ident[:, :], 0.0).then_inc(zeroed, 1)
            pool.memset(mask[:, :], 0.0).then_inc(zeroed, 1)
            pool.memset(fold[:, :], 0.0).then_inc(zeroed, 1)
            pool.wait_ge(zeroed, 3)
            pool.affine_select(out=ident[:, :], in_=ident[:, :], compare_op=ALU.not_equal, fill=1.0, base=0,
                               pattern=[[-1, P]], channel_multiplier=1).then_inc(const_ready, 1)
            pool.affine_select(out=mask[:, :], in_=mask[:, :], compare_op=ALU.is_ge, fill=MASKED, base=0,
                               pattern=[[-1, P]], channel_multiplier=1).then_inc(const_ready, 1)
            for h in range(2):
                pool.wait_ge(const_ready, 2 + h)
                pool.affine_select(out=fold[:, :], in_=fold[:, :], compare_op=ALU.not_equal, fill=1.0,
                                   base=-h * F_DH, pattern=[[-1, F_DH]], channel_multiplier=1).then_inc(const_ready, 1)

        @block.tensor
        def _(pe):
            pe.sem_inc(fold_psum, 1)
            pe.wait_ge(const_ready, 4)
            pe.wait_ge(masks_ready, 2)
            def pair_of_heads(n, last_pair):
                def scores(g, m, r, c, width, last):
                    h, J = ORDER[g % LAST]
                    at = chunks_before(g, m)
                    if m == 0 and J * NB % (SEQ // 2) == 0:
                        pe.wait_ge(head_landed[h][J * NB // (SEQ // 2)], (n + 1 + g // LAST) * 7 * 16)
                    pe.wait_ge(s_used, n * ALL_CHUNKS + at + 1)
                    q = q_pack[:, h, (J * QT + r) * P:(J * QT + r + 1) * P]
                    keys = slice(c * NB, c * NB + width)
                    bank = ps_s[:, at % 2, :]
                    pe.matmul(bank[:, 0:width], q, k_hi2[:, h, keys], start=True, stop=False)
                    ins = pe.matmul(bank[:, 0:width], q, k_lo2[:, h, keys], start=False, stop=not last)
                    if last:
                        ins = pe.matmul(bank[:, width - P:width], ident_r[:, :], mask_r[:, :], start=False, stop=True)
                    ins.then_inc(s_psum, 1)

                def turn(g, p):
                    h, J = ORDER[g % LAST]
                    at = pairs_before(g, p)
                    for r in range(QT):
                        if p == 0:
                            pe.wait_ge(exp_ready, n * ALL_ROWS + g * QT + r + 1)
                        for e in range(2):
                            kt = 2 * p + e
                            if r * P >= columns_of(J, kt):
                                ins = pe.transpose(ps_t[:, at % 2, e, r * P:(r + 1) * P],
                                                   probs[:, g % 2, r, kt * P:(kt + 1) * P], ident[:, :])
                    ins.then_inc(t_psum, 1)

                def product(g, p):
                    h, J = ORDER[g % LAST]
                    at = pairs_before(g, p)
                    pe.wait_ge(even_ready, n * ALL_PAIRS + at + 1)
                    pe.wait_ge(odd_ready, n * ALL_PAIRS + at + 1)
                    for half in range(2):
                        if h == 0 and 2 * p == half * TT // 2 and J == half * TT // 2 // QT:
                            pe.wait_ge(v_landed[half], (n + 1) * 16)
                    if p == 0:
                        pe.wait_ge(ot_ready, n * LAST + g + 1)
                    for e in range(2):
                        kt = 2 * p + e
                        first = columns_of(J, kt)
                        ins = pe.matmul(ps_o[e * F_DH:(e + 1) * F_DH, first:], v_tok[:, kt, h, :],
                                        probs_t[:, at % 2, e, first:], start=(p == 0), stop=(p == pairs(J) - 1))
                    ins.then_inc(pv_done, 1)

                def finish(g):
                    h, J = ORDER[g % LAST]
                    pe.wait_ge(ot_ready, n * LAST + g + 2)
                    pe.wait_ge(x_used, n * X_READS + x_reads_before(g) + 1)
                    for r in range(QT):
                        rows = slice(0, F_DH if J == 0 and r == 0 else P)
                        ins = pe.matmul(ps_x[:, r * F_DH:(r + 1) * F_DH], out_t[rows, r * P:(r + 1) * P],
                                        fold[rows, :], start=True, stop=True)
                    ins.then_inc(fold_psum, 1)

                def turn_back(g):
                    h, J = ORDER[g % LAST]
                    if h == HP - 1:
                        pe.wait_ge(x_used, n * X_READS + x_reads_before(g) + 2)
                        for r in range(QT):
                            ins = pe.transpose(ps_x[:, r * P:(r + 1) * P],
                                               out_tok[:, J % 2, r, :, :].rearrange("p h d -> p (h d)"), ident[:, :])
                        ins.then_inc(y_psum, 1)

                if n is None:
                    n = 0
                    for m, chunk in enumerate(chunks(ORDER[0][1])):
                        scores(0, m, *chunk)
                    turn(0, 0)
                    return
                for g, (h, J) in enumerate(ORDER):
                    for p, share in enumerate(plan(g, last_pair)):
                        for m, chunk in share[:1]:
                            scores(g + 1, m, *chunk)
                        if g or p:
                            turn(g, p)
                        for m, chunk in share[1:2]:
                            scores(g + 1, m, *chunk)
                        if p:
                            product(g, p - 1)
                        for m, chunk in share[2:]:
                            scores(g + 1, m, *chunk)
                        if p == 0 and g:
                            finish(g - 1)
                        if p == 1 and g:
                            turn_back(g - 1)
                    product(g, pairs(J) - 1)
                if not last_pair:
                    turn(LAST, 0)
                finish(LAST - 1)
                turn_back(LAST - 1)

            pair_of_heads(None, False)
            with pe.Fori(0, PAIRS - 1) as n:
                pair_of_heads(n, False)
            pair_of_heads(PAIRS - 1, True)

        @block.vector
        def _(dve):
            dve.wait_ge(const_ready, 4)
            dve.tensor_copy(ident_r[:, :], ident[:, :]).then_inc(masks_ready, 1)
            dve.tensor_copy(mask_r[:, :], mask[:, :]).then_inc(masks_ready, 1)
            dve.sem_inc(s_used, 2)
            dve.sem_inc(x_used, 1)
            def pair_of_heads(n, last_pair):
                def logits(g, m, r, c, width, last):
                    h, J = ORDER[g % LAST]
                    at = chunks_before(g, m)
                    dve.wait_ge(s_psum, n * ALL_CHUNKS + at + 1)
                    if m == 0 and J * NB % (SEQ // 2) == 0:
                        dve.wait_ge(head_landed[h][J * NB // (SEQ // 2)], (n + 1 + g // LAST) * 7 * 16)
                    keys = slice(c * NB, c * NB + width)
                    dve.sem_inc(logits_begun, 1)
                    dve.tensor_tensor_reduce(out=probs[:, g % 2, r, keys], in0=ps_s[:, at % 2, 0:width],
                                             in1=neg_f[:, h, keys], scale=1.0, scalar=MASKED, op0=ALU.add,
                                             op1=ALU.max, accum_out=part_max[:, g % 2, r, c:c + 1]
                                             ).then_inc(s_used, 1)
                    if last:
                        dve.wait_ge(s_used, n * ALL_CHUNKS + at + 3)
                        dve.tensor_reduce(neg_max[:, g % 2, r:r + 1], part_max[:, g % 2, r, 0:c + 1], axis=AX_X,
                                          op=ALU.max, negate=True).then_inc(max_ready, 1)

                def odd(g, p):
                    h, J = ORDER[g % LAST]
                    at = pairs_before(g, p)
                    first = columns_of(J, 2 * p + 1)
                    dve.wait_ge(t_psum, n * ALL_PAIRS + at + 1)
                    dve.wait_ge(pv_done, n * ALL_PAIRS + at + 1)
                    dve.tensor_copy(probs_t[:, at % 2, 1, first:], ps_t[:, at % 2, 1, first:]).then_inc(odd_ready, 1)

                def finish(g):
                    h, J = ORDER[g % LAST]
                    dve.wait_ge(exp_ready, n * ALL_ROWS + (g + 1) * QT)
                    dve.reciprocal(inv_sum[:, g % 4, :], row_sum[:, g % 4, :]).then_inc(inv_ready, 1)
                    dve.wait_ge(inv_ready, n * LAST + g + 1)
                    dve.wait_ge(fold_psum, n * LAST + g + 2)
                    dve.tensor_mul(out_tok[:, J % 2, :, h, :],
                                   ps_x[:, 0:QT * F_DH].rearrange("p (r d) -> p r d", d=F_DH),
                                   inv_sum[:, g % 4, :].unsqueeze(2).broadcast_to([P, QT, F_DH])).then_inc(x_used, 1)

                def output(g):
                    h, J = ORDER[g % LAST]
                    if h == HP - 1:
                        dve.wait_ge(y_psum, n * GROUPS + J + 1)
                        dve.wait_ge(z_landed, (n + 1) * 16)
                        dve.wait_ge(y_stored[J % 2], (n * GROUPS // 2 + J // 2 + 1) * 16)
                        dve.tensor_mul(y_out[:, J % 2, :], ps_x[:, :], gate_z[:, J * NB:(J + 1) * NB]).then_inc(x_used, 1)

                if n is None:
                    n = 0
                    for m, chunk in enumerate(chunks(ORDER[0][1])):
                        logits(0, m, *chunk)
                    odd(0, 0)
                    return
                for g, (h, J) in enumerate(ORDER):
                    for p, share in enumerate(plan(g, last_pair)):
                        for m, chunk in share[:1]:
                            logits(g + 1, m, *chunk)
                        if g or p:
                            odd(g, p)
                        for m, chunk in share[1:]:
                            logits(g + 1, m, *chunk)
                        if p == 0 and g:
                            finish(g - 1)
                        if p == 1 and g:
                            output(g - 1)
                if not last_pair:
                    odd(LAST, 0)
                finish(LAST - 1)
                output(LAST - 1)

            pair_of_heads(None, False)
            with dve.Fori(0, PAIRS - 1) as n:
                pair_of_heads(n, False)
            pair_of_heads(PAIRS - 1, True)

        @block.scalar
        def _(act):
            act.preload_act_table(ACT.Exp)
            act.sem_inc(ot_ready, 1)
            act.sem_inc(pv_done, 2)
            act.sem_inc(y_stored[0], 16)
            act.sem_inc(y_stored[1], 16)
            def pair_of_heads(n, last_pair):
                def exponential(g, m, r, c, width, last):
                    if not last:
                        return
                    act.wait_ge(max_ready, n * ALL_ROWS + g * QT + r + 1)
                    row = probs[:, g % 2, r, 0:c * NB + width]
                    act.activation(row, row, ACT.Exp, bias=neg_max[:, g % 2, r:r + 1],
                                   accum_out=row_sum[:, g % 4, r:r + 1]).then_inc(exp_ready, 1)

                def even(g, p):
                    h, J = ORDER[g % LAST]
                    at = pairs_before(g, p)
                    first = columns_of(J, 2 * p)
                    act.wait_ge(t_psum, n * ALL_PAIRS + at + 1)
                    act.wait_ge(pv_done, n * ALL_PAIRS + at + 1)
                    act.activation(probs_t[:, at % 2, 0, first:], ps_t[:, at % 2, 0, first:], ACT.Copy
                                   ).then_inc(even_ready, 1)

                if n is None:
                    n = 0
                    for m, chunk in enumerate(chunks(ORDER[0][1])):
                        exponential(0, m, *chunk)
                    even(0, 0)
                    return
                for g, (h, J) in enumerate(ORDER):
                    for p, share in enumerate(plan(g, last_pair)):
                        if g or p:
                            even(g, p)
                        for m, chunk in share:
                            exponential(g + 1, m, *chunk)
                    act.wait_ge(pv_done, n * ALL_PAIRS + 2 + pairs_before(g + 1))
                    act.wait_ge(fold_psum, n * LAST + g + 1)
                    if J == 0:
                        act.activation(out_t[0:F_DH, 0:P], ps_o[0:F_DH, 0:P], ACT.Copy)
                        act.activation(out_t[:, P:], ps_o[:, P:], ACT.Copy).then_inc(ot_ready, 1)
                    else:
                        act.activation(out_t[:, :], ps_o[:, :], ACT.Copy).then_inc(ot_ready, 1)
                if not last_pair:
                    even(LAST, 0)

            pair_of_heads(None, False)
            with act.Fori(0, PAIRS - 1) as n:
                pair_of_heads(n, False)
            pair_of_heads(PAIRS - 1, True)



def memory_heads_and_output(nc, a, scratch, keep, w_land, out):
    with ExitStack() as ctx:
        def sb(name, shape, dt=F32):
            return ctx.enter_context(nc.sbuf_tensor("m_" + name, shape, dt))

        def psum(name, shape):
            return ctx.enter_context(nc.psum_tensor("m_" + name, shape, F32))

        def sem(name):
            return ctx.enter_context(nc.semaphore("m_" + name))

        H, W = M_HEADS, M_DH + 1
        FT = F_W // P
        ON = D_MODEL // NB
        q_in = sb("q_in", [P, 2, H, CHUNK])
        k_in = sb("k_in", [P, 2, H, CHUNK])
        v_in = sb("v_in", [P, 2, H, W])
        o_in = sb("o_in", [P, 2, H, M_DH])
        z_in = sb("z_in", [P, 2, H, CHUNK])
        g_max = sb("g_max", [P, 2, H, CHUNK])
        w_in = sb("w_in", [P, 2, H, CHUNK])
        decay = sb("decay", [P, H, CHUNKS])
        m_prev = sb("m_prev", [P, H, CHUNKS])
        diff = sb("diff", [P, 2, H, CHUNK])
        q_w = sb("q_w", [P, 2, H, CHUNK])
        scores = sb("scores", [P, H, CHUNK])
        k_w = sb("k_w", [P, H, M_DH])
        state = sb("state", [P, 2, H, W])
        den = sb("den", [P, 2, H])
        gated = sb("gated", [P, H, M_DH])
        stats = sb("stats", [P, H, nc.vector.BN_STATS_DIM])
        moments = sb("moments", [P, H, 2])
        rstd = sb("rstd", [P, H])
        normed = sb("normed", [P, H, M_DH])
        ident = sb("ident", [P, P])
        future = sb("future", [P, CHUNK])
        w_hi = sb("w_hi", [P, KT, D_MODEL], F32R)
        w_lo = sb("w_lo", [P, KT, D_MODEL], F32R)
        gate = sb("gate", [P, D_MODEL])
        y = sb("y", [P, 2, KT, CHUNK])
        y_hi = sb("y_hi", [P, 2, KT, CHUNK], F32R)
        y_lo = sb("y_lo", [P, 2, KT, CHUNK], F32R)
        x_in = sb("x_in", [P, 2, D_MODEL])
        update = sb("update", [P, 2, D_MODEL])
        result = sb("result", [P, 2, D_MODEL])
        ps_s = psum("ps_s", [P, H, CHUNK])
        ps_k = psum("ps_k", [P, H, CHUNK])
        ps_m = psum("ps_m", [P, 3, NB])
        ps_y = psum("ps_y", [P, H, CHUNK])
        ps_out = psum("ps_out", [P, ON, NB])

        def at(i):
            return slice(i * W, (i + 1) * W)

        numerators = ps_m[:, 0:2, 0:2 * W].rearrange("p b (h w) -> p b h w", w=W)
        num = [ps_m[:, h // 2, at(h % 2)] for h in range(H)]
        new = [ps_m[:, 0, at(2)], ps_m[:, 1, at(2)], ps_m[:, 2, at(0)], ps_m[:, 2, at(1)]]

        zeroed = sem("zeroed")
        const_ready = sem("const_ready")
        state_zero = sem("state_zero")
        rows_landed = sem("rows_landed")
        landed = [sem(f"landed{i}") for i in range(2)]
        late_landed = [sem(f"late_landed{i}") for i in range(2)]
        x_landed = [sem(f"x_landed{i}") for i in range(2)]
        diff_ready = sem("diff_ready")
        masked = sem("masked")
        weights_ready = sem("weights_ready")
        win_ready = sem("win_ready")
        qw_ready = sem("qw_ready")
        s_psum = sem("s_psum")
        k_psum = sem("k_psum")
        scores_ready = sem("scores_ready")
        kw_ready = sem("kw_ready")
        products_done = sem("products_done")
        negative_ready = sem("negative_ready")
        den_ready = sem("den_ready")
        inv_ready = sem("inv_ready")
        hidden_ready = sem("hidden_ready")
        state_ready = sem("state_ready")
        stats_ready = sem("stats_ready")
        stats_seen = sem("stats_seen")
        moments_ready = sem("moments_ready")
        log_ready = sem("log_ready")
        rstd_ready = sem("rstd_ready")
        normed_ready = sem("normed_ready")
        y_psum = sem("y_psum")
        y_ready = sem("y_ready")
        yhi_ready = sem("yhi_ready")
        y_split = sem("y_split")
        w_hi_ready = sem("w_hi_ready")
        w_ready = sem("w_ready")
        projected = sem("projected")
        out_taken = sem("out_taken")
        added = sem("added")
        stored = [sem(f"stored{i}") for i in range(2)]
        LOADS, LATE_LOADS, ROW_LOADS = 5, 2, 3

        block = ctx.enter_context(nc.Block())

        @block.sync
        def _(sp):
            def tile_rows(first, c):
                return scratch["arrays"][first * P:(first + H) * P, bass.ds(c * CHUNK, CHUNK)].rearrange(
                    "(h p) t -> p h t", p=P)

            def load(par, c):
                for buf, src in ((k_in[:, par], tile_rows(A_MK, c)), (q_in[:, par], tile_rows(A_MQ, c)),
                                 (g_max[:, par], scratch["m_G"][:, bass.ds(c * CHUNK, CHUNK)].unsqueeze(0).broadcast_to(
                                     [P, H, CHUNK])),
                                 (v_in[:, par, :, 0:M_DH], tile_rows(A_MV, c)), (o_in[:, par], tile_rows(A_MO, c))):
                    sp.dma_start(buf, src).then_inc(landed[par], 16)

            def load_late(par, c):
                sp.dma_start(z_in[:, par], tile_rows(A_MZ, c)).then_inc(late_landed[par], 16)
                sp.dma_start(y[:, par, H:KT, :], scratch["yT"][:, bass.ds(c * CHUNK, CHUNK)].rearrange(
                    "(k p) t -> p k t", p=P)).then_inc(late_landed[par], 16)

            def load_x(par, c):
                sp.dma_start(x_in[:, par, :], a["x"][0, bass.ds(c * CHUNK, CHUNK), :]).then_inc(x_landed[par], 16)

            def store(par, c):
                sp.wait_ge(added, c + 3)
                sp.dma_start(out[0, bass.ds(c * CHUNK, CHUNK), :], result[:, par, :]).then_inc(stored[par], 16)

            for row, buf in (("m_decay", decay), ("m_prev", m_prev)):
                sp.dma_start(buf[:, :, :], scratch[row].unsqueeze(0).broadcast_to([P, H, CHUNKS])
                             ).then_inc(rows_landed, 16)
            load(0, 0)
            load(1, 1)
            load_late(0, 0)
            sp.dma_start(gate[:, :], scratch["gate"]).then_inc(rows_landed, 16)
            load_late(1, 1)
            for par in range(2):
                load_x(par, par)

            def reload(par, c):
                sp.wait_ge(state_ready, c)
                sp.wait_ge(hidden_ready, c)
                load(par, c)
                sp.wait_ge(y_split, c - 1)
                load_late(par, c)

            reload(0, 2)
            with sp.Fori(0, CHUNKS // 2 - 2) as n:
                for par in range(2):
                    reload(1 - par, n * 2 + par + 3)
                    store(par, n * 2 + par)
                    load_x(par, n * 2 + par + 2)
            reload(1, CHUNKS - 1)
            for par in range(2):
                store(par, CHUNKS - 4 + par)
                load_x(par, CHUNKS - 2 + par)
            for par in range(2):
                store(par, CHUNKS - 2 + par)
            for par in range(2):
                sp.wait_ge(stored[par], 16 + CHUNKS // 2 * 16)

        @block.gpsimd
        def _(pool):
            pool.memset(ident[:, :], 0.0).then_inc(zeroed, 1)
            pool.memset(future[:, :], 0.0).then_inc(zeroed, 1)
            pool.memset(v_in[:, :, :, M_DH:W], 1.0).then_inc(const_ready, 1)
            pool.wait_ge(zeroed, 2)
            pool.affine_select(out=ident[:, :], in_=ident[:, :], compare_op=ALU.not_equal, fill=1.0, base=0,
                               pattern=[[-1, P]], channel_multiplier=1).then_inc(const_ready, 1)
            pool.affine_select(out=future[:, :], in_=future[:, :], compare_op=ALU.is_ge, fill=MASKED, base=0,
                               pattern=[[1, CHUNK]], channel_multiplier=-1).then_inc(const_ready, 1)
            for par in range(2):
                pool.sem_inc(stored[par], 16)

            def weigh(par, c):
                pool.wait_ge(win_ready, c + 1)
                pool.tensor_tensor(out=q_w[:, par], in0=q_in[:, par], in1=w_in[:, par], op=ALU.mult
                                   ).then_inc(qw_ready, 1)

            def add(par, n, c):
                pool.wait_ge(out_taken, c + 2)
                pool.wait_ge(x_landed[par], (n + 1) * 16)
                pool.wait_ge(stored[par], (n + 1) * 16)
                pool.tensor_tensor(out=result[:, par, :], in0=update[:, par, :], in1=x_in[:, par, :], op=ALU.add
                                   ).then_inc(added, 1)

            weigh(0, 0)
            weigh(1, 1)
            with pool.Fori(0, CHUNKS // 2 - 1) as n:
                for par in range(2):
                    weigh(par, n * 2 + par + 2)
                    add(par, n, n * 2 + par)
            for par in range(2):
                add(par, CHUNKS // 2 - 1, CHUNKS - 2 + par)

        @block.tensor
        def _(pe):
            pe.wait_ge(const_ready, 3)
            pe.wait_ge(state_zero, 1)

            def score(par, n):
                pe.wait_ge(landed[par], (n + 1) * LOADS * 16)
                for h in range(H):
                    ins = pe.matmul(ps_s[:, h, :], k_in[:, par, h, :], q_in[:, par, h, :], start=True, stop=True)
                ins.then_inc(s_psum, 1)
                for h in range(H):
                    ins = pe.transpose(ps_k[:, h, :], k_in[:, par, h, :], ident[:, :])
                ins.then_inc(k_psum, 1)

            def products(par, c):
                pe.wait_ge(scores_ready, c + 1)
                pe.wait_ge(qw_ready, c + 1)
                pe.wait_ge(hidden_ready, c + 1)
                pe.wait_ge(state_ready, c + 1)
                for h in range(H):
                    pe.matmul(num[h], scores[:, h, :], v_in[:, par, h, :], start=True, stop=False)
                    pe.matmul(num[h], q_w[:, par, h, :], state[:, par, h, :], start=False, stop=True)
                pe.wait_ge(kw_ready, c + 1)
                for h in range(H):
                    ins = pe.matmul(new[h], k_w[:, h, :], v_in[:, par, h, :], start=True, stop=True)
                ins.then_inc(products_done, 1)

            def turn(c):
                pe.wait_ge(normed_ready, c + 1)
                for h in range(H):
                    ins = pe.transpose(ps_y[:, h, :], normed[:, h, :], ident[:, :])
                ins.then_inc(y_psum, 1)

            def project(par, c, between):
                pe.wait_ge(y_split, c + 1)
                pe.wait_ge(out_taken, c + 1)
                for k in range(KT):
                    for part, w in ((y_hi, w_hi), (y_hi, w_lo), (y_lo, w_hi)):
                        for b in range(ON):
                            ins = pe.matmul(ps_out[:, b, :], part[:, par, k, :], w[:, k, b * NB:(b + 1) * NB],
                                            start=(k == 0 and part is y_hi and w is w_hi),
                                            stop=(k == KT - 1 and part is y_lo))
                    if k == KT - 1:
                        ins.then_inc(projected, 1)
                    if k in between:
                        between[k]()

            score(0, 0)
            products(0, 0)
            score(1, 0)
            turn(0)
            pe.wait_ge(w_ready, KT)
            with pe.Fori(0, CHUNKS // 2 - 1) as n:
                for par in (1, 0):
                    c = n * 2 + 2 - par
                    products(par, c)
                    project(1 - par, c - 1, {1: lambda: score(1 - par, n + 1), 5: lambda: turn(c)})
            products(1, CHUNKS - 1)
            project(0, CHUNKS - 2, {5: lambda: turn(CHUNKS - 1)})
            project(1, CHUNKS - 1, {})

        @block.vector
        def _(dve):
            dve.memset(state[:, 0], 0.0).then_inc(state_zero, 1)
            dve.sem_inc(hidden_ready, 1)
            dve.sem_inc(state_ready, 1)
            dve.sem_inc(out_taken, 1)
            dve.sem_inc(added, 2)

            def low_weights(ks):
                for k in ks:
                    dve.wait_ge(w_hi_ready, k + 1)
                    dve.tensor_sub(w_lo[:, k, :], w_land[:, k, :], w_hi[:, k, :].bitcast(F32)).then_inc(w_ready, 1)

            low_weights(range(KT // 2))
            dve.wait_ge(const_ready, 3)
            dve.wait_ge(rows_landed, ROW_LOADS * 16)

            def prepare(par, n, c):
                dve.wait_ge(landed[par], (n + 1) * LOADS * 16)
                g_col = keep["gate_cols"][:, COL_G, :, bass.ds(c, 1)].broadcast_to([P, H, CHUNK])
                dve.tensor_sub(diff[:, par], g_col, g_max[:, par]).then_inc(diff_ready, 1)
                dve.wait_ge(diff_ready, c + 1)
                dve.scalar_tensor_tensor(out=diff[:, par], in0=diff[:, par], scalar=0.0,
                                         in1=future[:, :].unsqueeze(1).broadcast_to([P, H, CHUNK]),
                                         op0=ALU.min, op1=ALU.add).then_inc(masked, 1)
                dve.wait_ge(k_psum, c + 1)
                ws_col = keep["gate_cols"][:, COL_WS, :, bass.ds(c, 1)].broadcast_to([P, H, CHUNK])
                dve.tensor_mul(k_w[:, :, :], ps_k[:, :, :], ws_col).then_inc(kw_ready, 1)
                dve.wait_ge(weights_ready, c + 1)
                dve.wait_ge(s_psum, c + 1)
                dve.tensor_mul(scores[:, :, :], ps_s[:, :, :], diff[:, par]).then_inc(scores_ready, 1)

            def divide(par, c):
                em = keep["gate_cols"][:, COL_EM, :, bass.ds(c, 1)].rearrange("p (b h) o -> p b (h o)", b=2)
                bound = den[:, 0, :].rearrange("p (b h) -> p b h", b=2)
                dve.wait_ge(products_done, c + 1)
                dve.scalar_tensor_tensor(out=bound, in0=numerators[:, :, :, M_DH], scalar=-1.0, in1=em,
                                         op0=ALU.mult, op1=ALU.max).then_inc(negative_ready, 1)
                dve.wait_ge(negative_ready, c + 1)
                dve.tensor_max(bound, numerators[:, :, :, M_DH], bound).then_inc(den_ready, 1)
                dve.wait_ge(den_ready, c + 1)
                dve.reciprocal(den[:, 1, :], den[:, 0, :]).then_inc(inv_ready, 1)
                dve.wait_ge(inv_ready, c + 1)
                for h in range(H):
                    ins = dve.scalar_tensor_tensor(out=gated[:, h, :], in0=num[h][:, 0:M_DH],
                                                   scalar=den[:, 1, h:h + 1], in1=o_in[:, par, h, :],
                                                   op0=ALU.mult, op1=ALU.mult)
                ins.then_inc(hidden_ready, 1)

            def carry(par, c):
                for h in range(H):
                    ins = dve.scalar_tensor_tensor(out=state[:, 1 - par, h, :], in0=state[:, par, h, :],
                                                   scalar=decay[:, h, bass.ds(c, 1)],
                                                   in1=new[h], op0=ALU.mult, op1=ALU.add)
                ins.then_inc(state_ready, 1)

            def moments_of(c):
                dve.wait_ge(hidden_ready, c + 2)
                for h in range(H):
                    ins = dve.bn_stats(stats[:, h, :], gated[:, h, :])
                ins.then_inc(stats_ready, 1)
                dve.wait_ge(stats_ready, c + 1)
                dve.sem_inc(stats_seen, 1)
                for h in range(H):
                    ins = dve.bn_aggr(moments[:, h, :], stats[:, h, :])
                ins.then_inc(moments_ready, 1)

            def output(par, n, c):
                dve.wait_ge(rstd_ready, c + 1)
                for h in range(H):
                    ins = dve.tensor_scalar(normed[:, h, :], gated[:, h, :], moments[:, h, 0:1], rstd[:, h:h + 1],
                                            ALU.subtract, ALU.mult)
                ins.then_inc(normed_ready, 1)
                dve.wait_ge(y_psum, c + 1)
                dve.wait_ge(late_landed[par], (n + 1) * LATE_LOADS * 16)
                for h in range(H):
                    ins = dve.scalar_tensor_tensor(out=y[:, par, h, :], in0=ps_y[:, h, :],
                                                   scalar=keep["params"][:, NORM_GAIN + h:NORM_GAIN + h + 1],
                                                   in1=z_in[:, par, h, :], op0=ALU.mult, op1=ALU.mult)
                ins.then_inc(y_ready, 1)
                dve.wait_ge(yhi_ready, c + 1)
                dve.tensor_sub(y_lo[:, par], y[:, par], y_hi[:, par].bitcast(F32)).then_inc(y_split, 1)

            def residual(par, c):
                dve.wait_ge(projected, c + 1)
                dve.wait_ge(added, c + 1)
                dve.tensor_mul(update[:, par, :], ps_out[:, :, :].rearrange("p b n -> p (b n)"), gate[:, :]
                               ).then_inc(out_taken, 1)

            def chunk(par, c, n, following):
                divide(par, c)
                carry(par, c)
                moments_of(c)
                if following:
                    prepare(1 - par, *following)
                output(par, n, c)

            prepare(0, 0, 0)
            low_weights(range(KT // 2, KT))
            chunk(0, 0, 0, (0, 1))
            with dve.Fori(0, CHUNKS // 2 - 1) as n:
                for par in (1, 0):
                    c = n * 2 + 2 - par
                    chunk(par, c, n + 1 - par, (n + 1, c + 1))
                    residual(1 - par, c - 1)
            chunk(1, CHUNKS - 1, CHUNKS // 2 - 1, None)
            residual(0, CHUNKS - 2)
            residual(1, CHUNKS - 1)

        @block.scalar
        def _(act):
            act.preload_act_table_set("natural_log_exp_and_others")

            def high_weights(ks):
                for k in ks:
                    act.activation(w_hi[:, k, :], w_land[:, k, :], ACT.Copy).then_inc(w_hi_ready, 1)

            high_weights(range(KT // 2))
            act.wait_ge(rows_landed, ROW_LOADS * 16)

            def carried_weight(par, n, c):
                act.wait_ge(landed[par], (n + 1) * LOADS * 16)
                for h in range(H):
                    ins = act.activation(w_in[:, par, h, :], g_max[:, par, h, :], ACT.Exp,
                                         bias=m_prev[:, h, bass.ds(c, 1)], scale=-1.0)
                ins.then_inc(win_ready, 1)

            def weights(par, c):
                act.wait_ge(masked, c + 1)
                act.activation(diff[:, par], diff[:, par], ACT.Exp).then_inc(weights_ready, 1)

            def root(c):
                act.wait_ge(moments_ready, c + 1)
                act.activation(rstd[:, :], moments[:, :, 1], ACT.Ln, bias=keep["eps"][:, 0:1]).then_inc(log_ready, 1)
                act.wait_ge(log_ready, c + 1)
                act.activation(rstd[:, :], rstd[:, :], ACT.Exp, scale=-0.5).then_inc(rstd_ready, 1)

            def high(par, n, c):
                act.wait_ge(y_ready, c + 1)
                act.wait_ge(late_landed[par], (n + 1) * LATE_LOADS * 16)
                act.activation(y_hi[:, par], y[:, par], ACT.Copy).then_inc(yhi_ready, 1)

            carried_weight(0, 0, 0)
            weights(0, 0)
            high_weights(range(KT // 2, KT))
            carried_weight(1, 0, 1)
            root(0)
            weights(1, 1)
            high(0, 0, 0)
            with act.Fori(0, CHUNKS // 2 - 1) as n:
                for par in (1, 0):
                    c = n * 2 + 2 - par
                    carried_weight(1 - par, n + 1, c + 1)
                    root(c)
                    weights(1 - par, c + 1)
                    high(par, n + 1 - par, c)
            root(CHUNKS - 1)
            high(1, CHUNKS // 2 - 1, CHUNKS - 1)


_INS = ["x", "c", "norm_g", "w_ada", "b_ada", "w_in", "conv_w", "conv_b", "b_igate", "b_fgate_m",
        "mlstm_norm_g", "b_fgate_f", "fox_qnorm_g", "fox_knorm_g", "w_out"]


def layer(nc, a, out):
    def dram(name, shape):
        return nc.dram_tensor("scratch_" + name, shape, F32).ap()

    scratch = {
        "gate": dram("gate", (P, D_MODEL)),
        "gate_rows": dram("gate_rows", (GATE_ROWS, SEQ)),
        "qkT": dram("qkT", (2, 2 * F_W, SEQ)),
        "arrays": dram("arrays", (7 * M_W, SEQ)),
        "f_negF": dram("f_negF", (F_HEADS, SEQ)),
        "m_G": dram("m_G", (M_HEADS, SEQ)),
        "m_prev": dram("m_prev", (M_HEADS, CHUNKS)),
        "m_decay": dram("m_decay", (M_HEADS, CHUNKS)),
        "yT": dram("yT", (F_W, SEQ)),
    }
    with ExitStack() as ctx:
        keep = {
            "params": ctx.enter_context(nc.sbuf_tensor("params", [P, PARAM_ROWS], F32)),
            "gate_cols": ctx.enter_context(nc.sbuf_tensor("gate_cols", [P, 3, M_HEADS, CHUNKS], F32)),
            "eps": ctx.enter_context(nc.sbuf_tensor("eps", [P, 1], F32)),
            "qk_gain": ctx.enter_context(nc.sbuf_tensor("qk_gain", [P, 2 * M_HEADS], F32)),
        }
        modulate_and_project(nc, a, scratch, keep)
        w_land = ctx.enter_context(nc.sbuf_tensor("w_land", [P, KT, D_MODEL], F32))
        with ExitStack() as shared:
            fox = {name: shared.enter_context(nc.sbuf_tensor(name, shape, dt)) for name, shape, dt in (
                ("q_pack", [P, HEADS_IN_TILE, SEQ], F32R), ("k_hi2", [P, HEADS_IN_TILE, SEQ], F32R),
                ("k_lo2", [P, HEADS_IN_TILE, SEQ], F32R), ("v_tok", [P, TT, HEADS_IN_TILE, F_DH], F32),
                ("gate_z", [P, SEQ], F32))}
            fox["head_landed"] = [[shared.enter_context(nc.semaphore(f"head_landed{h}_{half}")) for half in range(2)]
                                  for h in range(HEADS_IN_TILE)]
            fox["v_landed"] = [shared.enter_context(nc.semaphore(f"v_landed{i}")) for i in range(2)]
            fox["z_landed"] = shared.enter_context(nc.semaphore("z_landed"))
            gate_rows(nc, a, scratch, keep, fox)
            forgetting_heads(nc, a, scratch, fox, w_land)
        memory_heads_and_output(nc, a, scratch, keep, w_land, out)


def kernel(**inputs):
    import numpy as _np
    import concourse.bacc as _bacc
    from concourse import mybir as _mybir
    from concourse.bass_utils import run_bass_kernel_spmd as _run

    nc = _bacc.Bacc("TRN2", target_bir_lowering=False, num_devices=1)
    arrays, aps = {}, {}
    for name in _INS:
        arr = _np.ascontiguousarray(inputs[name])
        arrays["in_" + name] = arr
        aps[name] = nc.dram_tensor("in_" + name, arr.shape, _mybir.dt.from_np(arr.dtype), kind="ExternalInput").ap()
    out = nc.dram_tensor("out_0", (1, SEQ, D_MODEL), F32, kind="ExternalOutput").ap()
    layer(nc, aps, out)
    r = _run(nc, [arrays], core_ids=[0])
    return r.results[0]["out_0"]
```
